# Optimizing a Trainium2 kernel written in Bass

```python
import math
import jax, jax.numpy as jnp
from jax import lax
import numpy as np
import jax
import jax.numpy as jnp

D_MODEL = 1024
BATCH = 1
SEQ = 512
DEPTH = 2

N_MIXERS = 4
D_FF = 2816
MEM_LEN = 256
X_HEADS = 4
X_HEAD_DIM = 128
X_WIDTH = X_HEADS * X_HEAD_DIM
POOL_WINDOWS = (2, 4, 8, 16)
POOL_GROUPS = len(POOL_WINDOWS)
POOL_GROUP_DIM = D_MODEL // POOL_GROUPS
DIFF_HEAD_DIM = 64
DIFF_HEADS = D_MODEL // (2 * DIFF_HEAD_DIM)
DIFF_QK = DIFF_HEADS * 2 * DIFF_HEAD_DIM
DIFF_V = DIFF_HEADS * 2 * DIFF_HEAD_DIM
Q_BLOCK = 128
MLSTM_HEADS = 4
MLSTM_HEAD_DIM = D_MODEL // MLSTM_HEADS
MLSTM_CONV = 4
MLSTM_CHUNK = 64
GLA_HEADS = 4
GLA_KEY_DIM = D_MODEL // 2 // GLA_HEADS
GLA_VALUE_DIM = D_MODEL // GLA_HEADS
GLA_GATE_RANK = 16
GLA_TAU = 16.0
GLA_CHUNK = 64
NORM_EPS = 1e-6
SUBLN_EPS = 1e-5
POOL_IN = D_MODEL + X_WIDTH
DIFF_IN = 2 * DIFF_QK + DIFF_V + X_WIDTH
MLSTM_IN = 4 * D_MODEL + 2 * MLSTM_HEADS + X_WIDTH
GLA_IN = 2 * GLA_HEADS * GLA_KEY_DIM + 2 * D_MODEL + GLA_GATE_RANK + X_WIDTH
MIX_OUT = D_MODEL + X_WIDTH


def rmsnorm(x, g, eps=NORM_EPS):
    x32 = x.astype(jnp.float32)
    y = x32 * lax.rsqrt(jnp.mean(x32 * x32, axis=-1, keepdims=True) + eps)
    return (y * g.astype(jnp.float32)).astype(x.dtype)

def swiglu(h, w_up, w_down):
    gate, up = jnp.split(h @ w_up, 2, axis=-1)
    return (jax.nn.silu(gate) * up) @ w_down

def causal_conv(x, w):
    K, C = w.shape
    return lax.conv_general_dilated(x, w[:, None, :].astype(x.dtype), (1,), [(K - 1, 0)],
                                    dimension_numbers=('NWC', 'WIO', 'NWC'), feature_group_count=C)

def alibi_slopes(n):
    return jnp.asarray([2.0 ** (-8.0 * (h + 1) / n) for h in range(n)], dtype=jnp.float32)

def memory_attention(xq, mem_k, mem_v):
    B, S, _ = xq.shape
    q = xq.reshape(B, S, X_HEADS, X_HEAD_DIM)
    s = jnp.einsum('bshd,bmhd->bhsm', q, mem_k).astype(jnp.float32) * (X_HEAD_DIM ** -0.5)
    p = jax.nn.softmax(s, axis=-1)
    o = jnp.einsum('bhsm,bmhd->bshd', p.astype(mem_v.dtype), mem_v)
    return o.reshape(B, S, X_WIDTH)

def _chunks(a, L):
    B, H, S = a.shape[:3]
    return jnp.moveaxis(a.reshape(B, H, S // L, L, *a.shape[3:]), 2, 0)

def _unchunk(a):
    NC, B, H, L = a.shape[:4]
    return jnp.moveaxis(a, 0, 2).reshape(B, H, NC * L, *a.shape[4:])

def multiscale_pool(u, w_group, scale):
    B, S, _ = u.shape
    u32 = u.astype(jnp.float32).reshape(B, S, POOL_GROUPS, POOL_GROUP_DIM)
    cs = jnp.cumsum(u32, axis=1)
    outs = []
    for g, w in enumerate(POOL_WINDOWS):
        c = cs[:, :, g]
        prev = jnp.pad(c[:, :S - w], ((0, 0), (w, 0), (0, 0)))
        count = jnp.minimum(jnp.arange(1, S + 1), w).astype(jnp.float32)
        outs.append((c - prev) / count[None, :, None] - u32[:, :, g])
    pooled = jnp.stack(outs, axis=2).astype(u.dtype)
    mixed = jnp.einsum('bsgc,gcd->bsgd', pooled, w_group).reshape(B, S, D_MODEL)
    return mixed * scale

def pool_layer(h, w_in, w_group, scale, w_out, mem_k, mem_v):
    proj = h @ w_in
    u, xq = proj[..., :D_MODEL], proj[..., D_MODEL:]
    mix = multiscale_pool(u, w_group, scale)
    xo = memory_attention(xq, mem_k, mem_v)
    return jnp.concatenate([mix, xo], axis=-1) @ w_out

def diff_attention(q, k, v, lam, slopes):
    S = q.shape[3]
    scale = DIFF_HEAD_DIM ** -0.5
    outs = []
    for start in range(0, S, Q_BLOCK):
        end = start + Q_BLOCK
        dist = (jnp.arange(start, end)[:, None] - jnp.arange(end)[None, :]).astype(jnp.float32)
        bias = jnp.where(dist >= 0, -slopes[:, None, None] * dist, -jnp.inf)
        s = jnp.einsum('bhcqd,bhckd->bhcqk', q[:, :, :, start:end], k[:, :, :, :end]).astype(jnp.float32) * scale
        p = jax.nn.softmax(s + bias[None, :, None], axis=-1)
        w = p[:, :, 0] - lam * p[:, :, 1]
        outs.append(jnp.einsum('bhqk,bhkd->bhqd', w.astype(v.dtype), v[:, :, :end]))
    return jnp.concatenate(outs, axis=2)

def diff_layer(h, w_in, lam_p, norm_g, w_out, mem_k, mem_v, slopes, layer_idx):
    B, S, _ = h.shape
    H, Dh = DIFF_HEADS, DIFF_HEAD_DIM
    proj = h @ w_in
    q = proj[..., :DIFF_QK].reshape(B, S, H, 2, Dh).transpose(0, 2, 3, 1, 4)
    k = proj[..., DIFF_QK:2 * DIFF_QK].reshape(B, S, H, 2, Dh).transpose(0, 2, 3, 1, 4)
    v = proj[..., 2 * DIFF_QK:2 * DIFF_QK + DIFF_V].reshape(B, S, H, 2 * Dh).transpose(0, 2, 1, 3)
    xq = proj[..., 2 * DIFF_QK + DIFF_V:]
    lam_init = 0.8 - 0.6 * math.exp(-0.3 * layer_idx)
    lp = lam_p.astype(jnp.float32)
    lam = jnp.exp(jnp.sum(lp[0] * lp[1])) - jnp.exp(jnp.sum(lp[2] * lp[3])) + lam_init
    o = diff_attention(q, k, v, lam, slopes)
    o = rmsnorm(o, norm_g, eps=SUBLN_EPS) * (1.0 - lam_init)
    o = o.transpose(0, 2, 1, 3).reshape(B, S, H * 2 * Dh)
    xo = memory_attention(xq, mem_k, mem_v)
    return jnp.concatenate([o, xo], axis=-1) @ w_out

def mlstm_chunkwise(q, k, v, i_pre, f_pre):
    B, H, S, Dk = q.shape
    Dv = v.shape[-1]
    L = MLSTM_CHUNK
    q = q * (Dk ** -0.5)
    lf = jax.nn.log_sigmoid(f_pre)
    causal = jnp.tril(jnp.ones((L, L), dtype=bool))

    def step(carry, inp):
        C, n, m = carry
        qc, kc, vc, ic, lfc = inp
        b = jnp.cumsum(lfc, axis=-1)
        dmat = jnp.where(causal, b[..., :, None] - b[..., None, :] + ic[..., None, :], -jnp.inf)
        inter = b + m[..., None]
        m_t = jnp.maximum(inter, jnp.max(dmat, axis=-1))
        dec = jnp.exp(inter - m_t)
        sqk = jnp.einsum('bhtd,bhsd->bhts', qc, kc) * jnp.exp(dmat - m_t[..., None])
        num = dec[..., None] * jnp.einsum('bhtd,bhde->bhte', qc, C) + jnp.einsum('bhts,bhse->bhte', sqk, vc)
        den = dec * jnp.einsum('bhtd,bhd->bht', qc, n) + jnp.sum(sqk, axis=-1)
        hc = num / jnp.maximum(jnp.abs(den), jnp.exp(-m_t))[..., None]
        bL = b[..., -1]
        gs = bL[..., None] - b + ic
        m_new = jnp.maximum(bL + m, jnp.max(gs, axis=-1))
        ws = jnp.exp(gs - m_new[..., None])
        carry_dec = jnp.exp(bL + m - m_new)
        C_new = carry_dec[..., None, None] * C + jnp.einsum('bhs,bhsd,bhse->bhde', ws, kc, vc)
        n_new = carry_dec[..., None] * n + jnp.einsum('bhs,bhsd->bhd', ws, kc)
        return (C_new, n_new, m_new), hc

    init = (jnp.zeros((B, H, Dk, Dv), jnp.float32), jnp.zeros((B, H, Dk), jnp.float32),
            jnp.zeros((B, H), jnp.float32))
    xs = (_chunks(q, L), _chunks(k, L), _chunks(v, L), _chunks(i_pre, L), _chunks(lf, L))
    _, hs = lax.scan(step, init, xs)
    return _unchunk(hs)

def mlstm_layer(h, w_in, conv_w, gate_b, norm_g, w_out, mem_k, mem_v):
    B, S, _ = h.shape
    H, Dh, D = MLSTM_HEADS, MLSTM_HEAD_DIM, D_MODEL
    proj = h @ w_in
    qk = jax.nn.silu(causal_conv(proj[..., :2 * D], conv_w))
    q, k = qk[..., :D], qk[..., D:]
    v = proj[..., 2 * D:3 * D]
    o = proj[..., 3 * D:4 * D]
    gates = proj[..., 4 * D:4 * D + 2 * H].astype(jnp.float32).reshape(B, S, 2, H) + gate_b.astype(jnp.float32)
    xq = proj[..., 4 * D + 2 * H:]

    def heads(a):
        return a.reshape(B, S, H, Dh).transpose(0, 2, 1, 3).astype(jnp.float32)

    hh = mlstm_chunkwise(heads(q), heads(k), heads(v),
                         gates[:, :, 0].transpose(0, 2, 1), gates[:, :, 1].transpose(0, 2, 1))
    hh = rmsnorm(hh.transpose(0, 2, 1, 3).astype(h.dtype), norm_g.reshape(H, Dh)).reshape(B, S, D)
    hh = hh * jax.nn.sigmoid(o)
    xo = memory_attention(xq, mem_k, mem_v)
    return jnp.concatenate([hh, xo], axis=-1) @ w_out

def gla_chunkwise(q, k, v, log_a):
    B, H, S, Dk = q.shape
    Dv = v.shape[-1]
    L = GLA_CHUNK
    q = q * (Dk ** -0.5)
    causal = jnp.tril(jnp.ones((L, L), dtype=bool))

    def step(state, inp):
        qc, kc, vc, ac = inp
        b = jnp.cumsum(ac, axis=2)
        inter = jnp.einsum('bhtd,bhde->bhte', qc * jnp.exp(b), state)
        diff = b[:, :, :, None, :] - b[:, :, None, :, :]
        decay = jnp.exp(jnp.where(causal[:, :, None], diff, -jnp.inf))
        amat = jnp.einsum('bhtd,bhsd,bhtsd->bhts', qc, kc, decay)
        intra = jnp.einsum('bhts,bhse->bhte', amat, vc)
        bL = b[:, :, -1]
        k_dec = kc * jnp.exp(bL[:, :, None, :] - b)
        new_state = jnp.exp(bL)[..., None] * state + jnp.einsum('bhsd,bhse->bhde', k_dec, vc)
        return new_state, inter + intra

    init = jnp.zeros((B, H, Dk, Dv), jnp.float32)
    xs = (_chunks(q, L), _chunks(k, L), _chunks(v, L), _chunks(log_a, L))
    _, os_ = lax.scan(step, init, xs)
    return _unchunk(os_)

def gla_layer(h, w_in, gate_w2, gate_b, norm_g, w_out, mem_k, mem_v):
    B, S, _ = h.shape
    H, Dk, Dv = GLA_HEADS, GLA_KEY_DIM, GLA_VALUE_DIM
    kw = H * Dk
    proj = h @ w_in
    q = proj[..., :kw]
    k = proj[..., kw:2 * kw]
    v = proj[..., 2 * kw:2 * kw + D_MODEL]
    g = proj[..., 2 * kw + D_MODEL:2 * kw + 2 * D_MODEL]
    z = proj[..., 2 * kw + 2 * D_MODEL:2 * kw + 2 * D_MODEL + GLA_GATE_RANK]
    xq = proj[..., 2 * kw + 2 * D_MODEL + GLA_GATE_RANK:]
    log_a = jax.nn.log_sigmoid((z @ gate_w2 + gate_b).astype(jnp.float32)) / GLA_TAU

    def heads(a, d):
        return a.reshape(B, S, H, d).transpose(0, 2, 1, 3).astype(jnp.float32)

    o = gla_chunkwise(heads(q, Dk), heads(k, Dk), heads(v, Dv), heads(log_a, Dk))
    o = rmsnorm(o.transpose(0, 2, 1, 3).astype(h.dtype), norm_g.reshape(H, Dv)).reshape(B, S, D_MODEL)
    o = o * jax.nn.silu(g)
    xo = memory_attention(xq, mem_k, mem_v)
    return jnp.concatenate([o, xo], axis=-1) @ w_out

def _layers_of(kind):
    return len(range(kind, DEPTH, N_MIXERS))

def first_inputs(seed: int = 0) -> dict:
    key = jax.random.key(seed)
    keys = iter(jax.random.split(key, 40))

    def nrm(shape, scale):
        return jax.random.normal(next(keys), shape, jnp.float32) * scale

    def gain(shape):
        return 1.0 + nrm(shape, 0.05)

    nA, nB, nC, nD = (_layers_of(kd) for kd in range(N_MIXERS))
    D = D_MODEL
    x = nrm((BATCH, SEQ, D), 1.0)
    mem = nrm((BATCH, MEM_LEN, D), 1.0)
    norm_g = gain((DEPTH, 3, D))
    ffn_w_up = nrm((DEPTH, 2, D, 2 * D_FF), D ** -0.5)
    ffn_w_down = nrm((DEPTH, 2, D_FF, D), D_FF ** -0.5)
    mem_norm_g = gain((D,))
    mem_w_kv = nrm((DEPTH, D, 2 * X_WIDTH), D ** -0.5)
    pool_w_in = nrm((nA, D, POOL_IN), D ** -0.5)
    pool_w_group = nrm((nA, POOL_GROUPS, POOL_GROUP_DIM, POOL_GROUP_DIM), POOL_GROUP_DIM ** -0.5)
    pool_scale = gain((nA, D))
    pool_w_out = nrm((nA, MIX_OUT, D), MIX_OUT ** -0.5)
    diff_w_in = nrm((nB, D, DIFF_IN), D ** -0.5)
    diff_lambda = nrm((nB, 4, DIFF_HEAD_DIM), 0.1)
    diff_norm_g = gain((nB, 2 * DIFF_HEAD_DIM))
    diff_w_out = nrm((nB, MIX_OUT, D), MIX_OUT ** -0.5)
    mlstm_w_in = nrm((nC, D, MLSTM_IN), D ** -0.5)
    mlstm_conv_w = nrm((nC, MLSTM_CONV, 2 * D), MLSTM_CONV ** -0.5)
    i_bias = nrm((nC, MLSTM_HEADS), 0.1)
    f_bias = jnp.linspace(3.0, 6.0, MLSTM_HEADS, dtype=jnp.float32)[None] + nrm((nC, MLSTM_HEADS), 0.01)
    mlstm_gate_b = jnp.stack([i_bias, f_bias], axis=1)
    mlstm_norm_g = gain((nC, D))
    mlstm_w_out = nrm((nC, MIX_OUT, D), MIX_OUT ** -0.5)
    gla_w_in = nrm((nD, D, GLA_IN), D ** -0.5)
    gla_gate_w2 = nrm((nD, GLA_GATE_RANK, GLA_HEADS * GLA_KEY_DIM), GLA_GATE_RANK ** -0.5)
    gla_gate_b = nrm((nD, GLA_HEADS * GLA_KEY_DIM), 0.1)
    gla_norm_g = gain((nD, D))
    gla_w_out = nrm((nD, MIX_OUT, D), MIX_OUT ** -0.5)
    final_norm_g = gain((D,))
    return {'x': x, 'mem': mem, 'norm_g': norm_g, 'ffn_w_up': ffn_w_up, 'ffn_w_down': ffn_w_down,
            'mem_norm_g': mem_norm_g, 'mem_w_kv': mem_w_kv,
            'pool_w_in': pool_w_in, 'pool_w_group': pool_w_group, 'pool_scale': pool_scale, 'pool_w_out': pool_w_out,
            'diff_w_in': diff_w_in, 'diff_lambda': diff_lambda, 'diff_norm_g': diff_norm_g, 'diff_w_out': diff_w_out,
            'mlstm_w_in': mlstm_w_in, 'mlstm_conv_w': mlstm_conv_w, 'mlstm_gate_b': mlstm_gate_b,
            'mlstm_norm_g': mlstm_norm_g, 'mlstm_w_out': mlstm_w_out,
            'gla_w_in': gla_w_in, 'gla_gate_w2': gla_gate_w2, 'gla_gate_b': gla_gate_b,
            'gla_norm_g': gla_norm_g, 'gla_w_out': gla_w_out, 'final_norm_g': final_norm_g}

def first_block(x, mem, norm_g, ffn_w_up, ffn_w_down, mem_norm_g, mem_w_kv,
              pool_w_in, pool_w_group, pool_scale, pool_w_out,
              diff_w_in, diff_lambda, diff_norm_g, diff_w_out,
              mlstm_w_in, mlstm_conv_w, mlstm_gate_b, mlstm_norm_g, mlstm_w_out,
              gla_w_in, gla_gate_w2, gla_gate_b, gla_norm_g, gla_w_out, final_norm_g):
    B, M, _ = mem.shape
    mem_n = rmsnorm(mem, mem_norm_g)
    slopes = alibi_slopes(DIFF_HEADS)
    for i in range(DEPTH):
        kind, j = i % N_MIXERS, i // N_MIXERS
        kv = mem_n @ mem_w_kv[i]
        mem_k = kv[..., :X_WIDTH].reshape(B, M, X_HEADS, X_HEAD_DIM)
        mem_v = kv[..., X_WIDTH:].reshape(B, M, X_HEADS, X_HEAD_DIM)
        x = x + 0.5 * swiglu(rmsnorm(x, norm_g[i, 0]), ffn_w_up[i, 0], ffn_w_down[i, 0])
        h = rmsnorm(x, norm_g[i, 1])
        if kind == 0:
            mix = pool_layer(h, pool_w_in[j], pool_w_group[j], pool_scale[j], pool_w_out[j], mem_k, mem_v)
        elif kind == 1:
            mix = diff_layer(h, diff_w_in[j], diff_lambda[j], diff_norm_g[j], diff_w_out[j], mem_k, mem_v, slopes, i)
        elif kind == 2:
            mix = mlstm_layer(h, mlstm_w_in[j], mlstm_conv_w[j], mlstm_gate_b[j], mlstm_norm_g[j], mlstm_w_out[j],
                              mem_k, mem_v)
        else:
            mix = gla_layer(h, gla_w_in[j], gla_gate_w2[j], gla_gate_b[j], gla_norm_g[j], gla_w_out[j], mem_k, mem_v)
        x = x + mix
        x = x + 0.5 * swiglu(rmsnorm(x, norm_g[i, 2]), ffn_w_up[i, 1], ffn_w_down[i, 1])
    return rmsnorm(x, final_norm_g)


GRID_W = 64
CTX_LEN = 256
N_MIXERS_2 = 3
EPS = 1e-6
F32 = jnp.float32

M_EXPAND = 2
M_DI = M_EXPAND * D_MODEL
M_HEADDIM = 64
M_NH = M_DI // M_HEADDIM
M_NG = 8
M_HPG = M_NH // M_NG
M_NS = 128
M_CONV_W = 5
M_CHUNK = 128
M_CONV_CH = M_DI + 2 * M_NG * M_NS
M_IN = M_DI + M_CONV_CH + 2 * M_NH

A_HEADDIM = 64
A_NH = D_MODEL // A_HEADDIM
A_NKV = 4
A_REP = A_NH // A_NKV
A_W = A_NH * A_HEADDIM
A_KW = A_NKV * A_HEADDIM
A_IN = 2 * A_W + 2 * A_KW
A_QBLOCK = 128
ROPE_BASE = 10000.0

S_DI = D_MODEL
S_GROUP = 16
S_NG = S_DI // S_GROUP
S_P = 64

N_A = (DEPTH + N_MIXERS_2 - 1) // N_MIXERS_2
N_B = (DEPTH + N_MIXERS_2 - 2) // N_MIXERS_2
N_C = DEPTH // N_MIXERS_2


def rmsnorm_2(x, w):
    xf = x.astype(F32)
    y = xf * lax.rsqrt(jnp.mean(xf * xf, axis=-1, keepdims=True) + EPS)
    return (y * w.astype(F32)).astype(x.dtype)

def dwconv_centred(u, w, b):
    pad = w.shape[0] // 2
    out = lax.conv_general_dilated(u, w[:, None, :], window_strides=(1,), padding=[(pad, pad)],
                                   dimension_numbers=('NWC', 'WIO', 'NWC'),
                                   feature_group_count=u.shape[-1])
    return out + b

def ssd_scan(xs, dt, a, bm, cm, init_state, need_y=True):
    bsz, L = xs.shape[:2]
    nc = L // M_CHUNK

    def chunks(t):
        return t.astype(F32).reshape((bsz, nc, M_CHUNK) + t.shape[2:])

    xc, dtc, bc, cc = chunks(xs), chunks(dt), chunks(bm), chunks(cm)
    la_cum = jnp.cumsum(dtc * a, axis=2)
    to_end = jnp.exp(la_cum[:, :, -1:] - la_cum) * dtc
    states = jnp.einsum('bcsgn,bcsgr,bcsgrp->bcgrpn', bc, to_end, xc)
    chunk_decay = jnp.exp(la_cum[:, :, -1])

    def step(carry, inp):
        st, dec = inp
        return carry * dec[..., None, None] + st, carry

    final, prev = lax.scan(step, init_state.astype(F32),
                           (jnp.moveaxis(states, 1, 0), jnp.moveaxis(chunk_decay, 1, 0)))
    if not need_y:
        return None, final
    prev = jnp.moveaxis(prev, 0, 1)
    causal = jnp.tril(jnp.ones((M_CHUNK, M_CHUNK), dtype=bool))[:, :, None, None]
    seg = la_cum[:, :, :, None] - la_cum[:, :, None, :]
    decay = jnp.exp(jnp.where(causal, seg, -jnp.inf))
    cb = jnp.einsum('bclgn,bcsgn->bclsg', cc, bc)
    w = cb[..., None] * decay * dtc[:, :, None]
    y_diag = jnp.einsum('bclsgr,bcsgrp->bclgrp', w, xc)
    y_off = jnp.einsum('bclgn,bcgrpn,bclgr->bclgrp', cc, prev, jnp.exp(la_cum))
    return (y_diag + y_off).reshape(xs.shape), final

def mamba_mixer(h_ctx, h_lat, in_w, conv_w, conv_b, a_log, dt_bias, d_skip, norm_w, out_w, ctx_out):
    a = -jnp.exp(a_log.astype(F32)).reshape(2, M_NG, M_HPG)
    dtb = dt_bias.astype(F32).reshape(2, M_NG, M_HPG)

    def project(h):
        bsz, L, _ = h.shape
        z, xbc, dt = jnp.split(h @ in_w, [M_DI, M_DI + M_CONV_CH], axis=-1)
        xbc = jax.nn.silu(dwconv_centred(xbc, conv_w, conv_b))
        xs, bm, cm = jnp.split(xbc, [M_DI, M_DI + M_NG * M_NS], axis=-1)
        xs = xs.reshape(bsz, L, M_NG, M_HPG, M_HEADDIM)
        bm = bm.reshape(bsz, L, M_NG, M_NS)
        cm = cm.reshape(bsz, L, M_NG, M_NS)
        dt = jax.nn.softplus(dt.astype(F32).reshape(bsz, L, 2, M_NG, M_HPG) + dtb)
        return z, xs, bm, cm, dt

    zc, xc, bc, cc, dtc = project(h_ctx)
    zl, xl, bl, cl, dtl = project(h_lat)
    bsz = h_lat.shape[0]
    zero = jnp.zeros((bsz, M_NG, M_HPG, M_HEADDIM, M_NS), F32)
    rev = lambda t: jnp.flip(t, axis=1)
    yc_f, st_f = ssd_scan(xc, dtc[:, :, 0], a[0], bc, cc, zero, ctx_out)
    yl_f, _ = ssd_scan(xl, dtl[:, :, 0], a[0], bl, cl, st_f)
    yc_b, st_b = ssd_scan(rev(xc), rev(dtc[:, :, 1]), a[1], rev(bc), rev(cc), zero, ctx_out)
    yl_b, _ = ssd_scan(rev(xl), rev(dtl[:, :, 1]), a[1], rev(bl), rev(cl), st_b)
    dsk = d_skip.astype(F32).reshape(M_NG, M_HPG, 1)

    def finish(y, xs, z):
        b_, L = xs.shape[:2]
        y = (y + dsk * xs.astype(F32)).reshape(b_, L, M_DI).astype(z.dtype)
        return rmsnorm_2(y * jax.nn.silu(z), norm_w) @ out_w

    o_lat = finish(yl_f + rev(yl_b), xl, zl)
    o_ctx = finish(yc_f + rev(yc_b), xc, zc) if ctx_out else None
    return o_ctx, o_lat

def axial_rope_tables(L):
    rows = L // GRID_W
    r_idx, c_idx = jnp.meshgrid(jnp.arange(rows), jnp.arange(GRID_W), indexing='ij')
    r_idx = r_idx.reshape(-1).astype(F32)
    c_idx = c_idx.reshape(-1).astype(F32)
    half = A_HEADDIM // 2
    inv = ROPE_BASE ** (-jnp.arange(0, half, 2, dtype=F32) / half)
    ang = jnp.concatenate([r_idx[:, None] * inv, c_idx[:, None] * inv], axis=-1)
    return jnp.cos(ang), jnp.sin(ang)

def apply_rope(t, cos, sin):
    b_, L, h, d = t.shape
    q = d // 4
    tf = t.astype(F32).reshape(b_, L, h, 2, 2, q)
    t1, t2 = tf[..., 0, :], tf[..., 1, :]
    cs = cos.reshape(1, L, 1, 2, q)
    sn = sin.reshape(1, L, 1, 2, q)
    out = jnp.stack([t1 * cs - t2 * sn, t1 * sn + t2 * cs], axis=-2)
    return out.reshape(b_, L, h, d).astype(t.dtype)

def attend(q, k, v):
    bsz, lq = q.shape[:2]
    q = q.reshape(bsz, lq, A_NKV, A_REP, A_HEADDIM)
    s = jnp.einsum('bqgrd,bkgd->bgrqk', q, k).astype(F32) * (A_HEADDIM ** -0.5)
    p = jax.nn.softmax(s, axis=-1).astype(v.dtype)
    o = jnp.einsum('bgrqk,bkgd->bqgrd', p, v)
    return o.reshape(bsz, lq, A_W)

def attn_mixer(h_ctx, h_lat, in_w, q_norm, k_norm, out_w, ctx_out):
    def project(h):
        bsz, L, _ = h.shape
        q, k, v, g = jnp.split(h @ in_w, [A_W, A_W + A_KW, A_W + 2 * A_KW], axis=-1)
        q = rmsnorm_2(q.reshape(bsz, L, A_NH, A_HEADDIM), q_norm)
        k = rmsnorm_2(k.reshape(bsz, L, A_NKV, A_HEADDIM), k_norm)
        v = v.reshape(bsz, L, A_NKV, A_HEADDIM)
        return q, k, v, g

    qc, kc, vc, gc = project(h_ctx)
    ql, kl, vl, gl = project(h_lat)
    bsz, L = h_lat.shape[:2]
    cos, sin = axial_rope_tables(L)
    ql = apply_rope(ql, cos, sin)
    kl = apply_rope(kl, cos, sin)
    k_all = jnp.concatenate([kc, kl], axis=1)
    v_all = jnp.concatenate([vc, vl], axis=1)
    nblk = L // A_QBLOCK
    q_blocks = jnp.moveaxis(ql.reshape(bsz, nblk, A_QBLOCK, A_NH, A_HEADDIM), 1, 0)
    ol = lax.map(lambda qb: attend(qb, k_all, v_all), q_blocks)
    ol = jnp.moveaxis(ol, 0, 1).reshape(bsz, L, A_W)
    o_lat = (ol * jax.nn.silu(gl)) @ out_w
    o_ctx = (attend(qc, kc, vc) * jax.nn.silu(gc)) @ out_w if ctx_out else None
    return o_ctx, o_lat

def s5_discretize(lam_re, lam_im, log_step, b_re, b_im):
    lr, li = lam_re.astype(F32), lam_im.astype(F32)
    step = jnp.exp(log_step.astype(F32))[:, None]
    mag = jnp.exp(lr * step)
    abar_re, abar_im = mag * jnp.cos(li * step), mag * jnp.sin(li * step)
    den = lr * lr + li * li
    nr, ni = abar_re - 1.0, abar_im
    coef_re = ((nr * lr + ni * li) / den)[..., None]
    coef_im = ((ni * lr - nr * li) / den)[..., None]
    br, bi = b_re.astype(F32), b_im.astype(F32)
    return abar_re, abar_im, coef_re * br - coef_im * bi, coef_re * bi + coef_im * br

def complex_affine_combine(e1, e2):
    a1r, a1i, b1r, b1i = e1
    a2r, a2i, b2r, b2i = e2
    return (a1r * a2r - a1i * a2i, a1r * a2i + a1i * a2r,
            a2r * b1r - a2i * b1i + b2r, a2r * b1i + a2i * b1r + b2i)

def s5_scan(u, abar_re, abar_im, bbar_re, bbar_im, init_re, init_im):
    L = u.shape[1]
    bu_re = jnp.einsum('blgh,gph->lbgp', u, bbar_re)
    bu_im = jnp.einsum('blgh,gph->lbgp', u, bbar_im)
    bu_re = bu_re.at[0].add(abar_re * init_re - abar_im * init_im)
    bu_im = bu_im.at[0].add(abar_re * init_im + abar_im * init_re)
    a_re = jnp.broadcast_to(abar_re, (L, 1) + abar_re.shape)
    a_im = jnp.broadcast_to(abar_im, (L, 1) + abar_im.shape)
    _, _, x_re, x_im = lax.associative_scan(complex_affine_combine, (a_re, a_im, bu_re, bu_im), axis=0)
    return x_re, x_im

def s5_mixer(h_ctx, h_lat, in_w, lam_re, lam_im, log_step, b_re, b_im, c_re, c_im,
             d_skip, glu_w, glu_b, out_w, ctx_out):
    bsz = h_lat.shape[0]
    disc = [s5_discretize(lam_re[k], lam_im[k], log_step[k], b_re[k], b_im[k]) for k in range(2)]
    cr, ci = c_re.astype(F32), c_im.astype(F32)

    def readout(x_re, x_im, k):
        return jnp.einsum('lbgp,ghp->blgh', x_re, cr[k]) - jnp.einsum('lbgp,ghp->blgh', x_im, ci[k])

    uc, zc = jnp.split(h_ctx @ in_w, 2, axis=-1)
    ul, zl = jnp.split(h_lat @ in_w, 2, axis=-1)
    grp = lambda u: u.astype(F32).reshape(u.shape[0], u.shape[1], S_NG, S_GROUP)
    rev = lambda t: jnp.flip(t, axis=1)
    ucg, ulg = grp(uc), grp(ul)
    zero = jnp.zeros((bsz, S_NG, S_P), F32)
    xr, xi = s5_scan(ucg, *disc[0], zero, zero)
    yc = readout(xr, xi, 0) if ctx_out else None
    xr, xi = s5_scan(ulg, *disc[0], xr[-1], xi[-1])
    yl = readout(xr, xi, 0)
    xr, xi = s5_scan(rev(ucg), *disc[1], zero, zero)
    if ctx_out:
        yc = yc + rev(readout(xr, xi, 1))
    xr, xi = s5_scan(rev(ulg), *disc[1], xr[-1], xi[-1])
    yl = yl + rev(readout(xr, xi, 1))
    dsk = d_skip.astype(F32)

    def finish(y, u, z):
        b_, L = u.shape[:2]
        y = (y.reshape(b_, L, S_DI) + dsk * u.astype(F32)).astype(z.dtype)
        y = jax.nn.gelu(y)
        y = y * jax.nn.sigmoid(y @ glu_w + glu_b)
        return (y * jax.nn.silu(z)) @ out_w

    o_lat = finish(yl, ul, zl)
    o_ctx = finish(yc, uc, zc) if ctx_out else None
    return o_ctx, o_lat

def second_inputs(seed: int = 0) -> dict:
    key = jax.random.key(seed)
    ks = iter(jax.random.split(key, 48))
    nrm = lambda shape, scale: jax.random.normal(next(ks), shape, F32) * scale
    gain = lambda shape: 1.0 + nrm(shape, 0.02)
    inp = {}
    inp['x'] = nrm((BATCH, SEQ, D_MODEL), 1.0)
    inp['c'] = nrm((BATCH, D_MODEL), 1.0)
    inp['ctx'] = nrm((BATCH, CTX_LEN, D_MODEL), 1.0)
    inp['c_ctx'] = nrm((D_MODEL,), 1.0)
    inp['norm_w'] = gain((DEPTH, D_MODEL))
    inp['mod_w'] = nrm((DEPTH, D_MODEL, 3 * D_MODEL), 0.5 * D_MODEL ** -0.5)
    inp['mod_b'] = nrm((DEPTH, 3 * D_MODEL), 0.02)
    inp['final_norm_w'] = gain((D_MODEL,))
    inp['m_in_w'] = nrm((N_A, D_MODEL, M_IN), D_MODEL ** -0.5)
    inp['m_conv_w'] = nrm((N_A, M_CONV_W, M_CONV_CH), M_CONV_W ** -0.5)
    inp['m_conv_b'] = nrm((N_A, M_CONV_CH), 0.02)
    inp['m_a_log'] = jnp.log(jax.random.uniform(next(ks), (N_A, 2, M_NH), F32, 1.0, 16.0))
    dt0 = jnp.exp(jax.random.uniform(next(ks), (N_A, 2, M_NH), F32, math.log(1e-3), math.log(1e-1)))
    inp['m_dt_bias'] = dt0 + jnp.log(-jnp.expm1(-dt0))
    inp['m_d'] = 1.0 + nrm((N_A, M_NH), 0.1)
    inp['m_norm_w'] = gain((N_A, M_DI))
    inp['m_out_w'] = nrm((N_A, M_DI, D_MODEL), M_DI ** -0.5)
    inp['a_in_w'] = nrm((N_B, D_MODEL, A_IN), D_MODEL ** -0.5)
    inp['a_q_norm'] = gain((N_B, A_HEADDIM))
    inp['a_k_norm'] = gain((N_B, A_HEADDIM))
    inp['a_out_w'] = nrm((N_B, A_W, D_MODEL), A_W ** -0.5)
    inp['s_in_w'] = nrm((N_C, D_MODEL, 2 * S_DI), D_MODEL ** -0.5)
    inp['s_lambda_re'] = -0.5 + nrm((N_C, 2, S_NG, S_P), 0.01)
    inp['s_lambda_im'] = math.pi * jnp.arange(S_P, dtype=F32) + nrm((N_C, 2, S_NG, S_P), 0.01)
    inp['s_log_step'] = jax.random.uniform(next(ks), (N_C, 2, S_NG), F32, math.log(1e-3), math.log(1e-1))
    inp['s_b_re'] = nrm((N_C, 2, S_NG, S_P, S_GROUP), (2 * S_GROUP) ** -0.5)
    inp['s_b_im'] = nrm((N_C, 2, S_NG, S_P, S_GROUP), (2 * S_GROUP) ** -0.5)
    inp['s_c_re'] = nrm((N_C, 2, S_NG, S_GROUP, S_P), S_P ** -0.5)
    inp['s_c_im'] = nrm((N_C, 2, S_NG, S_GROUP, S_P), S_P ** -0.5)
    inp['s_d'] = nrm((N_C, S_DI), 1.0)
    inp['s_glu_w'] = nrm((N_C, S_DI, S_DI), S_DI ** -0.5)
    inp['s_glu_b'] = nrm((N_C, S_DI), 0.02)
    inp['s_out_w'] = nrm((N_C, S_DI, D_MODEL), S_DI ** -0.5)
    return inp

def second_block(x, c, ctx, c_ctx, norm_w, mod_w, mod_b, final_norm_w,
              m_in_w, m_conv_w, m_conv_b, m_a_log, m_dt_bias, m_d, m_norm_w, m_out_w,
              a_in_w, a_q_norm, a_k_norm, a_out_w,
              s_in_w, s_lambda_re, s_lambda_im, s_log_step, s_b_re, s_b_im, s_c_re, s_c_im,
              s_d, s_glu_w, s_glu_b, s_out_w):
    h_lat, h_ctx = x, ctx
    sc, scc = jax.nn.silu(c), jax.nn.silu(c_ctx)
    for i in range(DEPTH):
        kind, j = i % N_MIXERS_2, i // N_MIXERS_2
        ctx_out = i < DEPTH - 1
        sh, scl, gt = jnp.split(sc @ mod_w[i] + mod_b[i], 3, axis=-1)
        shc, sclc, gtc = jnp.split(scc @ mod_w[i] + mod_b[i], 3, axis=-1)
        in_lat = rmsnorm_2(h_lat, norm_w[i]) * (1.0 + scl[:, None]) + sh[:, None]
        in_ctx = rmsnorm_2(h_ctx, norm_w[i]) * (1.0 + sclc) + shc
        if kind == 0:
            o_ctx, o_lat = mamba_mixer(in_ctx, in_lat, m_in_w[j], m_conv_w[j], m_conv_b[j], m_a_log[j],
                                       m_dt_bias[j], m_d[j], m_norm_w[j], m_out_w[j], ctx_out)
        elif kind == 1:
            o_ctx, o_lat = attn_mixer(in_ctx, in_lat, a_in_w[j], a_q_norm[j], a_k_norm[j], a_out_w[j], ctx_out)
        else:
            o_ctx, o_lat = s5_mixer(in_ctx, in_lat, s_in_w[j], s_lambda_re[j], s_lambda_im[j], s_log_step[j],
                                    s_b_re[j], s_b_im[j], s_c_re[j], s_c_im[j], s_d[j], s_glu_w[j],
                                    s_glu_b[j], s_out_w[j], ctx_out)
        h_lat = h_lat + gt[:, None] * o_lat
        if ctx_out:
            h_ctx = h_ctx + gtc * o_ctx
    return rmsnorm_2(h_lat, final_norm_w)


def setup_inputs(seed=0):
    out = dict(first_inputs(seed))
    for name, value in second_inputs(seed + 1).items():
        if name != "x":
            out[name + "_2"] = value
    return out


def reference(
    x, mem, norm_g, ffn_w_up, ffn_w_down, mem_norm_g, mem_w_kv, pool_w_in, pool_w_group,
    pool_scale, pool_w_out, diff_w_in, diff_lambda, diff_norm_g, diff_w_out, mlstm_w_in,
    mlstm_conv_w, mlstm_gate_b, mlstm_norm_g, mlstm_w_out, gla_w_in, gla_gate_w2, gla_gate_b,
    gla_norm_g, gla_w_out, final_norm_g, c_2, ctx_2, c_ctx_2, norm_w_2, mod_w_2, mod_b_2,
    final_norm_w_2, m_in_w_2, m_conv_w_2, m_conv_b_2, m_a_log_2, m_dt_bias_2, m_d_2, m_norm_w_2,
    m_out_w_2, a_in_w_2, a_q_norm_2, a_k_norm_2, a_out_w_2, s_in_w_2, s_lambda_re_2,
    s_lambda_im_2, s_log_step_2, s_b_re_2, s_b_im_2, s_c_re_2, s_c_im_2, s_d_2, s_glu_w_2,
    s_glu_b_2, s_out_w_2,
):
    x = first_block(
        x, mem, norm_g, ffn_w_up, ffn_w_down, mem_norm_g, mem_w_kv, pool_w_in, pool_w_group,
        pool_scale, pool_w_out, diff_w_in, diff_lambda, diff_norm_g, diff_w_out, mlstm_w_in,
        mlstm_conv_w, mlstm_gate_b, mlstm_norm_g, mlstm_w_out, gla_w_in, gla_gate_w2,
        gla_gate_b, gla_norm_g, gla_w_out, final_norm_g,
    )
    return second_block(
        x, c_2, ctx_2, c_ctx_2, norm_w_2, mod_w_2, mod_b_2, final_norm_w_2, m_in_w_2,
        m_conv_w_2, m_conv_b_2, m_a_log_2, m_dt_bias_2, m_d_2, m_norm_w_2, m_out_w_2, a_in_w_2,
        a_q_norm_2, a_k_norm_2, a_out_w_2, s_in_w_2, s_lambda_re_2, s_lambda_im_2, s_log_step_2,
        s_b_re_2, s_b_im_2, s_c_re_2, s_c_im_2, s_d_2, s_glu_w_2, s_glu_b_2, s_out_w_2,
    )


_drawn_inputs = setup_inputs


def setup_inputs(seed=0):
    import zlib

    import numpy as np

    out = dict(_drawn_inputs(seed))
    spreads = {}
    factors = {'mem_norm_g': 8.0,
     'diff_norm_g': 2.793,
     'ctx_2': 4.634,
     'norm_w_2': 6.55,
     'final_norm_w_2': 23.168,
     'm_conv_b_2': 6.802,
     'm_d_2': 200.0,
     'm_norm_w_2': 8.0,
     'a_q_norm_2': 8.0,
     'a_k_norm_2': 8.0}
    for name, (base, spread) in spreads.items():
        noise = np.random.default_rng([zlib.crc32(name.encode()), seed]).standard_normal(out[name].shape)
        drawn = base * np.exp(spread * noise) if base else spread * noise
        out[name] = jnp.asarray(drawn.astype(out[name].dtype))
    for name, factor in factors.items():
        out[name] = (out[name] * factor).astype(out[name].dtype)
    return out
```

```python
import math
import numpy as np
import concourse.bass as bass
from concourse import mybir
from contextlib import ExitStack

FP32 = mybir.dt.float32
F32R = mybir.dt.float32r
ALU = mybir.AluOpType
ACT = mybir.ActivationFunctionType
AX = mybir.AxisListType

P = 128
D = 1024
KD = D // P
T = 512
TC = 256
TA = T + TC
NB = T // P
D_FF = 2816
FF_PARTS = (8, 8, 6)
UNIT = 8 * P
RAW = 2
RING = 4
X_HEADS = 4
POOL_WINDOWS = (2, 4, 8, 16)
PAD = 16
DIFF_HEADS = 8
DIFF_SCALE = 64 ** -0.5
LAM_INIT = 0.8 - 0.6 * math.exp(-0.3)
MG = 8
HPG = 4
NCH = TA // P
A_HEADS = 16
A_KV = 4
A_SCALE = 64 ** -0.5
MASKED = -1e30

FF_UNITS = 2 * sum(FF_PARTS) + sum(FF_PARTS)
STAGE_UNITS = [
    ("memkv", 16), ("ffn0", FF_UNITS), ("pool", 14), ("pool_out", 12), ("ffn1", FF_UNITS),
    ("ffn2", FF_UNITS), ("diff", 36), ("diff_out", 4), ("ffn3", FF_UNITS), ("mamba", 64),
    ("attn_kv", 4), ("attn_qg", 16), ("attn_out", 8),
]
MOD_UNITS = 48
FIRST_UNIT = {}
UNITS = 0
for _name, _n in STAGE_UNITS:
    FIRST_UNIT[_name] = UNITS
    UNITS += _n

COLUMNS = [
    ("norm_g", 48), ("final_norm_g", 8), ("mem_norm_g", 8), ("pool_scale", 8), ("diff_norm_g", 1),
    ("norm_w_2", 16), ("final_norm_w_2", 8), ("mod_b_2", 48), ("conv_w", 5 * 32), ("conv_b", 32),
    ("m_norm_w", 16), ("a_q_norm", 1), ("a_k_norm", 1), ("c", 16), ("dt_bias", 64), ("a_log", 64),
    ("m_d", 32), ("diff_lambda", 256), ("slopes", 8), ("pool_rcount", 64),
]
COL = {}
NCOL = 0
for _name, _n in COLUMNS:
    COL[_name] = NCOL
    NCOL += _n

SQUARES = ["ident", "ones", "ones64", "upto", "from", "rot", "dup0", "dup1"]


class Link:

    def __init__(self, eng, sem):
        self.eng, self.sem, self.n, self.i, self.per = eng, sem, 0, None, 0

    def __call__(self, ins):
        self.until(self.mark(ins))

    def mark(self, ins):
        ins.then_inc(self.sem, 1)
        self.n += 1
        return self.n

    def until(self, n):
        self.eng.wait_ge(self.sem, n if self.i is None else self.i * self.per + n)

    def enter(self, i, per):
        self.i, self.per, self.first = i, per, self.n

    def leave(self, times):
        assert self.n - self.first == self.per, (self.n - self.first, self.per)
        self.i, self.n = None, self.first + self.per * times


def at(base, i=None, per=0):
    return base if i is None else i * per + base


def program(nc, A, cut=None):
    ctx = ExitStack()
    with ctx:
        build(nc, A, ctx, cut)


def build(nc, A, ctx, cut):
    def sb(name, shape, dt=FP32, scope=ctx):
        return scope.enter_context(nc.sbuf_tensor(name, shape, dt))

    def sem(name):
        return ctx.enter_context(nc.semaphore(name))

    x = sb("x", [P, KD, T])
    side = sb("side", [P, KD, TC])
    raw = sb("raw", [P, RAW, UNIT])
    wh = sb("wh", [P, RING, UNIT], F32R)
    wl = sb("wl", [P, RING, UNIT], F32R)
    cols = sb("cols", [P, NCOL])
    sq8 = sb("sq8", [P, len(SQUARES), P])
    SQ = {n: sq8[:, k, :] for k, n in enumerate(SQUARES)}
    ident, ones = SQ["ident"], SQ["ones"]
    eps6 = sb("eps6", [P, 1])
    eps5 = sb("eps5", [P, 1])
    credit = sb("credit", [P, 32])
    modv = sb("modv", [P, 48, 2])
    gmod = sb("gmod", [P, 16, 2])
    sqr = sb("sqr", [P, 2, T])
    rt = sb("rt", [P, T])
    rstd = sb("rstd", [P, T])
    tmp = sb("tmp", [P, 2, T])

    def scope():
        return ExitStack()

    with scope() as first:
        hh = sb("hh", [P, KD, T], F32R, first)
        hl = sb("hl", [P, KD, T], F32R, first)
        fh = sb("fh", [P, KD, T], F32R, first)
        fl = sb("fl", [P, KD, T], F32R, first)
        dist = sb("dist", [P, T], scope=first)
        csil = sb("csil", [P, KD, 2], scope=first)
        modw = sb("modw", [P, 2, UNIT], scope=first)
        mk = sb("mk", [P, 2 * X_HEADS, TC], scope=first)
        mv = sb("mv", [P, 2 * X_HEADS, 2, P], scope=first)
        with scope() as s:
            dq = sb("dq", [P, 2, T], scope=s)
            dk = sb("dk", [P, 2, T], scope=s)
            dv = sb("dv", [P, 2, T], scope=s)
            dvt = sb("dvt", [P, NB, P], scope=s)
            de = sb("de", [P, 2, T], scope=s)
            dw = sb("dw", [P, T], scope=s)
            dT = sb("dT", [P, NB, T], scope=s)
            dnm = sb("dnm", [P, 2], scope=s)
            drs = sb("drs", [P, 2], scope=s)
            drr = sb("drr", [P, 2], scope=s)
            drl = sb("drl", [P, 1], scope=s)
            lamt = sb("lamt", [P, 2, 64], scope=s)
            lams = sb("lams", [P, 2], scope=s)
            lame = sb("lame", [P, 2], scope=s)
            lam = sb("lam", [P, 1], scope=s)
            dgain = sb("dgain", [P, 1], scope=s)
        xoh = sb("xoh", [P, X_HEADS, T], F32R, first)
        xol = sb("xol", [P, X_HEADS, T], F32R, first)
        qx = sb("qx", [P, X_HEADS, T], scope=first)
        with scope() as s:
            sg = sb("sg", [P, 2, T], scope=s)
            ubuf = sb("ubuf", [P, 2, PAD + T], scope=s)
        vt = modw[:, :, 0:TC]
        modflat = modw[:].rearrange("p s n -> p (s n)")
        pa, pb_ = (modflat[:, n * (PAD + T):(n + 1) * (PAD + T)] for n in range(2))
        with scope() as s:
            qcur = sb("qcur", [P, T], scope=s)
            vcur = sb("vcur", [P, 2, P], scope=s)
            pexp = sb("pexp", [P, 2, TC], scope=s)
            pT = sb("pT", [P, 2, T], scope=s)
            nm = sb("nm", [P, 8], scope=s)
            rs = sb("rs", [P, 8], scope=s)
            rr = sb("rr", [P, 8], scope=s)

    with scope() as s:
        mh = sb("mh", [P, KD, TA], F32R, s)
        ml = sb("ml", [P, KD, TA], F32R, s)
        acc = sb("acc", [P, KD, TA], scope=s)
        zs = sb("zs", [P, 2, TA], scope=s)
        xs = sb("xs", [P, 2, TA], scope=s)
        cvin = sb("cvin", [P, 4, TA + 6], scope=s)
        Bm = sb("Bm", [P, TA], scope=s)
        Cm = sb("Cm", [P, TA], scope=s)
        da = sb("da", [P, 2, NCH, MG * HPG], scope=s)
        sqacc = sb("sqacc", [P, TA], scope=s)
        yt = sb("yt", [P, HPG, 64], scope=s)
        state = sb("state", [P, 2, HPG, 64], scope=s)
        xe = sb("xe", [P, 2, HPG, 64], scope=s)
        yh = sb("yh", [P, 2, TA], F32R, s)
        yl = sb("yl", [P, 2, TA], F32R, s)
        dag = sb("dag", [P, 2, NCH, HPG], scope=s)
    sideflat = side[:].rearrange("p k t -> p (k t)")
    dt, la, ela, tend, cdec = (sideflat[:, n * NCH * 64:(n + 1) * NCH * 64].rearrange("p (d c h) -> p d c h", d=2, c=NCH)
                               for n in range(5))
    wdt = acc[:, 0, 0:KD * 64].rearrange("p (k h) -> p k h", k=KD)
    aexp = acc[:, 1, 0:64]
    xflat = x[:].rearrange("p k t -> p (k t)")
    xtok = xflat[:, 0:NCH * 256].rearrange("p (c r e) -> p c r e", c=NCH, r=HPG)
    ytok = xflat[:, NCH * 256:NCH * 512].rearrange("p (c r e) -> p c r e", c=NCH, r=HPG)
    btok = xflat[:, NCH * 512:NCH * 640].rearrange("p (c n) -> p c n", c=NCH)
    xdt = xs[:].rearrange("p a t -> p (a t)").rearrange("p (c r e) -> p c r e", c=NCH, r=HPG)
    cbm = xflat[:, NCH * 640:NCH * 640 + P]
    decay = [tmp[:, 0, :], tmp[:, 1, :], sqr[:, 0, :], sqr[:, 1, :]]
    conv = [b[:].rearrange("p a t -> p (a t)")[:, 0:TA + 2] for b in (sqr, tmp)]
    one = sq8[:, 1, 0:1]

    with scope() as s:
        ah = sb("ah", [P, KD, TA], F32R, s)
        al = sb("al", [P, KD, TA], F32R, s)
        kd = sb("kd", [P, A_KV, TA], scope=s)
        vtok = sb("vtok", [P, NCH, A_KV * 64], scope=s)
        og = sb("og", [P, KD, T], scope=s)
        qr = sb("qr", [P, 2, T], scope=s)
        gs = sb("gs", [P, 2, T], scope=s)
        pe2 = sb("pe2", [P, 2, TA], scope=s)
        pT2 = sb("pT2", [P, NCH, T], scope=s)
        kcur = sb("kcur", [P, TA], scope=s)
        vcur2 = sb("vcur2", [P, NCH, 64], scope=s)
        cos, sin = sb("cos", [P, T], scope=s), sb("sin", [P, T], scope=s)
        nm2, rs2, rr2 = (sb(n, [P, 8], scope=s) for n in ("nm2", "rs2", "rr2"))
        aqg = sb("aqg", [P, 1], scope=s)
    ogflat = og[:].rearrange("p k t -> p (k t)")
    kraw, vraw = (ogflat[:, 2 * n * TA:2 * (n + 1) * TA].rearrange("p (j t) -> p j t", j=2) for n in range(2))
    pT2flat = pT2[:].rearrange("p k t -> p (k t)")
    kn, ksq = (pT2flat[:, n * TA:(n + 1) * TA] for n in range(2))
    krt, krs = (pT2flat[:, (2 + n) * TA:(3 + n) * TA] for n in range(2))

    ps = ctx.enter_context(nc.psum_tensor("ps", [P, 8 * T], FP32))
    B = [ps[:, k * T:(k + 1) * T] for k in range(8)]

    loaded = [sem(f"raw_loaded{s}") for s in range(RAW)]
    s_hi = sem("weights_hi")
    s_lo = sem("weights_lo")
    unit_done = sem("unit_done")
    consts_in, dist_in = sem("consts_in"), sem("dist_in")
    x_in = sem("x_in")
    side_in = sem("side_in")
    s_chain = sem("dve_chain")
    s_achain = sem("act_chain")
    s_pchain = sem("pe_chain")
    s_init = sem("init")
    c_silu = sem("c_silu")
    mod_loaded = [sem(f"mod_loaded{s}") for s in range(2)]
    mod_used, mod_read, gmod_ready = sem("mod_used"), sem("mod_read"), sem("gmod_ready")
    sq_ready, sq_used, rt_ready = sem("sq_ready"), sem("sq_used"), sem("rt_ready")
    tmp_ready, h_hi, h_ready = sem("tmp_ready"), sem("h_hi"), sem("h_ready")
    kv_copied, kv_t, kv_ready = sem("kv_copied"), sem("kv_t"), sem("kv_ready")
    silu_ready, gated, hid_hi, hid_lo = sem("silu_ready"), sem("gated"), sem("hid_hi"), sem("hid_lo")
    x_ready = sem("x_ready")
    pool_copied, pooled, pooled_hi, pooled_lo = sem("pool_copied"), sem("pooled"), sem("pooled_hi"), sem("pooled_lo")
    mix_hi, mix_lo = sem("mix_hi"), sem("mix_lo")
    att_q, att_v, att_s, att_max = sem("att_q"), sem("att_v"), sem("att_s"), sem("att_max")
    att_exp, att_p, att_t, att_pt, att_o = sem("att_exp"), sem("att_p"), sem("att_t"), sem("att_pt"), sem("att_o")
    xo_hi, xo_lo = sem("xo_hi"), sem("xo_lo")
    d_copied, d_vt, d_vtok, d_s, d_biased = sem("d_copied"), sem("d_vt"), sem("d_vtok"), sem("d_s"), sem("d_biased")
    d_max, d_exp, d_w, d_t, d_pt, d_o = sem("d_max"), sem("d_exp"), sem("d_w"), sem("d_t"), sem("d_pt"), sem("d_o")
    d_sq, d_ss, d_rt, d_ot, d_ohi, d_olo, d_m = (sem("d_sq"), sem("d_ss"), sem("d_rt"), sem("d_ot"), sem("d_ohi"),
                                                sem("d_olo"), sem("d_m"))
    lam_sums, lam_exp = sem("lam_sums"), sem("lam_exp")
    parked, ctx_in, wdt_in = sem("parked"), sem("ctx_in"), sem("wdt_in")
    cv_zero = sem("cv_zero")
    t_dt, t_x, t_abs, t_exp, t_ln, t_a = sem("t_dt"), sem("t_x"), sem("t_abs"), sem("t_exp"), sem("t_ln"), sem("t_a")
    t_da, t_cum, t_diff, t_dec, t_ready = sem("t_da"), sem("t_cum"), sem("t_diff"), sem("t_dec"), sem("t_ready")
    m_cv, m_z, m_acc, m_xbc, m_tr, m_tok = (sem("m_cv"), sem("m_z"), sem("m_acc"), sem("m_xbc"), sem("m_tr"), sem("m_tok"))
    m_cb, m_t, m_e, m_w, m_yp, m_sp = sem("m_cb"), sem("m_t"), sem("m_e"), sem("m_w"), sem("m_yp"), sem("m_sp")
    m_y, m_st, m_dag, m_x = sem("m_y"), sem("m_st"), sem("m_dag"), sem("m_x")
    m_yt, m_yg, m_sq, m_yh, m_yl, m_om, m_add = (sem("m_yt"), sem("m_yg"), sem("m_sq"), sem("m_yh"), sem("m_yl"),
                                                sem("m_om"), sem("m_add"))
    m_ss, m_rt, m_px, m_py = sem("m_ss"), sem("m_rt"), sem("m_px"), sem("m_py")
    ctx_ready, cs_in = sem("ctx_ready"), sem("cs_in")
    b_copied, b_sq, b_ss, b_rt, b_kn = sem("b_copied"), sem("b_sq"), sem("b_ss"), sem("b_rt"), sem("b_kn")
    b_rot, b_kr, b_dup, b_kd, b_vt, b_v = sem("b_rot"), sem("b_kr"), sem("b_dup"), sem("b_kd"), sem("b_vt"), sem("b_v")
    a_qc, a_sq, a_ss, a_rt, a_qn, a_rot, a_qr = (sem("a_qc"), sem("a_sq"), sem("a_ss"), sem("a_rt"), sem("a_qn"),
                                                 sem("a_rot"), sem("a_qr"))
    a_g, a_kv, a_s, a_max, a_exp = sem("a_g"), sem("a_kv"), sem("a_s"), sem("a_max"), sem("a_exp")
    a_p, a_t, a_pt, a_pv, a_o, a_oh, a_ol = (sem("a_p"), sem("a_t"), sem("a_pt"), sem("a_pv"), sem("a_o"), sem("a_oh"),
                                             sem("a_ol"))
    out_done = sem("out_done")

    STEPS = [(0, c) for c in (4, 5, 0, 1, 2, 3)] + [(1, c) for c in (5, 4, 3, 2, 1, 0)]
    NS = len(STEPS)
    Q_AT, SS_AT, ROT_AT, G_AT = 1, 3, 5, 6
    PAIRS = A_HEADS // 2
    UNDER = ((0, 3), (3, 6), (6, 8))

    def updates(t):
        return sum(1 for k in range(t + 1) if k % NCH != NCH - 1)

    def chunk(c):
        return slice(c * P, (c + 1) * P)

    stages = [n for n, _ in STAGE_UNITS]
    def runs(name):
        return cut is None or stages.index(name if name != "final" else "mamba") <= stages.index(cut)
    total = UNITS if cut is None else min(UNITS, FIRST_UNIT[cut] + dict(STAGE_UNITS)[cut])
    X0 = 2

    def xr(ffns, mixers):
        return X0 + 24 * ffns + (0, 16, 16 + 8 * DIFF_HEADS + 8)[mixers]

    X_ATTN = xr(4, 2) + 16
    MIXERS_BEFORE = {"ffn0": 0, "ffn1": 1, "ffn2": 1, "ffn3": 2}

    block = ctx.enter_context(nc.Block())

    def col(name, k=0, n=1):
        return cols[:, COL[name] + k:COL[name] + k + n]

    NORM = {n: k for k, n in enumerate(["mem", "ffn0", "pool", "ffn1", "ffn2", "diff", "ffn3", "final",
                                        "lat0", "ctx0", "lat1", "ctx1", "last"])}

    @block.sync
    def _(sp):
        sp.dma_start(side[:], A["memT"]).then_inc(side_in, 16)
        sp.dma_start(sq8[:], A["squares"]).then_inc(consts_in, 16)
        sp.dma_start(cols[:], A["cols"]).then_inc(consts_in, 16)

        def load(u, i=None, per=0):
            sp.dma_start(raw[:, u % RAW, :], A["stream"][at(u, i, per)]).then_inc(loaded[u % RAW], 16)

        for u in range(RING):
            if u >= RAW:
                sp.wait_ge(s_lo, u - RAW + 1)
            load(u)
        sp.dma_start(x[:], A["xT"]).then_inc(x_in, 16)
        sp.dma_start(dist[:], A["dist"]).then_inc(dist_in, 16)
        passes = (total - RING) // RING
        with sp.Fori(0, passes) as i:
            for j in range(RING):
                u = RING + j
                sp.wait_ge(s_lo, at(u - RAW + 1, i, RING))
                load(u, i, RING)
        for u in range(RING * (passes + 1), total):
            sp.wait_ge(s_lo, u - RAW + 1)
            load(u)
        if cut is None:
            sp.wait_ge(x_ready, X_ATTN + 16)
            sp.dma_start(A["out"], x[:]).then_inc(x_in, 16)
            sp.wait_ge(x_in, 32)
            sp.wait_ge(parked, 32)
        else:
            sp.wait_ge(out_done, 0 + 1)
            sp.dma_start(A["out"], x[:]).then_inc(x_in, 16)
            sp.wait_ge(x_in, 32)

    @block.gpsimd
    def _(pool):
        def rest(u, i=None, per=0):
            pool.wait_ge(s_hi, at(u + 1, i, per))
            nc.gpsimd.tensor_tensor(wl[:, u % RING, :], raw[:, u % RAW, :], wh[:, u % RING, :].bitcast(FP32),
                                    ALU.subtract).then_inc(s_lo, 1)

        def rests(u, end):
            passes = (end - u) // RING
            with pool.Fori(0, passes) as i:
                for j in range(RING):
                    rest(u + j, i, RING)
            for v in range(u + RING * passes, end):
                rest(v)

        def group(g, i=None, out=None, z=None, ahead=None):
            def c(per, n):
                return at(per * g + n, i, per)
            gg = g if i is None else i + g

            def per_head(a, d, k):
                return a[:, d, k, bass.ds(gg * HPG, HPG)].unsqueeze(2).to_broadcast([P, HPG, 64])

            def step(t):
                d, k = STEPS[t]
                if d:
                    pool.wait_ge(m_yp, c(NS, STEPS.index((0, k)) + 1))
                last = nc.gpsimd.tensor_tensor(xdt[:, k], xtok[:, k], per_head(dt, d, k), ALU.mult)
                if t % NCH != NCH - 1:
                    before = [v for v in range(t) if v % NCH != NCH - 1]
                    if len(before) >= 2:
                        pool.wait_ge(m_cb, c(NS, before[-2] + 1))
                    last = nc.gpsimd.tensor_tensor(xe[:, updates(t) % 2], xtok[:, k], per_head(tend, d, k), ALU.mult)
                last.then_inc(m_px, 1)

            for u in (z, z + 1) + ((out, out + 1) if out is not None else ()):
                rest(u + RING, i, 8)
            pool.wait_ge(m_tok, c(5, 5))
            step(0)
            step(1)
            for k in range(NCH):
                last = nc.gpsimd.tensor_tensor(ytok[:, k], xtok[:, k],
                                               cols[:, bass.ds(COL["m_d"] + gg * HPG, HPG)].unsqueeze(2)
                                               .to_broadcast([P, HPG, 64]), ALU.mult)
            last.then_inc(m_py, 1)
            for t in range(2, NS):
                step(t)
                if ahead is not None and t % 3 == 1 and t > 1:
                    rest(ahead + t // 3 - 1 + RING, i, 8)
            if ahead is not None:
                rest(ahead + 3 + RING, i, 8)
            for j in range(2):
                pool.wait_ge(m_x, c(2, j + 1))
                pool.wait_ge(m_sq, c(2, j + 1))
                nc.gpsimd.tensor_tensor(sqacc[:], sqacc[:], xs[:, j, :], ALU.add).then_inc(m_sq, 1)

        if cut is None or runs("mamba"):
            u = FIRST_UNIT["mamba"]
            rests(0, u + 8)
            pool.wait_ge(t_ready, 1)
            group(0, z=u + 4, ahead=u + 6)
            with pool.Fori(0, MG - 2) as i:
                group(1, i, z=u + 10, out=u + 12, ahead=u + 14)
            group(MG - 1, z=u + 58, out=u + 60)
            rests(u + 66, total)
        else:
            rests(0, total)

    @block.tensor
    def _(pe):
        def project(u, hi, lo, outs, i=None, per=0, arrive=None, part=(0, KD)):
            if part[0] == 0:
                pe.wait_ge(s_lo, at(u + 1, i, per))
            s = u % RING
            for k in range(*part):
                if arrive is not None:
                    arrive(k)
                w = slice(k * P, (k + 1) * P)
                for a, b in ((wh, hi), (wh, lo), (wl, hi)):
                    for bank, c0, c1 in outs:
                        last = nc.tensor.matmul(bank, a[:, s, w], b[:, k, c0:c1],
                                                start=(k == 0 and a is wh and b is hi),
                                                stop=(k == KD - 1 and a is wl))
            if part[1] == KD:
                last.then_inc(unit_done, 1)

        def blocks(u, plan, i=None, per=0):
            pe.wait_ge(s_lo, at(u + 1, i, per))
            s = u % RING
            for k, (before, hi, lo, bank, start, stop) in enumerate(plan):
                before()
                w = slice(k * P, (k + 1) * P)
                nc.tensor.matmul(bank, wh[:, s, w], hi, start=start, stop=False)
                nc.tensor.matmul(bank, wh[:, s, w], lo, start=False, stop=False)
                last = nc.tensor.matmul(bank, wl[:, s, w], hi, start=False, stop=stop)
            last.then_inc(unit_done, 1)

        def norm_sums(name, width):
            n = NORM[name]
            if n:
                pe.wait_ge(rt_ready, n)
            for k in range(KD):
                pe.wait_ge(sq_ready, 8 * n + k + 1)
                nc.tensor.matmul(B[7][:, 0:width], ones, sqr[:, k % 2, 0:width],
                                 start=(k == 0), stop=(k == KD - 1)).then_inc(sq_used, 1)

        def modulation(v, i):
            pe.wait_ge(mod_loaded[v % 2], at(16 * (v // 2 + 1), i, 16))
            for k in range(KD):
                last = nc.tensor.matmul(B[6][:, bass.ds(i * 4 + 2 * v, 2)], modw[:, v % 2, k * P:(k + 1) * P], csil[:, k, :],
                                        start=(k == 0), stop=(k == KD - 1))
            last.then_inc(mod_used, 1)

        def ffn(f, name, norm):
            n = NORM[norm]
            norm_sums(norm, T)
            u = FIRST_UNIT[name]
            pairs = f * sum(FF_PARTS)
            for p, w in enumerate(FF_PARTS):
                def arrive(k):
                    pe.wait_ge(h_ready, 8 * n + k + 1)
                with pe.Fori(0, w // 2) as i:
                    for jj in range(2):
                        pe.wait_ge(gated, at(pairs + jj + 1, i, 2))
                        g = u + 2 * jj
                        project(g, hh, hl, [(B[2 * jj][:], 0, T)], i, 4, arrive=arrive if p == 0 and jj == 0 else None)
                        project(g + 1, hh, hl, [(B[2 * jj + 1][:], 0, T)], i, 4)
                        if w == KD and f < 3:
                            modulation(16 * f + 8 * p + jj, i)
                u += 2 * w
                done = xr(f, MIXERS_BEFORE[name]) + 8 * p
                hidden = pairs + w

                def before(m, k, i=None, per=0):
                    def wait():
                        if k == 0:
                            pe.wait_ge(x_ready, at(done + m - 1, i, per))
                            pe.wait_ge(hid_lo, hidden - 2)
                        if k >= w - 2:
                            pe.wait_ge(hid_lo, hidden - w + k + 1)
                    return wait
                if w == KD:
                    with pe.Fori(0, 2) as i:
                        for m in range(4):
                            blocks(u + m, [(before(m, k, i, 4), fh[:, k, :], fl[:, k, :], B[4 + m % 2][:], k == 0,
                                            k == w - 1) for k in range(w)], i, 4)
                else:
                    for v in range(w):
                        plan = []
                        for b in range(8 * v, 8 * v + 8):
                            m, k = b // w, b % w
                            plan.append((before(m, k), fh[:, k, :], fl[:, k, :], B[4 + m % 2][:], k == 0, k == w - 1))
                        blocks(u + v, plan)
                u += w
                pairs += w

        def memory_attention(layer):
            with pe.Fori(0, X_HEADS) as i:
                n = 16 * layer

                def scores(b):
                    if b >= 2:
                        pe.wait_ge(att_exp, at(n + b - 1, i, 4))
                    nc.tensor.matmul(B[4 + b % 2][:, 0:TC], qcur[:, b * P:(b + 1) * P],
                                     mk[:, i + X_HEADS * layer, :], start=True, stop=True).then_inc(att_s, 1)

                def turn(b):
                    pe.wait_ge(att_p, at(n + b + 1, i, 4))
                    if b >= 2:
                        pe.wait_ge(att_pt, at(n + b - 1, i, 4))
                    for kb in range(2):
                        last = nc.tensor.transpose(B[6 + b % 2][:, kb * P:(kb + 1) * P],
                                                   pexp[:, b % 2, kb * P:(kb + 1) * P], ident)
                    last.then_inc(att_t, 1)

                pe.wait_ge(att_q, at(X_HEADS * layer + 1, i, 1))
                scores(0)
                scores(1)
                turn(0)
                scores(2)
                turn(1)
                scores(3)
                turn(2)
                turn(3)
                pe.wait_ge(att_pt, at(n + 4, i, 4))
                pe.wait_ge(att_v, at(X_HEADS * layer + 1, i, 1))
                for kb in range(2):
                    last = nc.tensor.matmul(B[2][:], vcur[:, kb, :], pT[:, kb, :], start=(kb == 0), stop=(kb == 1))
                last.then_inc(att_o, 1)

        def out_memory(u, done, mixers):
            for v in range(4):
                plan = []
                for b in range(8):
                    m, k = 2 * v + b // 4, b % 4

                    def before(m=m, k=k):
                        if k == 0:
                            pe.wait_ge(x_ready, done + m - 1)
                            pe.wait_ge(xo_lo, X_HEADS * mixers)
                    plan.append((before, xoh[:, k, :], xol[:, k, :], B[m % 2][:], k == 0, k == 3))
                blocks(u + v, plan)

        def diff_head(h, par, i=None, ahead=None, out=None):
            def c(n, per):
                return at(n, i, 2 * per)

            def scores(b):
                for r in range(2):
                    if b:
                        pe.wait_ge(d_biased, c(8 * h + 2 * (b - 1) + r + 1, 8))
                    nc.tensor.matmul(B[2 + r][:, 0:(b + 1) * P], dq[64 * r:64 * r + 64, par, b * P:(b + 1) * P],
                                     dk[64 * r:64 * r + 64, par, 0:(b + 1) * P], start=True, stop=True).then_inc(d_s, 1)

            def turn(b):
                pe.wait_ge(d_w, c(4 * h + b + 1, 4))
                if b:
                    pe.wait_ge(d_pt, c(4 * h + b, 4))
                else:
                    pe.wait_ge(d_vtok, c(h + 1, 1))
                for kb in range(b + 1):
                    last = nc.tensor.transpose(B[4][:, kb * P:(kb + 1) * P], dw[:, kb * P:(kb + 1) * P], ident)
                last.then_inc(d_t, 1)

            pe.wait_ge(d_copied, c(3 * h + 3, 3))
            for kb in range(NB):
                last = nc.tensor.transpose(B[4][:, kb * P:(kb + 1) * P], dv[:, par, kb * P:(kb + 1) * P], ident)
            last.then_inc(d_vt, 1)
            scores(0)
            for b in range(NB):
                if b < 3 and ahead is not None:
                    if b == 1 and not (i is None and h == 0):
                        pe.wait_ge(d_rt, c(h, 1))
                    if b == 2:
                        pe.wait_ge(d_copied, c(3 * h + 4, 3))
                    project(ahead + b, hh, hl, [(B[b % 2][:], 0, T)], i, 8)
                if b == 3 and out is not None:
                    out_head(h - 1, 1 - par, out, i)
                turn(b)
                if b < 3:
                    scores(b + 1)
            pe.wait_ge(d_pt, c(4 * h + 4, 4))
            if not (i is None and h == 0):
                pe.wait_ge(d_olo, c(h, 1))
            for kb in range(NB):
                last = nc.tensor.matmul(B[5][:, kb * P:T], dvt[:, kb, :], dT[:, kb, kb * P:T], start=(kb == 0),
                                        stop=(kb == NB - 1))
            last.then_inc(d_o, 1)
            pe.wait_ge(d_sq, c(h + 1, 1))
            if ahead is not None:
                pe.wait_ge(d_copied, c(3 * h + 5, 3))
            nc.tensor.matmul(B[1][:], ones, sqr[:, 0, :], start=True, stop=True).then_inc(d_ss, 1)

        def out_head(h, par, u, i=None):
            pe.wait_ge(s_lo, at(u + 1, i, 8))
            pe.wait_ge(d_olo, at(h + 1, i, 2))
            for m in range(KD):
                pe.wait_ge(x_ready, at(xr(3, 1) + 8 * h + m - 1, i, 16))
                w = slice(m * P, (m + 1) * P)
                nc.tensor.matmul(B[6 + m % 2][:], wh[:, u % RING, w], fh[:, par, :], start=True, stop=False)
                nc.tensor.matmul(B[6 + m % 2][:], wh[:, u % RING, w], fl[:, par, :], start=False, stop=False)
                nc.tensor.matmul(B[6 + m % 2][:], wl[:, u % RING, w], fh[:, par, :], start=False, stop=True)\
                  .then_inc(d_m if m < KD - 1 else unit_done, 1)

        def both(bank):
            return [(B[bank][:], 0, T), (B[bank + 1][:, 0:TC], T, TA)]

        def step_sizes():
            d3 = B[0][:, 0:NCH * 64].rearrange("p (d c h) -> p d c h", d=2, c=NCH)
            pe.wait_ge(wdt_in, 16)
            pe.wait_ge(h_ready, 8 * NORM["ctx0"])
            for c in range(NCH):
                for k in range(KD):
                    for half in (mh, ml):
                        last = nc.tensor.matmul(d3[:, :, c, :], half[:, k, chunk(c)].bitcast(FP32), wdt[:, k, :],
                                                start=(k == 0 and half is mh), stop=(k == KD - 1 and half is ml))
            last.then_inc(t_dt, 1)
            pe.wait_ge(t_da, 1)
            half = NCH * 32
            for d, tri in ((0, SQ["upto"]), (1, SQ["from"])):
                nc.tensor.matmul(B[1][:, d * half:(d + 1) * half], tri, da[:, d, :, :], start=True, stop=True)
            nc.tensor.matmul(B[2][:, 0:2 * half], ones, da[:], start=True, stop=True).then_inc(t_cum, 1)

        def group(g, i=None, out=None, z=None, ahead=None):
            def c(per, n):
                return at(per * g + n, i, per)
            pe.wait_ge(m_cv, c(4, 4))
            project(z, mh, ml, both(0), i, 8)
            project(z + 1, mh, ml, both(2), i, 8)
            if out is not None:
                group_out(g - 1, i, out)
            for n, cs in enumerate((range(4), range(4), range(4), range(4, 6), range(4, 6))):
                if n == 0:
                    pe.wait_ge(m_z, c(2, 2))
                    pe.wait_ge(m_xbc, c(4, 2))
                if n == 2:
                    pe.wait_ge(m_xbc, c(4, 3))
                if n == 4 and out is not None:
                    pe.wait_ge(m_add, c(8, 0))
                o = 0
                for src in {0: [xs[:, 0]], 1: [xs[:, 1]], 2: [Bm], 3: [xs[:, 0], xs[:, 1]], 4: [Bm]}[n]:
                    for k in cs:
                        last = nc.tensor.transpose(B[n][:, o:o + P], src[:, chunk(k)], ident)
                        o += P
                last.then_inc(m_tr, 1)
            pe.wait_ge(m_xbc, c(4, 4))
            pe.wait_ge(m_dag, c(1, 1))
            pe.wait_ge(m_tok, c(5, 5))

            def before(t):
                d, k = STEPS[t]
                pe.wait_ge(m_px, c(NS, t + 1))
                if t >= 2:
                    pe.wait_ge(m_w, c(NS, t - 1))
                    if (t - 2) % NCH != NCH - 1:
                        pe.wait_ge(m_st, c(updates(NS - 1), updates(t - 2)))
                bank = B[4 + t % 2]
                nc.tensor.matmul(bank[:, 0:P], Bm[:, chunk(k)], Cm[:, chunk(k)], start=True, stop=True)
                if t % NCH != NCH - 1:
                    nc.tensor.matmul(bank[:, P:P + 256], btok[:, k, :], xe[:, updates(t) % 2], start=True, stop=True)
                for r in range(HPG):
                    last = nc.tensor.matmul(B[2 + t % 2][:, chunk(r)], dag[:, d, k, r:r + 1].to_broadcast([P, P]),
                                            SQ["from" if d else "upto"], start=True, stop=True)
                last.then_inc(m_cb, 1)

            before(0)
            for t, (d, k) in enumerate(STEPS):
                if t + 1 < NS:
                    before(t + 1)
                pe.wait_ge(m_w, c(NS, t + 1))
                if t >= 2:
                    pe.wait_ge(m_y, c(NS, t - 1))
                bank = B[6 + t % 2]
                for r in range(HPG):
                    last = nc.tensor.matmul(bank[:, 64 * r:64 * r + 64], decay[t % 4][:, chunk(r)], xdt[:, k, r, :],
                                            start=True, stop=True)
                if t % NCH:
                    pe.wait_ge(m_st, c(updates(NS - 1), updates(t - 1)))
                    last = nc.tensor.matmul(bank[:, 256:512], Cm[:, chunk(k)], state[:, updates(t - 1) % 2],
                                            start=True, stop=True)
                last.then_inc(m_yp, 1)
                if ahead is not None:
                    n = t // 3
                    if t % 3 == 0:
                        if n:
                            pe.wait_ge(m_cv, c(4, 4 + n))
                    project(ahead + n, mh, ml, both(0), i, 8, part=UNDER[t % 3])
            pe.wait_ge(m_y, c(NS, NS))
            for j in range(2):
                lat, con = (B[6], B[7]) if j == 0 else (B[4], B[5])
                for k in range(NCH):
                    bank, o = (lat, k) if k < 4 else (con, k - 4)
                    last = nc.tensor.transpose(bank[:, chunk(o)], ytok[:, k, 2 * j:2 * j + 2, :].rearrange("p r e -> p (r e)"),
                                               ident)
                last.then_inc(m_yt, 1)

        def group_out(g, i, u):
            for a in range(2):
                pe.wait_ge(s_lo, at(u + a + 1, i, 8))
                if a == 0:
                    pe.wait_ge(m_yl, at(2 * g + 2, i, 2))
                for q in range(4):
                    m = 4 * a + q
                    lat, con = (B[6], B[7]) if m % 2 == 0 else (B[4], B[5])
                    if m >= 2:
                        pe.wait_ge(m_add, at(8 * g + m - 1, i, 8))
                    for k in range(2):
                        w = chunk(2 * q + k)
                        for wt, half in ((wh, yh), (wh, yl), (wl, yh)):
                            for bank, c0, c1 in ((lat[:], 0, T), (con[:, 0:TC], T, TA)):
                                last = nc.tensor.matmul(bank, wt[:, (u + a) % RING, w], half[:, k, c0:c1],
                                                        start=(k == 0 and wt is wh and half is yh),
                                                        stop=(k == 1 and wt is wl))
                    last.then_inc(m_om if q < 3 else unit_done, 1)

        def keys_values(u):
            pe.wait_ge(h_ready, 8 * NORM["ctx1"])
            pe.wait_ge(m_rt, 1)
            for n in range(4):
                project(u + n, ah, al, both(2 * n))
            for j in range(2):
                pe.wait_ge(b_sq, j + 1)
                pe.wait_ge(b_copied, j + 1)
                for c0, c1, bank in ((0, T, 2 * j), (T, TA, 2 * j + 1)):
                    last = nc.tensor.matmul(B[bank][:, 0:c1 - c0], SQ["ones64"], ksq[:, c0:c1], start=True, stop=True)
                last.then_inc(b_ss, 1)
                pe.wait_ge(b_copied, 3 + j)
                for k in range(NCH):
                    bank, o = (4 + 2 * j, k) if k < 4 else (5 + 2 * j, k - 4)
                    last = nc.tensor.transpose(B[bank][:, chunk(o)], vraw[:, j, chunk(k)], ident)
                last.then_inc(b_vt, 1)
                pe.wait_ge(b_kn, j + 1)
                nc.tensor.matmul(B[2 * j][:], SQ["rot"], kn[:, 0:T], start=True, stop=True).then_inc(b_rot, 1)
                pe.wait_ge(b_kr, j + 1)
                for r in range(2):
                    pe.wait_ge(b_v, j + 1) if r == 0 else pe.wait_ge(b_kd, 2 * j + 1)
                    for c0, c1, bank in ((0, T, 4 + 2 * j), (T, TA, 5 + 2 * j)):
                        last = nc.tensor.matmul(B[bank][:, 0:c1 - c0], SQ[f"dup{r}"], kraw[:, j, c0:c1], start=True, stop=True)
                    last.then_inc(b_dup, 1)

        def mean_square_q(p, i=None):
            def c(n):
                return at(p + n, i, 2)
            pe.wait_ge(a_qc, c(1))
            pe.wait_ge(a_sq, c(1))
            nc.tensor.matmul(B[0][:], SQ["ones64"], sqr[:, 0, :], start=True, stop=True).then_inc(a_ss, 1)

        def rotate_q(p, i=None):
            pe.wait_ge(a_qn, at(p + 1, i, 2))
            nc.tensor.matmul(B[0][:], SQ["rot"], tmp[:, 1, :], start=True, stop=True).then_inc(a_rot, 1)

        def pair(p, par, i=None, ahead=None):
            def c(per, n):
                return at(per * p + n, i, 2 * per)

            def scores(s):
                r, b = divmod(s, NB)
                if s >= 2:
                    pe.wait_ge(a_exp, c(8, s - 1))
                o = (2 + 2 * (s % 2)) * T
                h = slice(64 * r, 64 * r + 64)
                nc.tensor.matmul(ps[:, o:o + T], qr[h, par, b * P:(b + 1) * P], kcur[h, 0:T], start=True, stop=True)
                nc.tensor.matmul(ps[:, o + T:o + TA], qr[h, par, b * P:(b + 1) * P], kcur[h, T:TA], start=True, stop=True)\
                  .then_inc(a_s, 1)

            pe.wait_ge(a_qr, c(1, 1))
            pe.wait_ge(a_kv, at(p // 2 + 1, i, 1))
            scores(0)
            scores(1)
            for s in range(8):
                if ahead is not None:
                    if s == Q_AT:
                        pe.wait_ge(a_g, c(1, 1))
                        project(ahead, ah, al, [(B[0][:], 0, T)], i, 4)
                    if s == SS_AT:
                        mean_square_q(p + 1, i)
                    if s == ROT_AT:
                        rotate_q(p + 1, i)
                    if s == G_AT:
                        pe.wait_ge(a_qr, c(1, 2))
                        project(ahead + 1, ah, al, [(B[0][:], 0, T)], i, 4)
                pe.wait_ge(a_p, c(8, s + 1))
                if s:
                    pe.wait_ge(a_pt, c(8, s))
                for k in range(NCH):
                    last = nc.tensor.transpose(ps[:, 6 * T + k * P:6 * T + (k + 1) * P], pe2[:, s % 2, chunk(k)], ident)
                last.then_inc(a_t, 1)
                if s + 2 < 8:
                    scores(s + 2)
                if s % NB == NB - 1:
                    r = s // NB
                    pe.wait_ge(a_pt, c(8, s + 1))
                    if r == 0 and not (i is None and p == 0):
                        pe.wait_ge(a_o, c(1, 0))
                    for k in range(NCH):
                        last = nc.tensor.matmul(B[1][64 * r:64 * r + 64, :], vcur2[:, k, :], pT2[:, k, :], start=(k == 0),
                                                stop=(k == NCH - 1))
                    last.then_inc(a_pv, 1)

        pe.wait_ge(consts_in, 32)
        norm_sums("mem", TC)
        u = FIRST_UNIT["memkv"]
        pe.wait_ge(h_ready, 8)
        with pe.Fori(0, 4) as i:
            for j in range(4):
                pe.wait_ge(kv_copied, at(j + 1, i, 4))
                project(u + j, hh, hl, [(B[j][:, 0:TC], 0, TC)], i, 4)
                if j >= 2:
                    v = j - 2
                    pe.wait_ge(kv_copied, at(4 + 2 * v + 2, i, 4))
                    pe.wait_ge(kv_ready, at(v + 1, i, 2))
                    for kb in range(2):
                        last = nc.tensor.transpose(B[5 + v][:, kb * P:(kb + 1) * P], vt[:, v, kb * P:(kb + 1) * P], ident)
                    last.then_inc(kv_t, 1)

        if runs("ffn0"):
            pe.wait_ge(kv_copied, 4 + 16)
            pe.wait_ge(kv_ready, 2 + 8)
            pe.wait_ge(c_silu, 1)
            ffn(0, "ffn0", "ffn0")
        if runs("pool"):
            norm_sums("pool", T)
            n = NORM["pool"]
            u = FIRST_UNIT["pool"]
            order = ["u", "u", "u", "u", "q", "q", "w", "u", "u", "u", "u", "q", "q", "w"]
            t = 0
            mixed = 0
            pe.wait_ge(gated, 2 + 22)
            for v, kind in enumerate(order):
                if kind != "w":
                    if t >= 4:
                        pe.wait_ge(pool_copied, t - 3)
                    project(u + v, hh, hl, [(B[t % 4][:], 0, T)],
                            arrive=(lambda k: pe.wait_ge(h_ready, 8 * n + k + 1)) if v == 0 else None)
                    t += 1
                else:
                    plan = []
                    for b in range(8):
                        g, m, k = mixed + b // 4, b // 2 % 2, b % 2

                        def before(g=g, m=m, k=k):
                            if k == 0 and m == 0:
                                pe.wait_ge(pooled_lo, 2 * g + 2)
                                if g == 0:
                                    pe.wait_ge(rt_ready, n + 1)
                                if g >= 2:
                                    pe.wait_ge(mix_lo, 4)
                        plan.append((before, xoh[:, (2 * g + k) % 4, :], xol[:, (2 * g + k) % 4, :],
                                     B[4 + (2 * g + m) % 4][:], k == 0, k == 1))
                    blocks(u + v, plan)
                    mixed += 2
            pe.wait_ge(pool_copied, 12)
            pe.wait_ge(mix_lo, 8)
            memory_attention(0)
        if runs("pool_out"):
            u = FIRST_UNIT["pool_out"]
            done = xr(1, 0)
            with pe.Fori(0, 2) as i:
                for m in range(4):
                    def before(m=m, i=i):
                        pe.wait_ge(x_ready, at(done + m - 1, i, 4))
                    blocks(u + m, [(before if k == 0 else (lambda: None), fh[:, k, :], fl[:, k, :], B[m % 2][:],
                                    k == 0, k == KD - 1) for k in range(KD)], i, 4)
            out_memory(u + 8, done + 8, 1)
        if runs("ffn1"):
            ffn(1, "ffn1", "ffn1")
        if runs("ffn2"):
            ffn(2, "ffn2", "ffn2")
        if runs("diff"):
            norm_sums("diff", T)
            n = NORM["diff"]
            u = FIRST_UNIT["diff"]
            for b in range(3):
                if b == 2:
                    pe.wait_ge(d_copied, 1)
                project(u + b, hh, hl, [(B[b % 2][:], 0, T)],
                        arrive=(lambda k: pe.wait_ge(h_ready, 8 * n + k + 1)) if b == 0 else None)
            diff_head(0, 0, ahead=u + 3)
            with pe.Fori(0, 3) as i:
                diff_head(1, 1, i, ahead=u + 6, out=u + 9)
                diff_head(2, 0, i, ahead=u + 10, out=u + 13)
            diff_head(7, 1, out=u + 30)
            out_head(7, 1, u + 31)
            pe.wait_ge(d_rt, 8)
            for j in range(X_HEADS):
                project(u + 32 + j, hh, hl, [(B[j][:], 0, T)])
            pe.wait_ge(x_ready, xr(3, 1) + 64)
            pe.wait_ge(pool_copied, 16)
            memory_attention(1)
        if runs("diff_out"):
            out_memory(FIRST_UNIT["diff_out"], xr(3, 1) + 64, 2)
        if runs("ffn3"):
            ffn(3, "ffn3", "ffn3")
        if runs("mamba"):
            norm_sums("final", T)
            norm_sums("lat0", T)
            norm_sums("ctx0", TC)
            step_sizes()
            u = FIRST_UNIT["mamba"]
            for n in range(4):
                if n == 0:
                    pe.wait_ge(t_ready, 1)
                if n:
                    pe.wait_ge(m_cv, n)
                project(u + n, mh, ml, both(0))
            pe.wait_ge(m_cv, 4)
            group(0, z=u + 4, ahead=u + 6)
            with pe.Fori(0, MG - 2) as i:
                group(1, i, z=u + 10, out=u + 12, ahead=u + 14)
            group(MG - 1, z=u + 58, out=u + 60)
            group_out(MG - 1, None, u + 62)
            pe.wait_ge(m_sq, 2 * MG + 1)
            nc.tensor.matmul(B[2][:], ones, sqacc[:, 0:T], start=True, stop=True)
            nc.tensor.matmul(B[3][:, 0:TC], ones, sqacc[:, T:TA], start=True, stop=True).then_inc(m_ss, 1)
        if runs("attn_kv"):
            norm_sums("lat1", T)
            norm_sums("ctx1", TC)
            keys_values(FIRST_UNIT["attn_kv"])
            u = FIRST_UNIT["attn_qg"]
            pe.wait_ge(b_kd, 4)
            project(u, ah, al, [(B[0][:], 0, T)])
            mean_square_q(0)
            rotate_q(0)
            pe.wait_ge(a_qr, 1)
            project(u + 1, ah, al, [(B[0][:], 0, T)])
            with pe.Fori(0, 3) as i:
                pair(0, 0, i, ahead=u + 2)
                pair(1, 1, i, ahead=u + 4)
            pair(6, 0, ahead=u + 14)
            pair(7, 1)
            u = FIRST_UNIT["attn_out"]
            for m in range(KD):
                if m >= 2:
                    pe.wait_ge(x_ready, X_ATTN + m - 1)
                project(u + m, ah, al, [(B[2 + m % 2][:], 0, T)],
                        arrive=(lambda k: pe.wait_ge(a_ol, k + 1)) if m == 0 else None)
            norm_sums("last", T)

    @block.scalar
    def _(act):
        def split(u, i=None, per=0):
            if i is None and u >= total:
                return
            act.wait_ge(loaded[u % RAW], at(16 * (u // RAW + 1), i, 16 * per // RAW))
            if u >= RING:
                act.wait_ge(unit_done, at(u - RING + 1, i, per))
            nc.scalar.activation(wh[:, u % RING, :], raw[:, u % RAW, :], ACT.Copy).then_inc(s_hi, 1)

        def norm(name, src, width, ready, h0=0, eps=eps6, bias=None):
            n = NORM[name]
            for k in range(KD):
                act.wait_ge(*ready(k))
                if 8 * n + k >= 2:
                    act.wait_ge(sq_used, 8 * n + k - 1)
                nc.scalar.activation(sqr[:, k % 2, 0:width], src[:, k, 0:width], ACT.Square).then_inc(sq_ready, 1)
            act.wait_ge(sq_used, 8 * n + 8)
            nc.scalar.activation(rt[:, 0:width], B[7][:, 0:width], ACT.Sqrt, bias=eps[:, 0:1],
                                 scale=1.0 / D).then_inc(rt_ready, 1)

        def norm_hi(name, width, h0=0, bias=None, hh=hh):
            n = NORM[name] - (1 if NORM[name] > NORM["final"] else 0)
            for k in range(KD):
                act.wait_ge(tmp_ready, 8 * n + k + 1)
                if bias is None:
                    nc.scalar.activation(hh[:, k, h0:h0 + width], tmp[:, k % 2, 0:width], ACT.Copy).then_inc(h_hi, 1)
                else:
                    nc.scalar.activation(hh[:, k, h0:h0 + width], tmp[:, k % 2, 0:width], ACT.Identity,
                                         bias=bias(k)).then_inc(h_hi, 1)

        def x_blocks(done):
            return lambda k: (x_ready, done + k + 1)

        def ffn(f, name, norm_name, ready):
            norm(norm_name, x, T, ready)
            norm_hi(norm_name, T)
            u = FIRST_UNIT[name]
            pairs = f * sum(FF_PARTS)
            for p, w in enumerate(FF_PARTS):
                with act.Fori(0, w // 2) as i:
                    for jj in range(2):
                        g = u + 2 * jj
                        if w == KD and f < 3:
                            v = 16 * f + 8 * p + jj
                            act.wait_ge(mod_used, at(v + 1, i, 2))
                            act.dma_start(modw[:, jj:jj + 1, :], A["mod"][at(v, i, 2)].unsqueeze(1)).then_inc(mod_loaded[jj], 16)
                        act.wait_ge(unit_done, at(g + 1, i, 4))
                        nc.scalar.activation(sg[:, jj, :], B[2 * jj][:], ACT.Silu).then_inc(silu_ready, 1)
                        split(g + RING, i, 4)
                        split(g + 1 + RING, i, 4)
                        act.wait_ge(gated, at(2 + pairs + jj + 1, i, 2))
                        nc.scalar.activation(fh[:, bass.ds(i * 2 + jj, 1), :], tmp[:, jj:jj + 1, :], ACT.Copy)\
                           .then_inc(hid_hi, 1)
                u += 2 * w
                if w == KD:
                    with act.Fori(0, 2) as i:
                        for m in range(4):
                            split(u + m + RING, i, 4)
                else:
                    for v in range(w):
                        split(u + v + RING)
                u += w
                pairs += w

        def memory_attention(layer):
            with act.Fori(0, X_HEADS) as i:
                n = 16 * layer
                if True:
                    nc.scalar.activation(qcur[:, :].unsqueeze(1), qx[:, bass.ds(i, 1), :], ACT.Copy).then_inc(att_q, 1)

                def exps(b):
                    act.wait_ge(att_max, at(n + b + 1, i, 4))
                    if b >= 2:
                        act.wait_ge(att_t, at(n + b - 1, i, 4))
                    nc.scalar.activation(pexp[:, b % 2, 0:TC], B[4 + b % 2][:, 0:TC], ACT.Exp, bias=nm[:, b:b + 1],
                                         accum_out=rs[:, b:b + 1]).then_inc(att_exp, 1)

                def copy_out(b):
                    act.wait_ge(att_t, at(n + b + 1, i, 4))
                    nc.scalar.activation(pT[:, 0:2, b * P:(b + 1) * P],
                                         B[6 + b % 2][:, 0:2 * P].rearrange("p (k q) -> p k q", k=2),
                                         ACT.Copy).then_inc(att_pt, 1)
                exps(0)
                exps(1)
                copy_out(0)
                exps(2)
                copy_out(1)
                exps(3)
                copy_out(2)
                copy_out(3)
                act.wait_ge(att_o, at(X_HEADS * layer + 1, i, 1))
                nc.scalar.activation(xoh[:, bass.ds(i, 1), :], B[2][:].unsqueeze(1), ACT.Copy).then_inc(xo_hi, 1)

        def out_splits(u):
            with act.Fori(0, 2) as i:
                for m in range(4):
                    split(u + m + RING, i, 4)
            for v in range(4):
                split(u + 8 + v + RING)

        def diff_head(h, par, i=None, ahead=None, out=None):
            def c(n, per):
                return at(n, i, 2 * per)
            for b in range(NB):
                for r in range(2):
                    act.wait_ge(d_max, c(8 * h + 2 * b + r + 1, 8))
                    nc.scalar.activation(de[:, r, 0:(b + 1) * P], de[:, r, 0:(b + 1) * P], ACT.Exp, bias=dnm[:, r:r + 1],
                                         accum_out=drs[:, r:r + 1]).then_inc(d_exp, 1)
                if b < 3 and ahead is not None:
                    diff_copy(b, 1 - par, ahead + b, i)
                    split(ahead + b + RING, i, 8)
                if b == 3 and out is not None:
                    split(out + RING, i, 8)
                act.wait_ge(d_t, c(4 * h + b + 1, 4))
                nc.scalar.activation(dT[:, 0:b + 1, b * P:(b + 1) * P],
                                     B[4][:, 0:(b + 1) * P].rearrange("p (k q) -> p k q", q=P), ACT.Copy).then_inc(d_pt, 1)
            act.wait_ge(d_o, c(h + 1, 1))
            nc.scalar.activation(sqr[:, 0, :], B[5][:], ACT.Square).then_inc(d_sq, 1)
            act.wait_ge(d_ss, c(h + 1, 1))
            nc.scalar.activation(rt[:], B[1][:], ACT.Sqrt, bias=eps5[:, 0:1], scale=1.0 / P).then_inc(d_rt, 1)
            act.wait_ge(d_ot, c(h + 1, 1))
            nc.scalar.activation(fh[:, par, :], tmp[:, par, :], ACT.Copy).then_inc(d_ohi, 1)

        def diff_copy(b, par, u, i=None):
            act.wait_ge(unit_done, at(u + 1, i, 8))
            nc.scalar.activation((dq, dk, dv)[b][:, par, :], B[b % 2][:], ACT.Copy,
                                 scale=DIFF_SCALE if b == 0 else 1.0).then_inc(d_copied, 1)

        def step_sizes():
            f = lambda a: a.rearrange("p d c h -> p (d c h)")
            nc.scalar.activation(aexp, col("a_log", 0, 64), ACT.Exp).then_inc(t_a, 1)
            act.wait_ge(t_x, 1)
            nc.scalar.activation(f(ela), f(dt), ACT.Abs).then_inc(t_abs, 1)
            act.wait_ge(t_abs, 1)
            nc.scalar.activation(f(tend), f(ela), ACT.Exp, scale=-1.0).then_inc(t_exp, 1)
            act.wait_ge(t_exp, 1)
            nc.scalar.activation(f(cdec), f(tend), ACT.Ln, bias=one).then_inc(t_ln, 1)
            act.wait_ge(t_diff, 1)
            nc.scalar.activation(f(ela), f(la), ACT.Exp)
            nc.scalar.activation(f(tend), f(tend), ACT.Exp)
            nc.scalar.activation(f(cdec), B[2][:, 0:NCH * 64], ACT.Exp).then_inc(t_dec, 1)

        def copy_unit(n, u, i=None):
            act.wait_ge(unit_done, at(u + 1, i, 8))
            nc.scalar.activation(cvin[:, n, 2:2 + T], B[0][:], ACT.Copy)
            nc.scalar.activation(cvin[:, n, 4 + T:4 + TA], B[1][:, 0:TC], ACT.Copy).then_inc(m_cv, 1)

        def group(g, i=None, out=None, z=None, ahead=None):
            def c(per, n):
                return at(per * g + n, i, per)
            gg = g if i is None else i + g

            def convolved(n):
                act.wait_ge(m_acc, c(4, n + 1))
                to = (xs[:, 0], xs[:, 1], Bm, Cm)[n]
                k = COL["conv_b"] + ((gg * 2 + n) if n < 2 else (gg + 8 * n))
                for dst, a0, w in ((0, 0, T), (T, T + 2, TC)):
                    last = nc.scalar.activation(to[:, dst:dst + w], conv[n % 2][:, a0:a0 + w], ACT.Silu,
                                                bias=cols[:, bass.ds(k, 1)])
                last.then_inc(m_xbc, 1)

            def gate(j):
                act.wait_ge(unit_done, at(z + j + 1, i, 8))
                split(z + j + RING, i, 8)
                src = ps[:, 2 * j * T:2 * j * T + TA]
                nc.scalar.activation(zs[:, j, :], src, ACT.Silu).then_inc(m_z, 1)

            if not (i is None and g == 0):
                act.wait_ge(m_yl, c(2, 0))
            act.wait_ge(m_sq, c(2, 1))
            gate(0)
            convolved(0)
            convolved(1)
            gate(1)
            if out is not None:
                split(out + RING, i, 8)
            convolved(2)
            convolved(3)
            if out is not None:
                split(out + 1 + RING, i, 8)
            for n in range(5):
                act.wait_ge(m_tr, c(5, n + 1))
                if n < 2:
                    dst, src = xtok[:, 0:4, 2 * n:2 * n + 2, :], B[n][:].rearrange("p (c r e) -> p c r e", c=4, r=2)
                elif n == 2:
                    dst, src = btok[:, 0:4, :], B[2][:].rearrange("p (c n) -> p c n", c=4)
                elif n == 3:
                    for j in range(2):
                        last = nc.scalar.activation(xtok[:, 4:6, 2 * j:2 * j + 2, :],
                                                    B[3][:, 256 * j:256 * j + 256].rearrange("p (c r e) -> p c r e", c=2, r=2),
                                                    ACT.Copy)
                else:
                    dst, src = btok[:, 4:6, :], B[4][:, 0:256].rearrange("p (c n) -> p c n", c=2)
                if n != 3:
                    last = nc.scalar.activation(dst, src, ACT.Copy)
                last.then_inc(m_tok, 1)

            def exps(t):
                d, k = STEPS[t]
                act.wait_ge(m_cb, c(NS, t + 1))
                if t >= 4:
                    act.wait_ge(m_yp, c(NS, t - 3))
                for r in range(HPG):
                    last = nc.scalar.activation(decay[t % 4][:, chunk(r)], B[2 + t % 2][:, chunk(r)], ACT.Relu, scale=-1.0,
                                                bias=la[:, d, k, bass.ds(gg * HPG + r, 1)])
                last.then_inc(m_t, 1)
                act.wait_ge(m_t, c(NS, t + 1))
                nc.scalar.activation(decay[t % 4], decay[t % 4], ACT.Exp, scale=-1.0).then_inc(m_e, 1)
            exps(0)
            for t in range(NS):
                if t + 1 < NS:
                    exps(t + 1)
                if ahead is not None and t % 3 == 2:
                    n = t // 3
                    copy_unit(n, ahead + n, i)
                    split(ahead + n + RING, i, 8)
            for j in range(2):
                act.wait_ge(m_yg, c(2, j + 1))
                w = cols[:, bass.ds(COL["m_norm_w"] + gg * 2 + j, 1)]
                nc.scalar.activation(yh[:, j, :], zs[:, j, :], ACT.Copy, scale=w).then_inc(m_yh, 1)
                nc.scalar.activation(xs[:, j, :], zs[:, j, :], ACT.Square).then_inc(m_x, 1)

        def keys_values(u):
            for n in range(4):
                act.wait_ge(unit_done, u + n + 1)
                split(u + n + RING)
                src = ps[:, 2 * n * T:2 * n * T + TA]
                to = kraw[:, n] if n < 2 else vraw[:, n - 2]
                if n == 0:
                    nc.scalar.activation(ksq, src, ACT.Square).then_inc(b_sq, 1)
                nc.scalar.activation(to, src, ACT.Copy).then_inc(b_copied, 1)
            for j in range(2):
                act.wait_ge(b_ss, j + 1)
                nc.scalar.activation(krt, ps[:, 2 * j * T:2 * j * T + TA], ACT.Sqrt, bias=eps6[:, 0:1], scale=1.0 / 64)\
                  .then_inc(b_rt, 1)
                if j == 0:
                    act.wait_ge(b_copied, 2)
                    nc.scalar.activation(ksq, kraw[:, 1], ACT.Square).then_inc(b_sq, 1)
                act.wait_ge(b_vt, j + 1)
                nc.scalar.activation(vtok[:, :, j * P:(j + 1) * P],
                                     ps[:, (4 + 2 * j) * T:(4 + 2 * j) * T + TA].rearrange("p (c d) -> p c d", c=NCH),
                                     ACT.Copy).then_inc(b_v, 1)
                for r in range(2):
                    act.wait_ge(b_dup, 2 * j + r + 1)
                    nc.scalar.activation(kd[:, 2 * j + r], ps[:, (4 + 2 * j) * T:(4 + 2 * j) * T + TA], ACT.Copy).then_inc(b_kd, 1)

        def queries(p, u, i=None, per=4):
            act.wait_ge(unit_done, at(u + 1, i, per))
            split(u + RING, i, per)
            nc.scalar.activation(sqr[:, 0, :], B[0][:], ACT.Square).then_inc(a_sq, 1)
            nc.scalar.activation(tmp[:, 0, :], B[0][:], ACT.Copy).then_inc(a_qc, 1)

        def root_q(p, i=None):
            act.wait_ge(a_ss, at(p + 1, i, 2))
            nc.scalar.activation(rt[:], B[0][:], ACT.Sqrt, bias=eps6[:, 0:1], scale=1.0 / 64).then_inc(a_rt, 1)

        def gates(p, par, u, i=None, per=4):
            act.wait_ge(unit_done, at(u + 1, i, per))
            split(u + RING, i, per)
            nc.scalar.activation(gs[:, par, :], B[0][:], ACT.Silu).then_inc(a_g, 1)

        def pair(p, par, i=None, ahead=None):
            def c(per, n):
                return at(per * p + n, i, 2 * per)

            def exps(s):
                act.wait_ge(a_max, c(8, s + 1))
                if s >= 2:
                    act.wait_ge(a_t, c(8, s - 1))
                o = (2 + 2 * (s % 2)) * T
                nc.scalar.activation(pe2[:, s % 2, :], ps[:, o:o + TA], ACT.Exp, bias=nm2[:, s:s + 1],
                                     accum_out=rs2[:, s:s + 1]).then_inc(a_exp, 1)
            exps(0)
            for s in range(8):
                if s + 1 < 8:
                    exps(s + 1)
                if ahead is not None:
                    if s == Q_AT:
                        queries(p + 1, ahead, i)
                    if s == SS_AT:
                        root_q(p + 1, i)
                    if s == G_AT:
                        gates(p + 1, 1 - par, ahead + 1, i)
                elif s < 7:
                    out_half(s)
                act.wait_ge(a_t, c(8, s + 1))
                b = s % NB
                nc.scalar.activation(pT2[:, :, b * P:(b + 1) * P],
                                     ps[:, 6 * T:6 * T + TA].rearrange("p (k q) -> p k q", k=NCH), ACT.Copy).then_inc(a_pt, 1)

        def out_half(p):
            act.wait_ge(a_o, p + 1)
            nc.scalar.activation(ah[:, p, 0:T], og[:, p, :], ACT.Copy).then_inc(a_oh, 1)

        for u in range(RING):
            split(u)
        act.wait_ge(consts_in, 32)
        nc.scalar.activation(csil[:].rearrange("p k c -> p (k c)"), col("c", 0, 16), ACT.Silu).then_inc(c_silu, 1)
        act.wait_ge(s_init, 1)
        norm("mem", side, TC, lambda k: (side_in, 16))
        norm_hi("mem", TC)
        u = FIRST_UNIT["memkv"]
        with act.Fori(0, 4) as i:
            for j in range(4):
                split(u + j + RING, i, 4)
                act.wait_ge(unit_done, at(u + j + 1, i, 4))
                if j % 2 == 0:
                    dst = mk[:, bass.ds(i * 2 + j // 2, 1), :]
                else:
                    dst = vt[:, j // 2:j // 2 + 1, :]
                nc.scalar.activation(dst, B[j][:, 0:TC].unsqueeze(1), ACT.Copy).then_inc(kv_copied, 1)

        if runs("ffn0"):
            act.wait_ge(h_ready, 8)
            act.dma_start(side[:], A["ctxT"]).then_inc(ctx_in, 16)
            ffn(0, "ffn0", "ffn0", lambda k: (x_in, 16))
        if runs("pool"):
            norm("pool", x, T, x_blocks(xr(1, 0) - 8))
            norm_hi("pool", T)
            u = FIRST_UNIT["pool"]
            order = ["u", "u", "u", "u", "q", "q", "w", "u", "u", "u", "u", "q", "q", "w"]
            t = blk = head = 0

            halves = 0

            def pooled_half(b):
                act.wait_ge(pooled, b + 1)
                if b >= 4:
                    act.wait_ge(unit_done, u + 7)
                nc.scalar.activation(xoh[:, b % 4, :], tmp[:, b % 2, :], ACT.Copy).then_inc(pooled_hi, 1)

            for v, kind in enumerate(order):
                act.wait_ge(unit_done, u + v + 1)
                split(u + v + RING)
                if kind == "u":
                    if blk >= 2 and halves == blk - 2:
                        pooled_half(halves)
                        halves += 1
                    nc.scalar.activation(ubuf[:, blk % 2, PAD:], B[t % 4][:], ACT.Copy).then_inc(pool_copied, 1)
                    blk += 1
                    t += 1
                elif kind == "q":
                    nc.scalar.activation(qx[:, head, :], B[t % 4][:], ACT.Copy, scale=P ** -0.5).then_inc(pool_copied, 1)
                    head += 1
                    t += 1
                    while head % 2 == 0 and halves < blk:
                        pooled_half(halves)
                        halves += 1
                else:
                    for m in range(blk - 4, blk):
                        nc.scalar.activation(fh[:, m, :], B[4 + m % 4][:], ACT.Copy,
                                             scale=col("pool_scale", m)).then_inc(mix_hi, 1)
            memory_attention(0)
        if runs("pool_out"):
            out_splits(FIRST_UNIT["pool_out"])
        if runs("ffn1"):
            ffn(1, "ffn1", "ffn1", x_blocks(xr(1, 1) - 8))
        if runs("ffn2"):
            ffn(2, "ffn2", "ffn2", x_blocks(xr(2, 1) - 8))
        if runs("diff"):
            norm("diff", x, T, x_blocks(xr(3, 1) - 8))
            act.wait_ge(lam_sums, 1)
            nc.scalar.activation(lame[:], lams[:], ACT.Exp).then_inc(lam_exp, 1)
            norm_hi("diff", T)
            u = FIRST_UNIT["diff"]
            for b in range(3):
                diff_copy(b, 0, u + b)
                split(u + b + RING)
            diff_head(0, 0, ahead=u + 3)
            with act.Fori(0, 3) as i:
                diff_head(1, 1, i, ahead=u + 6, out=u + 9)
                diff_head(2, 0, i, ahead=u + 10, out=u + 13)
            diff_head(7, 1, out=u + 30)
            split(u + 31 + RING)
            for j in range(X_HEADS):
                act.wait_ge(unit_done, u + 32 + j + 1)
                split(u + 32 + j + RING)
                nc.scalar.activation(qx[:, j, :], B[j][:], ACT.Copy, scale=P ** -0.5).then_inc(pool_copied, 1)
            memory_attention(1)
        if runs("diff_out"):
            u = FIRST_UNIT["diff_out"]
            for v in range(4):
                split(u + v + RING)
        if runs("ffn3"):
            ffn(3, "ffn3", "ffn3", x_blocks(xr(3, 2) - 8))
        if runs("final"):
            norm("final", x, T, x_blocks(xr(4, 2) - 8))
        if runs("mamba"):
            norm("lat0", x, T, x_blocks(xr(4, 2)))
            norm_hi("lat0", T, 0, lambda k: modv[:, k, 0:1], mh)
            act.wait_ge(tmp_ready, 8 * NORM["lat0"])
            act.dma_start(A["park"], x[:]).then_inc(parked, 16)
            act.dma_start(wdt, A["wdt"]).then_inc(wdt_in, 16)
            norm("ctx0", side, TC, lambda k: (ctx_in, 16))
            norm_hi("ctx0", TC, T, lambda k: modv[:, k, 1:2], mh)
            step_sizes()
            u = FIRST_UNIT["mamba"]
            act.wait_ge(cv_zero, 1)
            act.wait_ge(parked, 16)
            for n in range(4):
                copy_unit(n, u + n)
                split(u + n + RING)
            group(0, z=u + 4, ahead=u + 6)
            with act.Fori(0, MG - 2) as i:
                group(1, i, z=u + 10, out=u + 12, ahead=u + 14)
            group(MG - 1, z=u + 58, out=u + 60)
            for n in range(2):
                split(u + 62 + n + RING)
            act.wait_ge(m_yp, NS * MG)
            act.wait_ge(m_yt, 2 * MG)
            act.dma_start(x[:], A["park"]).then_inc(parked, 16)
            act.wait_ge(m_y, NS * MG)
            act.dma_start(side[:], A["ctxT"]).then_inc(ctx_in, 16)
            act.wait_ge(m_ss, 1)
            nc.scalar.activation(rt[:], B[2][:], ACT.Sqrt, bias=eps6[:, 0:1], scale=1.0 / (2 * D))
            nc.scalar.activation(tmp[:, 0, 0:TC], B[3][:, 0:TC], ACT.Sqrt, bias=eps6[:, 0:1],
                                 scale=1.0 / (2 * D)).then_inc(m_rt, 1)
        if runs("attn_kv"):
            act.dma_start(cos[:], A["cos"]).then_inc(cs_in, 16)
            act.dma_start(sin[:], A["sin"]).then_inc(cs_in, 16)
            norm("lat1", x, T, x_blocks(X_ATTN - 8))
            norm_hi("lat1", T, 0, lambda k: modv[:, 24 + k, 0:1], ah)
            norm("ctx1", side, TC, lambda k: (ctx_ready, k + 1))
            norm_hi("ctx1", TC, T, lambda k: modv[:, 24 + k, 1:2], ah)
            keys_values(FIRST_UNIT["attn_kv"])
            u = FIRST_UNIT["attn_qg"]
            queries(0, u)
            root_q(0)
            gates(0, 0, u + 1)
            with act.Fori(0, 3) as i:
                pair(0, 0, i, ahead=u + 2)
                pair(1, 1, i, ahead=u + 4)
            pair(6, 0, ahead=u + 14)
            act.wait_ge(unit_done, u + 16)
            pair(7, 1)
            out_half(7)
            for n in range(4):
                split(FIRST_UNIT["attn_out"] + RING + n)
            norm("last", x, T, x_blocks(X_ATTN))

    @block.vector
    def _(dve):
        link = Link(dve, s_chain)

        def norm(name, src, width, gain, h0=0, bias=None, hh=hh, hl=hl):
            n0 = NORM[name]
            n = n0 - (1 if n0 > NORM["final"] else 0)
            dve.wait_ge(rt_ready, n0 + 1)
            link(nc.vector.reciprocal(rstd[:, 0:width], rt[:, 0:width]))

            def rest(k):
                dve.wait_ge(h_hi, 8 * n + k + 1)
                half = hh[:, k, h0:h0 + width].bitcast(FP32)
                if bias is None:
                    ins = nc.vector.tensor_tensor(hl[:, k, h0:h0 + width], tmp[:, k % 2, 0:width], half, ALU.subtract)
                else:
                    ins = nc.vector.scalar_tensor_tensor(hl[:, k, h0:h0 + width], tmp[:, k % 2, 0:width], bias(k),
                                                         half, ALU.add, ALU.subtract)
                ins.then_inc(h_ready, 1)
            for k in range(KD):
                if k >= 2:
                    dve.wait_ge(h_ready, 8 * n + k - 1)
                nc.vector.scalar_tensor_tensor(tmp[:, k % 2, 0:width], src[:, k, 0:width], gain(k), rstd[:, 0:width],
                                               ALU.mult, ALU.mult).then_inc(tmp_ready, 1)
                if k >= 1:
                    rest(k - 1)
            rest(KD - 1)

        def ffn(f, name, norm_name, gain):
            norm(norm_name, x, T, gain)
            u = FIRST_UNIT[name]
            pairs = f * sum(FF_PARTS)
            for p, w in enumerate(FF_PARTS):
                with dve.Fori(0, w // 2) as i:
                    for jj in range(2):
                        dve.wait_ge(silu_ready, at(pairs + jj + 1, i, 2))
                        dve.wait_ge(unit_done, at(u + 2 * jj + 2, i, 4))
                        nc.vector.tensor_tensor(tmp[:, jj, :], sg[:, jj, :], B[2 * jj + 1][:], ALU.mult).then_inc(gated, 1)
                        dve.wait_ge(hid_hi, at(pairs + jj + 1, i, 2))
                        nc.vector.tensor_tensor(fl[:, bass.ds(i * 2 + jj, 1), :], tmp[:, jj:jj + 1, :],
                                                fh[:, bass.ds(i * 2 + jj, 1), :].bitcast(FP32), ALU.subtract)\
                          .then_inc(hid_lo, 1)
                        dve.wait_ge(hid_lo, at(pairs + jj + 1, i, 2))
                u += 2 * w

                if p == 1 and f < 3:
                    dve.wait_ge(mod_used, 2 + 16 * (f + 1))
                    nc.vector.tensor_tensor(modv[:, 16 * f:16 * f + 16], B[6][:, 32 * f:32 * f + 32].rearrange("p (m c) -> p m c", c=2),
                                            col("mod_b_2", 16 * f, 16).unsqueeze(2).to_broadcast([P, 16, 2]), ALU.add)\
                      .then_inc(mod_read, 1)
                    if f == 2:
                        dve.wait_ge(mod_read, 3)
                        for layer in range(2):
                            for r in range(2):
                                nc.vector.scalar_tensor_tensor(gmod[:, 8 * layer:8 * layer + 8, r],
                                                               modv[:, 24 * layer + 8:24 * layer + 16, r], 1.0,
                                                               col("norm_w_2", 8 * layer, 8), ALU.add, ALU.mult)\
                                  .then_inc(gmod_ready, 1)

                def add(m, slot, unit, i=None, per=0):
                    dve.wait_ge(unit_done, at(unit + 1, i, per))
                    nc.vector.scalar_tensor_tensor(x[:, m, :], B[4 + slot][:].unsqueeze(1), 0.5, x[:, m, :],
                                                   ALU.mult, ALU.add).then_inc(x_ready, 1)
                if w == KD:
                    with dve.Fori(0, 2) as i:
                        for m in range(4):
                            add(bass.ds(i * 4 + m, 1), m % 2, u + m, i, 4)
                else:
                    for m in range(KD):
                        add(slice(m, m + 1), m % 2, u + (w * m + w - 1) // 8)
                u += w
                pairs += w

        def memory_attention(layer):
            with dve.Fori(0, X_HEADS) as i:
                link.enter(i, 4)
                n = 16 * layer
                nc.vector.tensor_copy(vcur[:].unsqueeze(1), mv[:, bass.ds(i + X_HEADS * layer, 1), :, :]).then_inc(att_v, 1)

                def maximum(b):
                    dve.wait_ge(att_s, at(n + b + 1, i, 4))
                    nc.vector.tensor_reduce(nm[:, b:b + 1], B[4 + b % 2][:, 0:TC], AX.X, ALU.max, negate=True)\
                      .then_inc(att_max, 1)

                def normalize(b):
                    dve.wait_ge(att_exp, at(n + b + 1, i, 4))
                    link(nc.vector.reciprocal(rr[:, b:b + 1], rs[:, b:b + 1]))
                    nc.vector.tensor_scalar(pexp[:, b % 2, 0:TC], pexp[:, b % 2, 0:TC], rr[:, b:b + 1], None,
                                            ALU.mult).then_inc(att_p, 1)
                maximum(0)
                maximum(1)
                normalize(0)
                maximum(2)
                normalize(1)
                maximum(3)
                normalize(2)
                normalize(3)
                dve.wait_ge(xo_hi, at(X_HEADS * layer + 1, i, 1))
                nc.vector.tensor_tensor(xol[:, bass.ds(i, 1), :], B[2][:].unsqueeze(1),
                                        xoh[:, bass.ds(i, 1), :].bitcast(FP32), ALU.subtract).then_inc(xo_lo, 1)
                link.leave(X_HEADS)

        def out_memory(u):
            for m in range(KD):
                dve.wait_ge(unit_done, u + m // 2 + 1)
                nc.vector.tensor_tensor(x[:, m, :], B[m % 2][:], x[:, m, :], ALU.add).then_inc(x_ready, 1)

        def diff_head(h, par, i=None, ahead=None, out=None):
            def c(n, per):
                return at(n, i, 2 * per)
            dve.wait_ge(d_vt, c(h + 1, 1))
            nc.vector.tensor_copy(dvt[:].rearrange("p k d -> p (k d)"), B[4][:]).then_inc(d_vtok, 1)
            hcol = h if i is None else i * 2 + h
            for b in range(NB):
                n = (b + 1) * P
                if not (i is None and h == 0 and b == 0):
                    dve.wait_ge(d_w, c(4 * h + b, 4))
                for r in range(2):
                    dve.wait_ge(d_s, c(8 * h + 2 * b + r + 1, 8))
                    nc.vector.scalar_tensor_tensor(de[:, r, 0:n], dist[:, T - n:T], cols[:, bass.ds(hcol + COL["slopes"], 1)],
                                                   B[2 + r][:, 0:n], ALU.mult, ALU.add).then_inc(d_biased, 1)
                for r in range(2):
                    dve.wait_ge(d_biased, c(8 * h + 2 * b + r + 1, 8))
                    nc.vector.tensor_reduce(dnm[:, r:r + 1], de[:, r, 0:n], AX.X, ALU.max, negate=True).then_inc(d_max, 1)
                dve.wait_ge(d_exp, c(8 * h + 2 * b + 2, 8))
                link(nc.vector.reciprocal(drr[:], drs[:]))
                link(nc.vector.tensor_tensor(drl[:], drr[:, 1:2], lam[:], ALU.mult))
                link(nc.vector.tensor_scalar(de[:, 1, 0:n], de[:, 1, 0:n], drl[:, 0:1], None, ALU.mult))
                if b:
                    dve.wait_ge(d_t, c(4 * h + b, 4))
                nc.vector.scalar_tensor_tensor(dw[:, 0:n], de[:, 0, 0:n], drr[:, 0:1], de[:, 1, 0:n],
                                               ALU.mult, ALU.subtract).then_inc(d_w, 1)
            if out is not None:
                out_head(h - 1, out, i)
            dve.wait_ge(d_rt, c(h + 1, 1))
            link(nc.vector.reciprocal(rstd[:], rt[:]))
            nc.vector.scalar_tensor_tensor(tmp[:, par, :], B[5][:], dgain[:, 0:1], rstd[:], ALU.mult, ALU.mult)\
              .then_inc(d_ot, 1)
            dve.wait_ge(d_ohi, c(h + 1, 1))
            nc.vector.tensor_tensor(fl[:, par, :], tmp[:, par, :], fh[:, par, :].bitcast(FP32), ALU.subtract).then_inc(d_olo, 1)

        def out_head(h, u, i=None):
            for m in range(KD):
                if m < KD - 1:
                    dve.wait_ge(d_m, at(7 * h + m + 1, i, 14))
                else:
                    dve.wait_ge(unit_done, at(u + 1, i, 8))
                nc.vector.tensor_tensor(x[:, m, :], B[6 + m % 2][:], x[:, m, :], ALU.add).then_inc(x_ready, 1)

        def keys_values():
            link(nc.vector.tensor_scalar(aqg[:], col("a_q_norm"), A_SCALE, None, ALU.mult))
            dve.wait_ge(cs_in, 32)
            for j in range(2):
                dve.wait_ge(b_rt, j + 1)
                link(nc.vector.reciprocal(krs, krt))
                nc.vector.scalar_tensor_tensor(kn, kraw[:, j], col("a_k_norm"), krs, ALU.mult, ALU.mult).then_inc(b_kn, 1)
                dve.wait_ge(b_kn, j + 1)
                link(nc.vector.tensor_tensor(kraw[:, j, 0:T], kn[:, 0:T], cos[:], ALU.mult))
                nc.vector.tensor_copy(kraw[:, j, T:TA], kn[:, T:TA])
                dve.wait_ge(b_rot, j + 1)
                link(nc.vector.tensor_tensor(krs[:, 0:T], B[2 * j][:], sin[:], ALU.mult))
                nc.vector.tensor_tensor(kraw[:, j, 0:T], kraw[:, j, 0:T], krs[:, 0:T], ALU.add).then_inc(b_kr, 1)
                dve.wait_ge(b_kr, j + 1)

        def normed_q(p, i=None):
            dve.wait_ge(a_rt, at(p + 1, i, 2))
            link(nc.vector.reciprocal(rstd[:], rt[:]))
            nc.vector.scalar_tensor_tensor(tmp[:, 1, :], tmp[:, 0, :], aqg[:, 0:1], rstd[:], ALU.mult, ALU.mult).then_inc(a_qn, 1)

        def rotated_q(p, par, i=None):
            dve.wait_ge(a_qn, at(p + 1, i, 2))
            link(nc.vector.tensor_tensor(qr[:, par, :], tmp[:, 1, :], cos[:], ALU.mult))
            dve.wait_ge(a_rot, at(p + 1, i, 2))
            link(nc.vector.tensor_tensor(sqr[:, 1, :], B[0][:], sin[:], ALU.mult))
            nc.vector.tensor_tensor(qr[:, par, :], qr[:, par, :], sqr[:, 1, :], ALU.add).then_inc(a_qr, 1)

        def pair(p, par, i=None, ahead=None):
            def c(per, n):
                return at(per * p + n, i, 2 * per)
            if p % 2 == 0:
                if not (i is None and p == 0):
                    dve.wait_ge(a_pv, at(2 * p + 2, i, 4))
                gk = p // 2 if i is None else i + p // 2
                nc.vector.tensor_copy(kcur[:].unsqueeze(1), kd[:, bass.ds(gk, 1), :])
                nc.vector.tensor_copy(vcur2[:], vtok[:, :, bass.ds(gk * 64, 64)]).then_inc(a_kv, 1)

            def maximum(s):
                dve.wait_ge(a_s, c(8, s + 1))
                o = (2 + 2 * (s % 2)) * T
                nc.vector.tensor_reduce(nm2[:, s:s + 1], ps[:, o:o + TA], AX.X, ALU.max, negate=True).then_inc(a_max, 1)
            maximum(0)
            maximum(1)
            for s in range(8):
                dve.wait_ge(a_exp, c(8, s + 1))
                link(nc.vector.reciprocal(rr2[:, s:s + 1], rs2[:, s:s + 1]))
                nc.vector.tensor_scalar(pe2[:, s % 2, :], pe2[:, s % 2, :], rr2[:, s:s + 1], None, ALU.mult).then_inc(a_p, 1)
                if s + 2 < 8:
                    maximum(s + 2)
                if ahead is not None:
                    if s == SS_AT:
                        normed_q(p + 1, i)
                    if s == ROT_AT:
                        rotated_q(p + 1, 1 - par, i)
                elif s < 7:
                    out_rest(s)
            dve.wait_ge(a_pv, at(2 * p + 2 + 2, i, 4))
            dve.wait_ge(a_g, c(1, 1))
            nc.vector.tensor_tensor(og[:, bass.ds(p if i is None else i * 2 + p, 1), :], B[1][:].unsqueeze(1),
                                    gs[:, par:par + 1, :], ALU.mult).then_inc(a_o, 1)

        def out_rest(p):
            dve.wait_ge(a_oh, p + 1)
            nc.vector.tensor_tensor(al[:, p, 0:T], og[:, p, :], ah[:, p, 0:T].bitcast(FP32), ALU.subtract).then_inc(a_ol, 1)

        def norm_in_place(name, gain="final_norm_g"):
            dve.wait_ge(rt_ready, NORM[name] + 1)
            link(nc.vector.reciprocal(rstd[:], rt[:]))
            for k in range(KD):
                nc.vector.scalar_tensor_tensor(x[:, k, :], x[:, k, :], col(gain, k), rstd[:],
                                               ALU.mult, ALU.mult).then_inc(x_ready, 1)

        def step_sizes():
            f = lambda a: a.rearrange("p d c h -> p (d c h)")
            n = NCH * 64
            heads = [P, NCH, 32]
            dve.wait_ge(t_dt, 1)
            for d in range(2):
                last = nc.vector.tensor_tensor(dt[:, d], B[0][:, d * n // 2:(d + 1) * n // 2].rearrange("p (c h) -> p c h", c=NCH),
                                               col("dt_bias", 32 * d, 32).unsqueeze(1).to_broadcast(heads), ALU.add)
            last.then_inc(t_x, 1)
            dve.wait_ge(t_ln, 1)
            link(nc.vector.scalar_tensor_tensor(f(dt), f(dt), 0.0, f(cdec), ALU.max, ALU.add))
            dve.wait_ge(t_a, 1)
            for d in range(2):
                link(nc.vector.tensor_tensor(da[:, d], dt[:, d], aexp[:, 32 * d:32 * d + 32].unsqueeze(1).to_broadcast(heads),
                                             ALU.mult))
            nc.vector.tensor_scalar(f(da[:]), f(da[:]), -1.0, None, ALU.mult).then_inc(t_da, 1)
            dve.wait_ge(t_cum, 1)
            link(nc.vector.tensor_copy(f(la), B[1][:, 0:n]))
            nc.vector.tensor_tensor(f(tend), B[2][:, 0:n], f(la), ALU.subtract).then_inc(t_diff, 1)
            dve.wait_ge(t_dec, 1)
            nc.vector.tensor_tensor(f(tend), f(tend), f(dt), ALU.mult).then_inc(t_ready, 1)

        def group(g, i=None, out=None, z=None, ahead=None):
            def c(per, n):
                return at(per * g + n, i, per)
            gg = g if i is None else i + g

            def per_head(a, d, k):
                return a[:, d, k, bass.ds(gg * HPG, HPG)].unsqueeze(2).to_broadcast([P, HPG, 64])

            nc.vector.tensor_copy(dag[:].rearrange("p d c r -> p (d c) r"),
                                  da[:, :, :, bass.ds(gg * HPG, HPG)].rearrange("p d c r -> p (d c) r")).then_inc(m_dag, 1)
            dve.wait_ge(m_cv, c(4, 4))
            done = {}

            def taps(tap, pair):
                for n in pair:
                    k = (gg * 2 + n) if n < 2 else (gg + 8 * n)
                    to = conv[n % 2]
                    w = cols[:, bass.ds(COL["conv_w"] + 32 * tap + k, 1)]
                    src = cvin[:, n, tap:tap + TA + 2]
                    if tap == 0:
                        if n >= 2:
                            dve.wait_ge(m_xbc, c(4, n - 1))
                        ins = nc.vector.tensor_scalar(to, src, w, None, ALU.mult)
                    else:
                        link.until(done[n])
                        ins = nc.vector.scalar_tensor_tensor(to, src, w, to, ALU.mult, ALU.add)
                    if tap < 4:
                        done[n] = link.mark(ins)
                    else:
                        ins.then_inc(m_acc, 1)

            for tap in range(5):
                taps(tap, (0, 1))
            for tap, adds in enumerate(((), (0,), (1, 2), (3, 4), (5, 6, 7))):
                taps(tap, (2, 3))
                if out is not None:
                    for m in adds:
                        group_add(g - 1, i, out, m)
            dve.wait_ge(m_py, c(1, 1))

            def weigh(t):
                d, k = STEPS[t]
                dve.wait_ge(m_cb, c(NS, t + 1))
                if not (i is None and g == 0 and t == 0):
                    dve.wait_ge(m_w, c(NS, t))
                link(nc.vector.tensor_tensor(cbm, B[4 + t % 2][:, 0:P], SQ["from" if d else "upto"], ALU.mult))
                dve.wait_ge(m_e, c(NS, t + 1))
                e = decay[t % 4].rearrange("p (r l) -> p r l", r=HPG)
                nc.vector.tensor_tensor(e, e, cbm.unsqueeze(1).to_broadcast([P, HPG, P]), ALU.mult).then_inc(m_w, 1)

            def update(t):
                d, k = STEPS[t]
                if t % NCH == NCH - 1:
                    return
                n = updates(t)
                dve.wait_ge(m_cb, c(NS, t + 1))
                st = B[4 + t % 2][:, P:P + 256].rearrange("p (r e) -> p r e", r=HPG)
                if t % NCH == 0:
                    nc.vector.tensor_copy(state[:, n % 2], st).then_inc(m_st, 1)
                else:
                    dve.wait_ge(m_st, c(updates(NS - 1), n - 1))
                    link(nc.vector.tensor_tensor(state[:, n % 2], state[:, 1 - n % 2], per_head(cdec, d, k), ALU.mult))
                    nc.vector.tensor_tensor(state[:, n % 2], st, state[:, n % 2], ALU.add).then_inc(m_st, 1)

            def output(t):
                d, k = STEPS[t]
                dve.wait_ge(m_yp, c(NS, t + 1))
                if not (i is None and g == 0 and t == 0):
                    dve.wait_ge(m_y, c(NS, t))
                bank = B[6 + t % 2]
                inner = bank[:, 0:256].rearrange("p (r e) -> p r e", r=HPG)
                if t % NCH:
                    link.mark(nc.vector.tensor_tensor(yt[:], bank[:, 256:512].rearrange("p (r e) -> p r e", r=HPG),
                                                      per_head(ela, d, k), ALU.mult))
                    link(nc.vector.tensor_tensor(ytok[:, k], inner, ytok[:, k], ALU.add))
                    nc.vector.tensor_tensor(ytok[:, k], ytok[:, k], yt[:], ALU.add).then_inc(m_y, 1)
                else:
                    nc.vector.tensor_tensor(ytok[:, k], inner, ytok[:, k], ALU.add).then_inc(m_y, 1)

            weigh(0)
            for t in range(NS):
                update(t)
                output(t)
                if t + 1 < NS:
                    weigh(t + 1)
            for j in range(2):
                dve.wait_ge(m_yt, c(2, j + 1))
                lat, con = (B[6], B[7]) if j == 0 else (B[4], B[5])
                link(nc.vector.tensor_tensor(zs[:, j, 0:T], lat[:], zs[:, j, 0:T], ALU.mult))
                nc.vector.tensor_tensor(zs[:, j, T:TA], con[:, 0:TC], zs[:, j, T:TA], ALU.mult).then_inc(m_yg, 1)
            for j in range(2):
                dve.wait_ge(m_yh, c(2, j + 1))
                w = cols[:, bass.ds(COL["m_norm_w"] + gg * 2 + j, 1)]
                nc.vector.scalar_tensor_tensor(yl[:, j, :], zs[:, j, :], w, yh[:, j, :].bitcast(FP32),
                                               ALU.mult, ALU.subtract).then_inc(m_yl, 1)

        def group_add(g, i, u, m):
            if m % 4 < 3:
                dve.wait_ge(m_om, at(6 * g + 3 * (m // 4) + m % 4 + 1, i, 6))
            else:
                dve.wait_ge(unit_done, at(u + m // 4 + 1, i, 8))
            lat, con = (B[6], B[7]) if m % 2 == 0 else (B[4], B[5])
            nc.vector.tensor_tensor(acc[:, m, 0:T], lat[:], acc[:, m, 0:T], ALU.add)
            nc.vector.tensor_tensor(acc[:, m, T:TA], con[:, 0:TC], acc[:, m, T:TA], ALU.add).then_inc(m_add, 1)

        nc.vector.memset(eps6[:], 1e-6)
        nc.vector.memset(eps5[:], 1e-5).then_inc(s_init, 1)
        free = 0
        for signal, banks in ((gated, 2), (x_ready, X0), (kv_ready, 2), (kv_copied, 4), (mod_used, 2)):
            for _ in range(banks):
                nc.vector.memset(credit[:, free:free + 1], 0.0).then_inc(signal, 1)
                free += 1
        dve.wait_ge(consts_in, 32)
        dve.wait_ge(side_in, 16)
        norm("mem", side, TC, lambda k: col("mem_norm_g", k))
        u = FIRST_UNIT["memkv"]
        with dve.Fori(0, 4) as i:
            for v in range(2):
                dve.wait_ge(kv_t, at(v + 1, i, 2))
                nc.vector.tensor_copy(mv[:, bass.ds(i * 2 + v, 1), :, :],
                                      B[5 + v][:, 0:TC].rearrange("p (o k d) -> p o k d", o=1, k=2)).then_inc(kv_ready, 1)

        if runs("ffn0"):
            dve.wait_ge(x_in, 16)
            ffn(0, "ffn0", "ffn0", lambda k: col("norm_g", k))
        if runs("pool"):
            norm("pool", x, T, lambda k: col("norm_g", 8 + k))
            nc.vector.memset(ubuf[:, :, 0:PAD], 0.0)
            nc.vector.memset(pa[:, 0:PAD], 0.0)
            link(nc.vector.memset(pb_[:, 0:PAD], 0.0))
            u = FIRST_UNIT["pool"]
            copied = [1, 2, 3, 4, 7, 8, 9, 10]

            def half(b):
                dve.wait_ge(pooled_hi, b + 1)
                nc.vector.tensor_tensor(xol[:, b % 4, :], tmp[:, b % 2, :], xoh[:, b % 4, :].bitcast(FP32),
                                        ALU.subtract).then_inc(pooled_lo, 1)

            def mixed(m):
                dve.wait_ge(mix_hi, m + 1)
                nc.vector.scalar_tensor_tensor(fl[:, m, :], B[4 + m % 4][:], col("pool_scale", m),
                                               fh[:, m, :].bitcast(FP32), ALU.mult, ALU.subtract).then_inc(mix_lo, 1)
            for b in range(KD):
                if b == 2 * 2:
                    half(2)
                    half(3)
                    for m in range(4):
                        mixed(m)
                elif b >= 2 and b != 5:
                    half(b - 2)
                w = POOL_WINDOWS[b // 2]
                if b >= 1:
                    dve.wait_ge(pooled, b)
                if b >= 2:
                    dve.wait_ge(pooled_lo, b - 1)
                dve.wait_ge(pool_copied, copied[b])
                s, d, to = ubuf[:, b % 2, :], 1, pa
                while d < w:
                    link(nc.vector.tensor_tensor(to[:, PAD:], s[:, PAD:], s[:, PAD - d:PAD + T - d], ALU.add))
                    s, to, d = to, (pb_ if to is pa else pa), 2 * d
                c = ubuf[:, b % 2, :]
                link(nc.vector.scalar_tensor_tensor(tmp[:, b % 2, :], s[:, PAD:], 1.0 / w, c[:, PAD:],
                                                    ALU.mult, ALU.subtract))
                link(nc.vector.tensor_tensor(to[:, PAD:PAD + w], s[:, PAD:PAD + w],
                                             col("pool_rcount", 16 * (b // 2), w), ALU.mult))
                nc.vector.tensor_tensor(tmp[:, b % 2, 0:w], to[:, PAD:PAD + w], c[:, PAD:PAD + w],
                                        ALU.subtract).then_inc(pooled, 1)
            half(6)
            half(7)
            for m in range(4, 8):
                mixed(m)
            memory_attention(0)
        if runs("pool_out"):
            u = FIRST_UNIT["pool_out"]
            with dve.Fori(0, 2) as i:
                for m in range(4):
                    dve.wait_ge(unit_done, at(u + m + 1, i, 4))
                    nc.vector.tensor_tensor(x[:, bass.ds(i * 4 + m, 1), :], B[m % 2][:].unsqueeze(1),
                                            x[:, bass.ds(i * 4 + m, 1), :], ALU.add).then_inc(x_ready, 1)
            out_memory(u + 8)
        if runs("ffn1"):
            ffn(1, "ffn1", "ffn1", lambda k: col("norm_g", 16 + k))
        if runs("ffn2"):
            ffn(2, "ffn2", "ffn2", lambda k: col("norm_g", 24 + k))
        if runs("diff"):
            dve.wait_ge(dist_in, 16)
            lp = col("diff_lambda", 0, 256).rearrange("p (a b d) -> p a b d", a=2, b=2)
            link(nc.vector.tensor_tensor(lamt[:], lp[:, :, 0, :], lp[:, :, 1, :], ALU.mult))
            nc.vector.tensor_reduce(lams[:], lamt[:], AX.X, ALU.add).then_inc(lam_sums, 1)
            dve.wait_ge(lam_exp, 1)
            link(nc.vector.tensor_tensor(lam[:], lame[:, 0:1], lame[:, 1:2], ALU.subtract))
            link(nc.vector.tensor_scalar(lam[:], lam[:], LAM_INIT, None, ALU.add))
            link(nc.vector.tensor_scalar(dgain[:], col("diff_norm_g"), 1.0 - LAM_INIT, None, ALU.mult))
            norm("diff", x, T, lambda k: col("norm_g", 32 + k))
            u = FIRST_UNIT["diff"]
            diff_head(0, 0)
            with dve.Fori(0, 3) as i:
                link.enter(i, 2 * (3 * NB + 1))
                diff_head(1, 1, i, out=u + 9)
                diff_head(2, 0, i, out=u + 13)
                link.leave(3)
            diff_head(7, 1, out=u + 30)
            out_head(7, u + 31)
            memory_attention(1)
        if runs("diff_out"):
            out_memory(FIRST_UNIT["diff_out"])
        if runs("ffn3"):
            ffn(3, "ffn3", "ffn3", lambda k: col("norm_g", 40 + k))
        if runs("mamba"):
            norm_in_place("final")
            dve.wait_ge(gmod_ready, 4)
            dve.wait_ge(x_ready, xr(4, 2) + 8)
            norm("lat0", x, T, lambda k: gmod[:, k, 0:1], 0, lambda k: modv[:, k, 0:1], mh, ml)
            norm("ctx0", side, TC, lambda k: gmod[:, k, 1:2], T, lambda k: modv[:, k, 1:2], mh, ml)
            for n, (w, at0) in enumerate(((2, 0), (2, 2 + T), (2, 4 + TA))):
                link(nc.vector.memset(cvin[:, :, at0:at0 + w], 0.0))
            nc.vector.memset(credit[:, 29:30], 0.0).then_inc(cv_zero, 1)
            nc.vector.memset(sqacc[:], 0.0).then_inc(m_sq, 1)
            step_sizes()
            dve.wait_ge(t_ready, 1)
            link(nc.vector.memset(acc[:], 0.0))
            dve.wait_ge(m_sq, 1)
            dve.wait_ge(parked, 16)
            u = FIRST_UNIT["mamba"]
            group(0, z=u + 4, ahead=u + 6)
            with dve.Fori(0, MG - 2) as i:
                link.enter(i, 4 * 4 + NS + 2 * (NS - 2) + (NS - 4) + 2)
                group(1, i, z=u + 10, out=u + 12, ahead=u + 14)
                link.leave(MG - 2)
            group(MG - 1, z=u + 58, out=u + 60)
            for m in range(KD):
                group_add(MG - 1, None, u + 62, m)
            dve.wait_ge(m_add, 8 * MG)
            dve.wait_ge(m_rt, 1)
            link(nc.vector.reciprocal(rstd[:], rt[:]))
            link(nc.vector.reciprocal(tmp[:, 1, 0:TC], tmp[:, 0, 0:TC]))
            dve.wait_ge(parked, 32)
            dve.wait_ge(ctx_in, 32)
            for m in range(KD):
                link(nc.vector.scalar_tensor_tensor(acc[:, m, 0:T], acc[:, m, 0:T], modv[:, 16 + m, 0:1], rstd[:],
                                                    ALU.mult, ALU.mult))
                nc.vector.tensor_tensor(x[:, m, :], acc[:, m, 0:T], x[:, m, :], ALU.add).then_inc(x_ready, 1)
            for m in range(KD):
                link(nc.vector.scalar_tensor_tensor(acc[:, m, T:TA], acc[:, m, T:TA], modv[:, 16 + m, 1:2], tmp[:, 1, 0:TC],
                                                    ALU.mult, ALU.mult))
                nc.vector.tensor_tensor(side[:, m, :], acc[:, m, T:TA], side[:, m, :], ALU.add).then_inc(ctx_ready, 1)
        if runs("attn_kv"):
            norm("lat1", x, T, lambda k: gmod[:, 8 + k, 0:1], 0, lambda k: modv[:, 24 + k, 0:1], ah, al)
            norm("ctx1", side, TC, lambda k: gmod[:, 8 + k, 1:2], T, lambda k: modv[:, 24 + k, 1:2], ah, al)
            keys_values()
            dve.wait_ge(b_kd, 4)
            for _ in range(2):
                nc.vector.memset(credit[:, 27 + _:28 + _], 0.0).then_inc(a_pv, 1)
            normed_q(0)
            rotated_q(0, 0)
            with dve.Fori(0, 3) as i:
                link.enter(i, 2 * (8 + 3))
                pair(0, 0, i, ahead=True)
                pair(1, 1, i, ahead=True)
                link.leave(3)
            pair(6, 0, ahead=True)
            pair(7, 1)
            out_rest(7)
            u = FIRST_UNIT["attn_out"]
            for m in range(KD):
                dve.wait_ge(unit_done, u + m + 1)
                nc.vector.scalar_tensor_tensor(x[:, m, :], B[2 + m % 2][:], modv[:, 40 + m, 0:1], x[:, m, :],
                                               ALU.mult, ALU.add).then_inc(x_ready, 1)
            norm_in_place("last", "final_norm_w_2")
        if cut is not None:
            nc.vector.memset(credit[:, 31:32], 0.0).then_inc(out_done, 1)


CUT = None


def square_constants():
    i = np.arange(P)
    upto = (i[:, None] <= i[None, :]).astype(np.float32)
    rot = np.zeros((P, P), np.float32)
    for b in range(P):
        half = b // 16 % 2
        if half == 0:
            rot[b + 16, b] = -1.0
        else:
            rot[b - 16, b] = 1.0
    dup = np.zeros((2, P, P), np.float32)
    for r in range(2):
        dup[r, 64 * r + i % 64, i] = 1.0
    return np.stack([np.eye(P, dtype=np.float32), np.ones((P, P), np.float32),
                     (i[:, None] // 64 == i[None, :] // 64).astype(np.float32), upto, upto.T,
                     rot, dup[0], dup[1]], 1)


def distances():
    q, k = np.arange(P)[:, None], np.arange(T)[None, :]
    d = (q + T - P - k).astype(np.float32)
    return np.where(d >= 0, -d, np.float32(MASKED))


def rope():
    t, half = np.arange(T), 32
    inv = (np.float32(10000.0) ** (-np.arange(0, half, 2, dtype=np.float32) / np.float32(half))).astype(np.float32)
    b = np.arange(P) % 64
    place = np.where(b[:, None] // 32 == 0, t[None, :] // 64, t[None, :] % 64).astype(np.float32)
    angle = (place * inv[b % 16][:, None]).astype(np.float32)
    return np.cos(angle).astype(np.float32), np.sin(angle).astype(np.float32)


def columns(a):
    return np.ascontiguousarray(a, np.float32).reshape(-1, P).T


def outputs_first(w, m0, m1):
    k = w.shape[0] // P
    return [w[b * P:(b + 1) * P, m * P:(m + 1) * P] for m in range(m0, m1) for b in range(k)]


def units(blocks):
    return np.ascontiguousarray(np.stack(blocks).reshape(-1, 8, P, P).transpose(0, 2, 1, 3).reshape(-1, P, UNIT))


def weight_stream(I):
    blocks = []
    for i in range(2):
        for h in range(X_HEADS):
            blocks += outputs_first(I["mem_w_kv"][i], h, h + 1) + outputs_first(I["mem_w_kv"][i], 4 + h, 5 + h)

    def ffn(i, j):
        up, down, out, b0 = I["ffn_w_up"][i, j], I["ffn_w_down"][i, j], [], 0
        for w in FF_PARTS:
            for b in range(b0, b0 + w):
                out += outputs_first(up, b, b + 1) + outputs_first(up, D_FF // P + b, D_FF // P + b + 1)
            out += outputs_first(down[b0 * P:(b0 + w) * P], 0, KD)
            b0 += w
        return out

    blocks += ffn(0, 0)
    win, wg = I["pool_w_in"][0], I["pool_w_group"][0]
    for r in range(2):
        blocks += outputs_first(win, 4 * r, 4 * r + 4) + outputs_first(win, 8 + 2 * r, 10 + 2 * r)
        for g in range(2 * r, 2 * r + 2):
            blocks += outputs_first(wg[g], 0, 2)
    blocks += outputs_first(I["pool_w_out"][0][:D], 0, 8) + outputs_first(I["pool_w_out"][0][D:], 0, 8)
    blocks += ffn(0, 1) + ffn(1, 0)
    win, wout = I["diff_w_in"][0], I["diff_w_out"][0]

    def head(h):
        return sum((outputs_first(win, 8 * r + h, 8 * r + h + 1) for r in range(3)), [])

    def head_out(h):
        return outputs_first(wout[h * P:(h + 1) * P], 0, 8)
    blocks += head(0) + head(1)
    for h in range(1, 7):
        blocks += head(h + 1) + head_out(h - 1)
    blocks += head_out(6) + head_out(7) + outputs_first(win, 24, 28)
    blocks += outputs_first(wout[D:], 0, 8)
    blocks += ffn(1, 1)
    win, wout = I["m_in_w_2"][0], I["m_out_w_2"][0]

    def z(g):
        return outputs_first(win, 2 * g, 2 * g + 2)

    def xbc(g):
        return sum((outputs_first(win, m, m + 1) for m in (16 + 2 * g, 17 + 2 * g, 32 + g, 40 + g)), [])

    def group_out(g):
        return outputs_first(wout[2 * P * g:2 * P * (g + 1)], 0, 8)
    blocks += xbc(0) + z(0) + xbc(1)
    for g in range(1, MG - 1):
        blocks += z(g) + group_out(g - 1) + xbc(g + 1)
    blocks += z(MG - 1) + group_out(MG - 2) + group_out(MG - 1)
    win = I["a_in_w_2"][0]
    blocks += outputs_first(win, 8, 12)
    for p in range(A_HEADS // 2):
        blocks += outputs_first(win, p, p + 1) + outputs_first(win, 12 + p, 13 + p)
    blocks += outputs_first(I["a_out_w_2"][0], 0, 8)
    return blocks


def kernel(**inputs):
    import concourse.bacc as _bacc
    from concourse.bass_utils import run_bass_kernel_spmd as _run

    I = {k: np.asarray(v) for k, v in inputs.items()}
    f32 = np.float32
    parts = {
        "norm_g": columns(I["norm_g"]), "final_norm_g": columns(I["final_norm_g"]),
        "mem_norm_g": columns(I["mem_norm_g"]), "pool_scale": columns(I["pool_scale"]),
        "diff_norm_g": columns(I["diff_norm_g"]), "norm_w_2": columns(I["norm_w_2"]),
        "final_norm_w_2": columns(I["final_norm_w_2"]), "mod_b_2": columns(I["mod_b_2"]),
        "conv_w": columns(I["m_conv_w_2"]), "conv_b": columns(I["m_conv_b_2"]), "m_norm_w": columns(I["m_norm_w_2"]),
        "a_q_norm": columns(np.tile(I["a_q_norm_2"][0], 2)), "a_k_norm": columns(np.tile(I["a_k_norm_2"][0], 2)),
        "c": np.stack([columns(I["c_2"]), columns(I["c_ctx_2"])], 2).reshape(P, 16),
        "dt_bias": np.tile(I["m_dt_bias_2"].reshape(1, 64), (P, 1)),
        "a_log": np.tile(I["m_a_log_2"].reshape(1, 64), (P, 1)),
        "m_d": np.tile(I["m_d_2"].reshape(1, 32), (P, 1)),
        "diff_lambda": np.tile(I["diff_lambda"].reshape(1, 256), (P, 1)),
        "slopes": np.tile(np.array([2.0 ** (-8.0 * (h + 1) / DIFF_HEADS) for h in range(DIFF_HEADS)], f32), (P, 1)),
        "pool_rcount": np.tile(np.concatenate([1.0 / np.minimum(np.arange(1, 17), w) for w in POOL_WINDOWS])
                               .astype(f32), (P, 1)),
    }
    arrays = {
        "xT": np.ascontiguousarray(I["x"][0].T.reshape(KD, P, T).transpose(1, 0, 2)),
        "memT": np.ascontiguousarray(I["mem"][0].T.reshape(KD, P, TC).transpose(1, 0, 2)),
        "cols": np.ascontiguousarray(np.concatenate([parts[n] for n, _ in COLUMNS], 1)),
        "ctxT": np.ascontiguousarray(I["ctx_2"][0].T.reshape(KD, P, TC).transpose(1, 0, 2)),
        "wdt": np.ascontiguousarray(I["m_in_w_2"][0][:, 6144:].reshape(KD, P, 64).transpose(1, 0, 2)),
        "dist": distances(),
        "cos": rope()[0],
        "sin": rope()[1],
        "squares": np.ascontiguousarray(square_constants()),
        "stream": units(weight_stream(I)),
        "mod": units(outputs_first(I["mod_w_2"][0], 0, 24) + outputs_first(I["mod_w_2"][1], 0, 24)),
    }
    nc = _bacc.Bacc("TRN2", target_bir_lowering=False, num_devices=1)
    A = {k: nc.dram_tensor(k + "_dram", v.shape, FP32, kind="ExternalInput").ap() for k, v in arrays.items()}
    A["out"] = nc.dram_tensor("out_dram", (P, KD, T), FP32, kind="ExternalOutput").ap()
    A["park"] = nc.dram_tensor("park_dram", (P, KD, T), FP32, kind="Internal").ap()
    program(nc, A, CUT)
    r = _run(nc, [{k + "_dram": v for k, v in arrays.items()}], core_ids=[0])
    out = np.asarray(r.results[0]["out_dram"])
    return np.ascontiguousarray(out.transpose(2, 1, 0).reshape(1, T, D))
```

```python
import math
import numpy as np
import concourse.bass as bass
from concourse import mybir
from contextlib import ExitStack

FP32 = mybir.dt.float32
F32R = mybir.dt.float32r
ALU = mybir.AluOpType
ACT = mybir.ActivationFunctionType
AX = mybir.AxisListType

P = 128
D = 1024
KD = D // P
T = 512
TC = 256
TA = T + TC
NB = T // P
D_FF = 2816
FF_PARTS = (8, 8, 6)
UNIT = 8 * P
RAW = 2
RING = 4
X_HEADS = 4
POOL_WINDOWS = (2, 4, 8, 16)
PAD = 16
DIFF_HEADS = 8
DIFF_SCALE = 64 ** -0.5
LAM_INIT = 0.8 - 0.6 * math.exp(-0.3)
MG = 8
HPG = 4
NCH = TA // P
A_HEADS = 16
A_KV = 4
A_SCALE = 64 ** -0.5
MASKED = -1e30

FF_UNITS = 2 * sum(FF_PARTS) + sum(FF_PARTS)
STAGE_UNITS = [
    ("memkv", 16), ("ffn0", FF_UNITS), ("pool", 14), ("pool_out", 12), ("ffn1", FF_UNITS),
    ("ffn2", FF_UNITS), ("diff", 36), ("diff_out", 4), ("ffn3", FF_UNITS), ("mamba", 64),
    ("attn_kv", 6), ("attn_qg", 14), ("attn_out", 8),
]
FIRST_UNIT = {}
UNITS = 0
for _name, _n in STAGE_UNITS:
    FIRST_UNIT[_name] = UNITS
    UNITS += _n

COLUMNS = [
    ("norm_g", 48), ("final_norm_g", 8), ("mem_norm_g", 8), ("pool_scale", 8), ("diff_norm_g", 1),
    ("norm_w_2", 16), ("final_norm_w_2", 8), ("mod_b_2", 48), ("conv_w", 5 * 32), ("conv_b", 32),
    ("m_norm_w", 16), ("a_q_norm", 1), ("a_k_norm", 1), ("c", 16), ("dt_bias", 64), ("a_log", 64),
    ("m_d", 32), ("diff_lambda", 256), ("slopes", 8), ("pool_rcount", 64),
]
COL = {}
NCOL = 0
for _name, _n in COLUMNS:
    COL[_name] = NCOL
    NCOL += _n

SQUARES = ["ident", "ones", "ones64", "upto", "from", "rot", "dup0", "dup1"]


class Link:

    def __init__(self, eng, sem):
        self.eng, self.sem, self.n, self.i, self.per = eng, sem, 0, None, 0

    def __call__(self, ins):
        self.until(self.mark(ins))

    def mark(self, ins):
        ins.then_inc(self.sem, 1)
        self.n += 1
        return self.n

    def until(self, n):
        self.eng.wait_ge(self.sem, n if self.i is None else self.i * self.per + n)

    def enter(self, i, per):
        self.i, self.per, self.first = i, per, self.n

    def leave(self, times):
        assert self.n - self.first == self.per, (self.n - self.first, self.per)
        self.i, self.n = None, self.first + self.per * times


def at(base, i=None, per=0):
    return base if i is None else i * per + base


def program(nc, A):
    with ExitStack() as ctx:
        build(nc, A, ctx)


def build(nc, A, ctx):
    def sb(name, shape, dt=FP32, scope=ctx):
        return scope.enter_context(nc.sbuf_tensor(name, shape, dt))

    def sem(name):
        return ctx.enter_context(nc.semaphore(name))

    x = sb("x", [P, KD, T])
    side = sb("side", [P, KD, TC])
    raw = sb("raw", [P, RAW, UNIT])
    wh = sb("wh", [P, RING, UNIT], F32R)
    wl = sb("wl", [P, RING, UNIT], F32R)
    cols = sb("cols", [P, NCOL])
    sq8 = sb("sq8", [P, len(SQUARES), P])
    SQ = {n: sq8[:, k, :] for k, n in enumerate(SQUARES)}
    ident, ones = SQ["ident"], SQ["ones"]
    eps6 = sb("eps6", [P, 1])
    eps5 = sb("eps5", [P, 1])
    credit = sb("credit", [P, 32])
    modv = sb("modv", [P, 48, 2])
    gmod = sb("gmod", [P, 16, 2])
    sqr = sb("sqr", [P, 2, T])
    rt = sb("rt", [P, T])
    rstd = sb("rstd", [P, T])
    tmp = sb("tmp", [P, 2, T])

    def scope():
        return ExitStack()

    with scope() as first:
        hh = sb("hh", [P, KD, T], F32R, first)
        hl = sb("hl", [P, KD, T], F32R, first)
        fh = sb("fh", [P, KD, T], F32R, first)
        fl = sb("fl", [P, KD, T], F32R, first)
        dist = sb("dist", [P, T], scope=first)
        csil = sb("csil", [P, KD, 2], scope=first)
        modw = sb("modw", [P, 2, UNIT], scope=first)
        mk = sb("mk", [P, 2 * X_HEADS, TC], scope=first)
        mv = sb("mv", [P, 2 * X_HEADS, 2, P], scope=first)
        with scope() as s:
            dq = sb("dq", [P, 2, T], scope=s)
            dk = sb("dk", [P, 2, T], scope=s)
            dv = sb("dv", [P, 2, T], scope=s)
            dvt = sb("dvt", [P, NB, P], scope=s)
            de = sb("de", [P, 2, 2, T], scope=s)
            dw = sb("dw", [P, T], scope=s)
            dT = sb("dT", [P, NB, T], scope=s)
            dnm = sb("dnm", [P, 2, 2], scope=s)
            drs = sb("drs", [P, 2, 2], scope=s)
            drr = sb("drr", [P, 2, 2], scope=s)
            drl = sb("drl", [P, 1], scope=s)
            lamt = sb("lamt", [P, 2, 64], scope=s)
            lams = sb("lams", [P, 2], scope=s)
            lame = sb("lame", [P, 2], scope=s)
            lam = sb("lam", [P, 1], scope=s)
            dgain = sb("dgain", [P, 1], scope=s)
        xoh = sb("xoh", [P, X_HEADS, T], F32R, first)
        xol = sb("xol", [P, X_HEADS, T], F32R, first)
        qx = sb("qx", [P, X_HEADS, T], scope=first)
        with scope() as s:
            ubuf = sb("ubuf", [P, 2, PAD + T], scope=s)
            sg = ubuf[:, :, 0:T]
            modp = sb("modp", [P, 2, 2, P], scope=s)
        vt = modw[:, :, 0:TC]
        modflat = modw[:].rearrange("p s n -> p (s n)")
        pa, pb_ = (modflat[:, n * (PAD + T):(n + 1) * (PAD + T)] for n in range(2))
        with scope() as s:
            vcur = sb("vcur", [P, 2, 2, P], scope=s)
            pexp = sb("pexp", [P, 2, TC], scope=s)
            pT = sb("pT", [P, 2, 2, P], scope=s)
            nm = sb("nm", [P, 8], scope=s)
            rs = sb("rs", [P, 8], scope=s)
            rr = sb("rr", [P, 8], scope=s)

    qcur = sqr

    with scope() as s:
        mh = sb("mh", [P, KD, TA], F32R, s)
        ml = sb("ml", [P, KD, TA], F32R, s)
        acc = sb("acc", [P, KD, TA], scope=s)
        zs = sb("zs", [P, 2, TA], scope=s)
        xs = sb("xs", [P, 2, TA], scope=s)
        cvin = sb("cvin", [P, 4, TA + 6], scope=s)
        Bm = sb("Bm", [P, TA], scope=s)
        Cm = sb("Cm", [P, TA], scope=s)
        da = sb("da", [P, 2, NCH, MG * HPG], scope=s)
        sqacc = sb("sqacc", [P, TA], scope=s)
        yt = sb("yt", [P, HPG, 64], scope=s)
        state = sb("state", [P, 2, HPG, 64], scope=s)
        xe = sb("xe", [P, 2, HPG, 64], scope=s)
        yh = sb("yh", [P, 2, TA], F32R, s)
        yl = sb("yl", [P, 2, TA], F32R, s)
        dag = sb("dag", [P, 2, NCH, HPG], scope=s)
    sideflat = side[:].rearrange("p k t -> p (k t)")
    dt, la, ela, tend, cdec = (sideflat[:, n * NCH * 64:(n + 1) * NCH * 64].rearrange("p (d c h) -> p d c h", d=2, c=NCH)
                               for n in range(5))
    wdt = acc[:, 0, 0:KD * 64].rearrange("p (k h) -> p k h", k=KD)
    aexp = acc[:, 1, 0:64]
    wdth, wdtl = (b[:, 0, 0:KD * 64].rearrange("p (k h) -> p k h", k=KD) for b in (yh, yl))
    dtT = acc[0:64, 4, :]
    xflat = x[:].rearrange("p k t -> p (k t)")
    xtok = xflat[:, 0:NCH * 256].rearrange("p (c r e) -> p c r e", c=NCH, r=HPG)
    ytok = xflat[:, NCH * 256:NCH * 512].rearrange("p (c r e) -> p c r e", c=NCH, r=HPG)
    btok = xflat[:, NCH * 512:NCH * 640].rearrange("p (c n) -> p c n", c=NCH)
    xdt = xs[:].rearrange("p a t -> p (a t)").rearrange("p (c r e) -> p c r e", c=NCH, r=HPG)
    cbm = xflat[:, NCH * 640:NCH * 640 + P]
    decay = [tmp[:, 0, :], tmp[:, 1, :], sqr[:, 0, :], sqr[:, 1, :]]
    conv = [b[:].rearrange("p a t -> p (a t)")[:, 0:TA + 2] for b in (sqr, tmp)]
    one = sq8[:, 1, 0:1]

    with scope() as s:
        ah = sb("ah", [P, KD, TA], F32R, s)
        al = sb("al", [P, KD, TA], F32R, s)
        kd = sb("kd", [P, A_KV, TA], scope=s)
        vtok = sb("vtok", [P, NCH, A_KV * 64], scope=s)
        og = sb("og", [P, KD, T], scope=s)
        qr = sb("qr", [P, 2, T], scope=s)
        gs = sb("gs", [P, 2, T], scope=s)
        pe2 = sb("pe2", [P, 2, TA], scope=s)
        pT2 = sb("pT2", [P, 2, NCH, P], scope=s)
        krn = sb("krn", [P, 2, TA], scope=s)
        kcur = sb("kcur", [P, 2, TA], scope=s)
        vcur2 = sb("vcur2", [P, NCH, 64], scope=s)
        cos, sin = sb("cos", [P, T], scope=s), sb("sin", [P, T], scope=s)
        nm2, rs2, rr2 = (sb(n, [P, 8], scope=s) for n in ("nm2", "rs2", "rr2"))
        aqg = sb("aqg", [P, 1], scope=s)
    ogflat = og[:].rearrange("p k t -> p (k t)")
    kraw, vraw = (ogflat[:, 2 * n * TA:2 * (n + 1) * TA].rearrange("p (j t) -> p j t", j=2) for n in range(2))
    pT2flat = pT2[:].rearrange("p s k t -> p (s k t)")
    kn, ksq = (pT2flat[:, n * TA:(n + 1) * TA] for n in range(2))
    krt, krs = krn[:, 0], krn[:, 1]

    ps = ctx.enter_context(nc.psum_tensor("ps", [P, 8 * T], FP32))
    B = [ps[:, k * T:(k + 1) * T] for k in range(8)]

    loaded = [sem(f"raw_loaded{s}") for s in range(RAW)]
    s_hi = sem("weights_hi")
    s_lo = sem("weights_lo")
    unit_done = sem("unit_done")
    consts_in, dist_in = sem("consts_in"), sem("dist_in")
    x_in = sem("x_in")
    side_in = sem("side_in")
    s_chain = sem("dve_chain")
    s_init = sem("init")
    c_silu = sem("c_silu")
    mod_loaded = [sem(f"mod_loaded{s}") for s in range(2)]
    mod_part = sem("mod_part")
    mod_used, mod_read, gmod_ready = sem("mod_used"), sem("mod_read"), sem("gmod_ready")
    sq_ready, sq_used, rt_ready = sem("sq_ready"), sem("sq_used"), sem("rt_ready")
    ss_ready, rs_ready, rb_ready = sem("ss_ready"), sem("rs_ready"), sem("rb_ready")
    tmp_ready, h_hi, h_ready = sem("tmp_ready"), sem("h_hi"), sem("h_ready")
    kv_copied, kv_t, kv_ready = sem("kv_copied"), sem("kv_t"), sem("kv_ready")
    silu_ready, gated, hid_hi, hid_lo = sem("silu_ready"), sem("gated"), sem("hid_hi"), sem("hid_lo")
    x_ready = sem("x_ready")
    pool_copied, pooled, pooled_hi, pooled_lo = sem("pool_copied"), sem("pooled"), sem("pooled_hi"), sem("pooled_lo")
    mix_hi, mix_lo = sem("mix_hi"), sem("mix_lo")
    att_q, att_v, att_s, att_max = sem("att_q"), sem("att_v"), sem("att_s"), sem("att_max")
    att_exp, att_p, att_t, att_pt, att_o = sem("att_exp"), sem("att_p"), sem("att_t"), sem("att_pt"), sem("att_o")
    xo_hi, xo_lo = sem("xo_hi"), sem("xo_lo")
    d_copied, d_vt, d_vtok, d_s, d_biased = sem("d_copied"), sem("d_vt"), sem("d_vtok"), sem("d_s"), sem("d_biased")
    d_max, d_exp, d_w, d_t, d_pt, d_o = sem("d_max"), sem("d_exp"), sem("d_w"), sem("d_t"), sem("d_pt"), sem("d_o")
    d_sq, d_ss, d_rt, d_ot, d_ohi, d_olo, d_m = (sem("d_sq"), sem("d_ss"), sem("d_rt"), sem("d_ot"), sem("d_ohi"),
                                                sem("d_olo"), sem("d_m"))
    lam_sums, lam_exp = sem("lam_sums"), sem("lam_exp")
    parked, ctx_in, wdt_in = sem("parked"), sem("ctx_in"), sem("wdt_in")
    cv_zero, m_zero = sem("cv_zero"), sem("m_zero")
    t_dt, t_x, t_abs, t_exp, t_ln, t_a = sem("t_dt"), sem("t_x"), sem("t_abs"), sem("t_exp"), sem("t_ln"), sem("t_a")
    t_wh, t_wl, t_raw, t_copied = sem("t_wh"), sem("t_wl"), sem("t_raw"), sem("t_copied")
    t_da, t_cum, t_diff, t_dec, t_ready = sem("t_da"), sem("t_cum"), sem("t_diff"), sem("t_dec"), sem("t_ready")
    m_cv, m_z, m_acc, m_xbc, m_tr, m_tok = (sem("m_cv"), sem("m_z"), sem("m_acc"), sem("m_xbc"), sem("m_tr"), sem("m_tok"))
    m_cb, m_t, m_e, m_w, m_yp = sem("m_cb"), sem("m_t"), sem("m_e"), sem("m_w"), sem("m_yp")
    m_y, m_st, m_dag, m_x = sem("m_y"), sem("m_st"), sem("m_dag"), sem("m_x")
    m_yt, m_yg, m_sq, m_yh, m_yl, m_om, m_add = (sem("m_yt"), sem("m_yg"), sem("m_sq"), sem("m_yh"), sem("m_yl"),
                                                sem("m_om"), sem("m_add"))
    m_rs, m_rb = sem("m_rs"), sem("m_rb")
    m_ss, m_rt, m_px, m_py = sem("m_ss"), sem("m_rt"), sem("m_px"), sem("m_py")
    ctx_ready, cs_in = sem("ctx_ready"), sem("cs_in")
    b_copied, b_sq, b_ss, b_rt, b_kn = sem("b_copied"), sem("b_sq"), sem("b_ss"), sem("b_rt"), sem("b_kn")
    b_rot, b_kr, b_dup, b_kd, b_vt, b_v = sem("b_rot"), sem("b_kr"), sem("b_dup"), sem("b_kd"), sem("b_vt"), sem("b_v")
    a_qc, a_sq, a_ss, a_rt, a_qn, a_rot, a_qr = (sem("a_qc"), sem("a_sq"), sem("a_ss"), sem("a_rt"), sem("a_qn"),
                                                 sem("a_rot"), sem("a_qr"))
    a_kc = sem("a_kc")
    a_g, a_kv, a_s, a_max, a_exp = sem("a_g"), sem("a_kv"), sem("a_s"), sem("a_max"), sem("a_exp")
    a_p, a_t, a_pt, a_pv, a_o, a_oh, a_ol = (sem("a_p"), sem("a_t"), sem("a_pt"), sem("a_pv"), sem("a_o"), sem("a_oh"),
                                             sem("a_ol"))

    STEPS = [(0, c) for c in (4, 5, 0, 1, 2, 3)] + [(1, c) for c in (5, 4, 3, 2, 1, 0)]
    NS = len(STEPS)
    Q_AT, SS_AT, ROT_AT, G_AT = 0, 2, 4, 5
    UNDER = ((0, 3), (3, 6), (6, 8))

    def updates(t):
        return sum(1 for k in range(t + 1) if k % NCH != NCH - 1)

    def chunk(c):
        return slice(c * P, (c + 1) * P)

    X0 = 2

    def xr(ffns, mixers):
        return X0 + 24 * ffns + (0, 16, 16 + 8 * DIFF_HEADS + 8)[mixers]

    X_ATTN = xr(4, 2) + 16
    MIXERS_BEFORE = {"ffn0": 0, "ffn1": 1, "ffn2": 1, "ffn3": 2}

    w = FF_PARTS[-1]
    FF_TAIL = [[m for m in range(KD) if (w * m + w - 1) // 8 == v - 1] for v in range(w + 1)]
    MIX_TAIL = [[], [0, 1], [2, 3], [4, 5], [6, 7]]

    block = ctx.enter_context(nc.Block())

    def col(name, k=0, n=1):
        return cols[:, COL[name] + k:COL[name] + k + n]

    NORM = {n: k for k, n in enumerate(["mem", "ffn0", "pool", "ffn1", "ffn2", "diff", "ffn3", "final",
                                        "lat0", "ctx0", "lat1", "ctx1", "last"])}

    @block.sync
    def _(sp):
        sp.dma_start(side[:], A["memT"]).then_inc(side_in, 16)
        sp.dma_start(sq8[:], A["squares"]).then_inc(consts_in, 16)
        sp.dma_start(cols[:], A["cols"]).then_inc(consts_in, 16)

        def load(u, i=None, per=0):
            sp.dma_start(raw[:, u % RAW, :], A["stream"][at(u, i, per)]).then_inc(loaded[u % RAW], 16)

        for u in range(RING):
            if u >= RAW:
                sp.wait_ge(s_lo, u - RAW + 1)
            load(u)
        sp.dma_start(x[:], A["xT"]).then_inc(x_in, 16)
        sp.dma_start(dist[:], A["dist"]).then_inc(dist_in, 16)
        passes = (UNITS - RING) // RING
        with sp.Fori(0, passes) as i:
            for j in range(RING):
                u = RING + j
                sp.wait_ge(s_lo, at(u - RAW + 1, i, RING))
                load(u, i, RING)
        for u in range(RING * (passes + 1), UNITS):
            sp.wait_ge(s_lo, u - RAW + 1)
            load(u)
        for k in range(KD):
            sp.wait_ge(x_ready, X_ATTN + 8 + k + 1)
            sp.dma_start(A["out"][:, k, :], x[:, k, :]).then_inc(x_in, 16)
        sp.wait_ge(x_in, 16 + 16 * KD)
        sp.wait_ge(parked, 32)

    @block.gpsimd
    def _(pool):
        def rest(u, i=None, per=0):
            pool.wait_ge(s_hi, at(u + 1, i, per))
            nc.gpsimd.tensor_tensor(wl[:, u % RING, :], raw[:, u % RAW, :], wh[:, u % RING, :].bitcast(FP32),
                                    ALU.subtract).then_inc(s_lo, 1)

        def rests(u, end):
            passes = (end - u) // RING
            with pool.Fori(0, passes) as i:
                for j in range(RING):
                    rest(u + j, i, RING)
            for v in range(u + RING * passes, end):
                rest(v)

        def group(g, i=None, out=None, z=None, ahead=None):
            def c(per, n):
                return at(per * g + n, i, per)
            gg = g if i is None else i + g

            def per_head(a, d, k):
                return a[:, d, k, bass.ds(gg * HPG, HPG)].unsqueeze(2).to_broadcast([P, HPG, 64])

            def step(t):
                d, k = STEPS[t]
                if d:
                    pool.wait_ge(m_yp, c(NS, STEPS.index((0, k)) + 1))
                last = nc.gpsimd.tensor_tensor(xdt[:, k], xtok[:, k], per_head(dt, d, k), ALU.mult)
                if t % NCH != NCH - 1:
                    before = [v for v in range(t) if v % NCH != NCH - 1]
                    if len(before) >= 2:
                        pool.wait_ge(m_cb, c(NS, before[-2] + 1))
                    last = nc.gpsimd.tensor_tensor(xe[:, updates(t) % 2], xtok[:, k], per_head(tend, d, k), ALU.mult)
                last.then_inc(m_px, 1)

            for u in (z, z + 1) + ((out, out + 1) if out is not None else ()):
                rest(u + RING, i, 8)
            pool.wait_ge(m_tok, c(5, 5))
            step(0)
            step(1)
            for k in range(NCH):
                last = nc.gpsimd.tensor_tensor(ytok[:, k], xtok[:, k],
                                               cols[:, bass.ds(COL["m_d"] + gg * HPG, HPG)].unsqueeze(2)
                                               .to_broadcast([P, HPG, 64]), ALU.mult)
            last.then_inc(m_py, 1)
            for t in range(2, NS):
                step(t)
                if ahead is not None and t % 3 == 1 and t > 1:
                    rest(ahead + t // 3 - 1 + RING, i, 8)
            if ahead is not None:
                rest(ahead + 3 + RING, i, 8)
            for j in range(2):
                pool.wait_ge(m_x, c(2, j + 1))
                pool.wait_ge(m_sq, c(2, j + 1))
                nc.gpsimd.tensor_tensor(sqacc[:], sqacc[:], xs[:, j, :], ALU.add).then_inc(m_sq, 1)

        u = FIRST_UNIT["mamba"]
        rests(0, u + 8)
        pool.wait_ge(t_ready, 1)
        nc.gpsimd.memset(acc[:], 0.0).then_inc(m_zero, 1)
        group(0, z=u + 4, ahead=u + 6)
        with pool.Fori(0, MG - 2) as i:
            group(1, i, z=u + 10, out=u + 12, ahead=u + 14)
        group(MG - 1, z=u + 58, out=u + 60)
        rests(u + 66, UNITS)

    @block.tensor
    def _(pe):
        def project(u, hi, lo, outs, i=None, per=0, arrive=None, part=(0, KD)):
            if part[0] == 0:
                pe.wait_ge(s_lo, at(u + 1, i, per))
            s = u % RING
            for k in range(*part):
                if arrive is not None:
                    arrive(k)
                w = slice(k * P, (k + 1) * P)
                for a, b in ((wh, hi), (wh, lo), (wl, hi)):
                    for bank, c0, c1 in outs:
                        last = nc.tensor.matmul(bank, a[:, s, w], b[:, k, c0:c1],
                                                start=(k == 0 and a is wh and b is hi),
                                                stop=(k == KD - 1 and a is wl))
            if part[1] == KD:
                last.then_inc(unit_done, 1)

        def blocks(u, plan, i=None, per=0):
            pe.wait_ge(s_lo, at(u + 1, i, per))
            s = u % RING
            for k, (before, hi, lo, bank, start, stop) in enumerate(plan):
                before()
                w = slice(k * P, (k + 1) * P)
                nc.tensor.matmul(bank, wh[:, s, w], hi, start=start, stop=False)
                nc.tensor.matmul(bank, wh[:, s, w], lo, start=False, stop=False)
                last = nc.tensor.matmul(bank, wl[:, s, w], hi, start=False, stop=stop)
            last.then_inc(unit_done, 1)

        def norm_sum(name, k, width=T):
            n = NORM[name]
            if n and k == 0:
                pe.wait_ge(rt_ready, n)
            pe.wait_ge(sq_ready, 8 * n + k + 1)
            for c in range(width // P):
                last = nc.tensor.matmul(B[7][:, KD * c + k:KD * c + k + 1], sqr[:, k % 2, chunk(c)], ones[:, 0:1],
                                        start=True, stop=True)
            last.then_inc(sq_used, 1)

        def norm_sums(name, width):
            for k in range(KD):
                norm_sum(name, k, width)

        def norm_spread(name, width):
            pe.wait_ge(rs_ready, NORM[name] + 1)
            for c in range(width // P):
                last = nc.tensor.matmul(B[6][:, chunk(c)], rstd[:, c:c + 1].to_broadcast([P, P]), ident, start=True, stop=True)
            last.then_inc(rb_ready, 1)

        def modulation(v, i):
            pe.wait_ge(mod_part, at(2 * v + 2, i, 4))
            for r in range(2):
                last = nc.tensor.matmul(B[6][:, bass.ds(i * 4 + (2 * v + r), 1)], modp[:, v % 2, r, :], ones[:, 0:1],
                                        start=True, stop=True)
            last.then_inc(mod_used, 1)

        def ffn(f, name, norm, following):
            n = NORM[norm]
            norm_spread(norm, T)
            u = FIRST_UNIT[name]
            pairs = f * sum(FF_PARTS)
            for p, w in enumerate(FF_PARTS):
                def arrive(k):
                    pe.wait_ge(h_ready, 8 * n + k + 1)
                with pe.Fori(0, w // 2) as i:
                    for jj in range(2):
                        pe.wait_ge(gated, at(pairs + jj + 1, i, 2))
                        g = u + 2 * jj
                        project(g, hh, hl, [(B[2 * jj][:], 0, T)], i, 4, arrive=arrive if p == 0 and jj == 0 else None)
                        project(g + 1, hh, hl, [(B[2 * jj + 1][:], 0, T)], i, 4)
                        if w == KD and f < 3 and jj == 1:
                            modulation(16 * f + 8 * p, i)
                            modulation(16 * f + 8 * p + 1, i)
                u += 2 * w
                done = xr(f, MIXERS_BEFORE[name]) + 8 * p
                hidden = pairs + w

                def before(m, k, i=None, per=0):
                    def wait():
                        if k == 0:
                            pe.wait_ge(x_ready, at(done + m - 1, i, per))
                            pe.wait_ge(hid_lo, hidden - 2)
                        if k >= w - 2:
                            pe.wait_ge(hid_lo, hidden - w + k + 1)
                    return wait
                if w == KD:
                    with pe.Fori(0, 2) as i:
                        for m in range(4):
                            blocks(u + m, [(before(m, k, i, 4), fh[:, k, :], fl[:, k, :], B[4 + m % 2][:], k == 0,
                                            k == w - 1) for k in range(w)], i, 4)
                else:
                    for v in range(w):
                        plan = []
                        for b in range(8 * v, 8 * v + 8):
                            m, k = b // w, b % w
                            plan.append((before(m, k), fh[:, k, :], fl[:, k, :], B[4 + m % 2][:], k == 0, k == w - 1))
                        blocks(u + v, plan)
                        for m in FF_TAIL[v]:
                            norm_sum(following, m)
                u += w
                pairs += w
            for m in FF_TAIL[-1]:
                norm_sum(following, m)

        def memory_attention(layer, u=None, done=0):
            with pe.Fori(0, X_HEADS // 2) as i:
                def c(n):
                    return at(16 * layer + n, i, 8)

                def scores(s):
                    r, b = divmod(s, NB)
                    if s >= 2:
                        pe.wait_ge(att_exp, c(s - 1))
                    nc.tensor.matmul(B[4 + s % 2][:, 0:TC], qcur[:, r, b * P:(b + 1) * P],
                                     mk[:, i * 2 + (r + X_HEADS * layer), :], start=True, stop=True).then_inc(att_s, 1)

                def weighted(s):
                    r, b = divmod(s, NB)
                    pe.wait_ge(att_pt, c(s + 1))
                    if s == 0:
                        pe.wait_ge(att_v, at(2 * layer + 1, i, 1))
                    for kb in range(2):
                        last = nc.tensor.matmul(B[2 + r][:, chunk(b)], vcur[:, r, kb, :], pT[:, s % 2, kb, :],
                                                start=(kb == 0), stop=(kb == 1))
                    last.then_inc(att_o, 1)

                pe.wait_ge(att_q, at(2 * layer + 1, i, 1))
                scores(0)
                scores(1)
                for s in range(8):
                    pe.wait_ge(att_p, c(s + 1))
                    if s >= 2:
                        pe.wait_ge(att_pt, c(s - 1))
                    for kb in range(2):
                        last = nc.tensor.transpose(B[6 + s % 2][:, chunk(kb)], pexp[:, s % 2, chunk(kb)], ident)
                    last.then_inc(att_t, 1)
                    if s:
                        weighted(s - 1)
                    if s + 2 < 8:
                        scores(s + 2)
                    if u is not None and s % 2:
                        m = s // 2

                        def before(m=m):
                            pe.wait_ge(x_ready, at(done + m - 1, i, 4))
                        blocks(u + m, [(before if k == 0 else (lambda: None), fh[:, k, :], fl[:, k, :], B[m % 2][:],
                                        k == 0, k == KD - 1) for k in range(KD)], i, 4)
                weighted(7)

        def out_memory(u, done, mixers, following):
            for v in range(4):
                plan = []
                for b in range(8):
                    m, k = 2 * v + b // 4, b % 4

                    def before(m=m, k=k):
                        if k == 0:
                            pe.wait_ge(x_ready, done + m - 1)
                            pe.wait_ge(xo_lo, X_HEADS * mixers)
                    plan.append((before, xoh[:, k, :], xol[:, k, :], B[m % 2][:], k == 0, k == 3))
                blocks(u + v, plan)
                for m in MIX_TAIL[v]:
                    norm_sum(following, m)
            for m in MIX_TAIL[-1]:
                norm_sum(following, m)

        def diff_head(h, par, i=None, ahead=None, out=None):
            def c(n, per):
                return at(n, i, 2 * per)

            def scores(b):
                for r in range(2):
                    if b:
                        pe.wait_ge(d_biased, c(8 * h + 2 * (b - 1) + r + 1, 8))
                    nc.tensor.matmul(B[2 + r][:, 0:(b + 1) * P], dq[64 * r:64 * r + 64, par, b * P:(b + 1) * P],
                                     dk[64 * r:64 * r + 64, par, 0:(b + 1) * P], start=True, stop=True).then_inc(d_s, 1)

            def turn(b):
                pe.wait_ge(d_w, c(4 * h + b + 1, 4))
                if b:
                    pe.wait_ge(d_pt, c(4 * h + b, 4))
                else:
                    pe.wait_ge(d_vtok, c(h + 1, 1))
                for kb in range(b + 1):
                    last = nc.tensor.transpose(B[4][:, kb * P:(kb + 1) * P], dw[:, kb * P:(kb + 1) * P], ident)
                last.then_inc(d_t, 1)

            pe.wait_ge(d_copied, c(3 * h + 3, 3))
            scores(0)
            scores(1)
            if h or i is not None:
                pe.wait_ge(d_pt, c(4 * h, 4))
            for kb in range(NB):
                last = nc.tensor.transpose(B[4][:, kb * P:(kb + 1) * P], dv[:, par, kb * P:(kb + 1) * P], ident)
            last.then_inc(d_vt, 1)
            if h or i is not None:
                mean_square(h - 1, i)
            for b in range(NB):
                if b < 3 and ahead is not None:
                    if b == 1 and (h or i is not None):
                        pe.wait_ge(d_rt, c(h, 1))
                    if b == 2:
                        pe.wait_ge(d_copied, c(3 * h + 4, 3))
                    project(ahead + b, hh, hl, [(B[b % 2][:], 0, T)], i, 8)
                if b == 3 and out is not None:
                    out_head(h - 1, 1 - par, out, i)
                turn(b)
                if b < 2:
                    scores(b + 2)
            pe.wait_ge(d_pt, c(4 * h + 4, 4))
            if h or i is not None:
                pe.wait_ge(d_olo, c(h, 1))
            for kb in range(NB):
                last = nc.tensor.matmul(B[5][:, kb * P:T], dvt[:, kb, :], dT[:, kb, kb * P:T], start=(kb == 0),
                                        stop=(kb == NB - 1))
            last.then_inc(d_o, 1)

        def mean_square(h, i=None):
            pe.wait_ge(d_sq, at(h + 1, i, 2))
            pe.wait_ge(d_copied, at(3 * h + 6, i, 6))
            nc.tensor.matmul(B[1][:], ones, sqr[:, 0, :], start=True, stop=True).then_inc(d_ss, 1)

        def out_head(h, par, u, i=None):
            pe.wait_ge(s_lo, at(u + 1, i, 8))
            pe.wait_ge(d_olo, at(h + 1, i, 2))
            for m in range(KD):
                pe.wait_ge(x_ready, at(xr(3, 1) + 8 * h + m - 1, i, 16))
                w = slice(m * P, (m + 1) * P)
                nc.tensor.matmul(B[6 + m % 2][:], wh[:, u % RING, w], fh[:, par, :], start=True, stop=False)
                nc.tensor.matmul(B[6 + m % 2][:], wh[:, u % RING, w], fl[:, par, :], start=False, stop=False)
                nc.tensor.matmul(B[6 + m % 2][:], wl[:, u % RING, w], fh[:, par, :], start=False, stop=True)\
                  .then_inc(d_m if m < KD - 1 else unit_done, 1)

        def both(bank):
            return [(B[bank][:], 0, T), (B[bank + 1][:, 0:TC], T, TA)]

        def step_sizes():
            d3 = B[3][:, 0:NCH * 64].rearrange("p (d c h) -> p d c h", d=2, c=NCH)
            pe.wait_ge(t_wl, 1)
            for (bank, c0, c1), name in zip(both(0), ("lat0", "ctx0")):
                pe.wait_ge(h_ready, 8 * NORM[name])
                for k in range(KD):
                    for a, b in ((wdth, mh), (wdth, ml), (wdtl, mh)):
                        last = nc.tensor.matmul(bank[0:64, :], a[:, k, :], b[:, k, c0:c1], start=(k == 0 and a is wdth and b is mh),
                                                stop=(k == KD - 1 and a is wdtl))
            last.then_inc(t_raw, 1)
            pe.wait_ge(t_copied, 1)
            for c in range(NCH):
                last = nc.tensor.transpose(d3[:, :, c, :], dtT[:, chunk(c)], ident[0:64, 0:64])
            last.then_inc(t_dt, 1)
            pe.wait_ge(t_da, 1)
            half = NCH * 32
            for d, tri in ((0, SQ["upto"]), (1, SQ["from"])):
                nc.tensor.matmul(B[1][:, d * half:(d + 1) * half], tri, da[:, d, :, :], start=True, stop=True)
            nc.tensor.matmul(B[2][:, 0:2 * half], ones, da[:], start=True, stop=True).then_inc(t_cum, 1)

        def group(g, i=None, out=None, z=None, ahead=None):
            def c(per, n):
                return at(per * g + n, i, per)
            pe.wait_ge(m_cv, c(4, 4))
            project(z, mh, ml, both(0), i, 8)
            project(z + 1, mh, ml, both(2), i, 8)
            if out is not None:
                group_out(g - 1, i, out)
            for n, cs in enumerate((range(4), range(4), range(4), range(4, 6), range(4, 6))):
                if n == 0:
                    pe.wait_ge(m_z, c(2, 2))
                    pe.wait_ge(m_xbc, c(4, 2))
                if n == 2:
                    pe.wait_ge(m_xbc, c(4, 3))
                if n == 4 and out is not None:
                    pe.wait_ge(m_add, c(8, 0))
                o = 0
                for src in {0: [xs[:, 0]], 1: [xs[:, 1]], 2: [Bm], 3: [xs[:, 0], xs[:, 1]], 4: [Bm]}[n]:
                    for k in cs:
                        last = nc.tensor.transpose(B[n][:, o:o + P], src[:, chunk(k)], ident)
                        o += P
                last.then_inc(m_tr, 1)
            pe.wait_ge(m_xbc, c(4, 4))
            pe.wait_ge(m_dag, c(1, 1))
            pe.wait_ge(m_tok, c(5, 5))

            def before(t):
                d, k = STEPS[t]
                pe.wait_ge(m_px, c(NS, t + 1))
                if t >= 2:
                    pe.wait_ge(m_w, c(NS, t - 1))
                    if (t - 2) % NCH != NCH - 1:
                        pe.wait_ge(m_st, c(updates(NS - 1), updates(t - 2)))
                bank = B[4 + t % 2]
                nc.tensor.matmul(bank[:, 0:P], Bm[:, chunk(k)], Cm[:, chunk(k)], start=True, stop=True)
                if t % NCH != NCH - 1:
                    nc.tensor.matmul(bank[:, P:P + 256], btok[:, k, :], xe[:, updates(t) % 2], start=True, stop=True)
                for r in range(HPG):
                    last = nc.tensor.matmul(B[2 + t % 2][:, chunk(r)], dag[:, d, k, r:r + 1].to_broadcast([P, P]),
                                            SQ["from" if d else "upto"], start=True, stop=True)
                last.then_inc(m_cb, 1)

            before(0)
            for t, (d, k) in enumerate(STEPS):
                if t + 1 < NS:
                    before(t + 1)
                pe.wait_ge(m_w, c(NS, t + 1))
                if t >= 2:
                    pe.wait_ge(m_y, c(NS, t - 1))
                bank = B[6 + t % 2]
                for r in range(HPG):
                    last = nc.tensor.matmul(bank[:, 64 * r:64 * r + 64], decay[t % 4][:, chunk(r)], xdt[:, k, r, :],
                                            start=True, stop=True)
                if t % NCH:
                    pe.wait_ge(m_st, c(updates(NS - 1), updates(t - 1)))
                    last = nc.tensor.matmul(bank[:, 256:512], Cm[:, chunk(k)], state[:, updates(t - 1) % 2],
                                            start=True, stop=True)
                last.then_inc(m_yp, 1)
                if ahead is not None:
                    n = t // 3
                    if t % 3 == 0:
                        if n:
                            pe.wait_ge(m_cv, c(4, 4 + n))
                    project(ahead + n, mh, ml, both(0), i, 8, part=UNDER[t % 3])
            pe.wait_ge(m_y, c(NS, NS))
            for j in range(2):
                lat, con = (B[6], B[7]) if j == 0 else (B[4], B[5])
                for k in range(NCH):
                    bank, o = (lat, k) if k < 4 else (con, k - 4)
                    last = nc.tensor.transpose(bank[:, chunk(o)], ytok[:, k, 2 * j:2 * j + 2, :].rearrange("p r e -> p (r e)"),
                                               ident)
                last.then_inc(m_yt, 1)

        def group_out(g, i, u):
            for a in range(2):
                pe.wait_ge(s_lo, at(u + a + 1, i, 8))
                if a == 0:
                    pe.wait_ge(m_yl, at(2 * g + 2, i, 2))
                for q in range(4):
                    m = 4 * a + q
                    lat, con = (B[6], B[7]) if m % 2 == 0 else (B[4], B[5])
                    if m >= 2:
                        pe.wait_ge(m_add, at(8 * g + m - 1, i, 8))
                    for k in range(2):
                        w = chunk(2 * q + k)
                        for wt, half in ((wh, yh), (wh, yl), (wl, yh)):
                            for bank, c0, c1 in ((lat[:], 0, T), (con[:, 0:TC], T, TA)):
                                last = nc.tensor.matmul(bank, wt[:, (u + a) % RING, w], half[:, k, c0:c1],
                                                        start=(k == 0 and wt is wh and half is yh),
                                                        stop=(k == 1 and wt is wl))
                    last.then_inc(m_om if q < 3 else unit_done, 1)

        def keys_values(u):
            pe.wait_ge(h_ready, 8 * NORM["ctx1"])
            pe.wait_ge(m_rt, 1)
            for n in range(4):
                if n == 0:
                    pe.wait_ge(a_qc, 1)
                if n == 1:
                    pe.wait_ge(a_g, 1)
                project(u + n, ah, al, both(2 * n))
            for j in range(2):
                pe.wait_ge(b_sq, j + 1)
                pe.wait_ge(b_copied, j + 1)
                for c0, c1, bank in ((0, T, 2 * j), (T, TA, 2 * j + 1)):
                    last = nc.tensor.matmul(B[bank][:, 0:c1 - c0], SQ["ones64"], ksq[:, c0:c1], start=True, stop=True)
                last.then_inc(b_ss, 1)
                pe.wait_ge(b_copied, 3 + j)
                for k in range(NCH):
                    bank, o = (4 + 2 * j, k) if k < 4 else (5 + 2 * j, k - 4)
                    last = nc.tensor.transpose(B[bank][:, chunk(o)], vraw[:, j, chunk(k)], ident)
                last.then_inc(b_vt, 1)
                pe.wait_ge(b_kn, j + 1)
                nc.tensor.matmul(B[2 * j][:], SQ["rot"], kn[:, 0:T], start=True, stop=True).then_inc(b_rot, 1)
                pe.wait_ge(b_kr, j + 1)
                for r in range(2):
                    pe.wait_ge(b_v, j + 1) if r == 0 else pe.wait_ge(b_kd, 2 * j + 1)
                    for c0, c1, bank in ((0, T, 4 + 2 * j), (T, TA, 5 + 2 * j)):
                        last = nc.tensor.matmul(B[bank][:, 0:c1 - c0], SQ[f"dup{r}"], kraw[:, j, c0:c1], start=True, stop=True)
                    last.then_inc(b_dup, 1)

        def mean_square_q(p, i=None):
            def c(n):
                return at(p + n, i, 2)
            pe.wait_ge(a_qc, c(1))
            pe.wait_ge(a_sq, c(1))
            nc.tensor.matmul(B[0][:], SQ["ones64"], sqr[:, 0, :], start=True, stop=True).then_inc(a_ss, 1)

        def rotate_q(p, i=None):
            pe.wait_ge(a_qn, at(p + 1, i, 2))
            nc.tensor.matmul(B[0][:], SQ["rot"], tmp[:, 1, :], start=True, stop=True).then_inc(a_rot, 1)

        def pair(p, par, i=None, ahead=None):
            def c(per, n):
                return at(per * p + n, i, 2 * per)

            def scores(s):
                if s == 8:
                    pe.wait_ge(a_qr, c(1, 2))
                    pe.wait_ge(a_kc, c(1, 2))
                if s >= 2 or p or i is not None:
                    pe.wait_ge(a_exp, c(8, s - 1))
                r, b = divmod(s % 8, NB)
                o = (2 + 2 * (s % 2)) * T
                h = slice(64 * r, 64 * r + 64)
                to = par if s < 8 else 1 - par
                queries = qr[h, to, b * P:(b + 1) * P]
                nc.tensor.matmul(ps[:, o:o + T], queries, kcur[h, to, 0:T], start=True, stop=True)
                nc.tensor.matmul(ps[:, o + T:o + TA], queries, kcur[h, to, T:TA], start=True, stop=True).then_inc(a_s, 1)

            if p == 0 and i is None:
                pe.wait_ge(a_qr, 1)
                pe.wait_ge(a_kc, 1)
                scores(0)
                scores(1)

            def weighted(s):
                r, b = divmod(s, NB)
                pe.wait_ge(a_pt, c(8, s + 1))
                if s == 0:
                    pe.wait_ge(a_kv, at(p // 2 + 1, i, 1))
                    if p or i is not None:
                        pe.wait_ge(a_o, c(1, 0))
                for k in range(NCH):
                    last = nc.tensor.matmul(B[1][64 * r:64 * r + 64, b * P:(b + 1) * P], vcur2[:, k, :], pT2[:, s % 2, k, :],
                                            start=(k == 0), stop=(k == NCH - 1))
                last.then_inc(a_pv, 1)

            for s in range(8):
                pe.wait_ge(a_p, c(8, s + 1))
                if s or p or i is not None:
                    pe.wait_ge(a_pt, c(8, s))
                for k in range(NCH):
                    last = nc.tensor.transpose(ps[:, 6 * T + k * P:6 * T + (k + 1) * P], pe2[:, s % 2, chunk(k)], ident)
                last.then_inc(a_t, 1)
                if s:
                    weighted(s - 1)
                if s + 2 < 8 or ahead is not None:
                    scores(s + 2)
                if ahead is not None:
                    if Q_AT <= s < Q_AT + 2:
                        if s == Q_AT:
                            pe.wait_ge(a_g, c(1, 1))
                        project(ahead, ah, al, [(B[0][:], 0, T)], i, 4, part=(4 * (s - Q_AT), 4 * (s - Q_AT) + 4))
                    if s == SS_AT:
                        mean_square_q(p + 1, i)
                    if s == ROT_AT:
                        rotate_q(p + 1, i)
                    if s >= G_AT:
                        if s == G_AT:
                            pe.wait_ge(a_qr, c(1, 2))
                        project(ahead + 1, ah, al, [(B[0][:], 0, T)], i, 4, part=UNDER[s - G_AT])
            weighted(7)

        pe.wait_ge(consts_in, 32)
        norm_sums("mem", TC)
        norm_spread("mem", TC)
        u = FIRST_UNIT["memkv"]
        pe.wait_ge(h_ready, 8)
        with pe.Fori(0, 4) as i:
            for j in range(4):
                pe.wait_ge(kv_copied, at(j + 1, i, 4))
                project(u + j, hh, hl, [(B[j][:, 0:TC], 0, TC)], i, 4)
                if j >= 2:
                    v = j - 2
                    pe.wait_ge(kv_copied, at(4 + 2 * v + 2, i, 4))
                    pe.wait_ge(kv_ready, at(v + 1, i, 2))
                    for kb in range(2):
                        last = nc.tensor.transpose(B[5 + v][:, kb * P:(kb + 1) * P], vt[:, v, kb * P:(kb + 1) * P], ident)
                    last.then_inc(kv_t, 1)

        pe.wait_ge(kv_copied, 4 + 16)
        pe.wait_ge(kv_ready, 2 + 8)
        norm_sums("ffn0", T)
        ffn(0, "ffn0", "ffn0", "pool")
        norm_spread("pool", T)
        n = NORM["pool"]
        u = FIRST_UNIT["pool"]
        order = ["u", "u", "u", "u", "q", "q", "w", "u", "u", "u", "u", "q", "q", "w"]
        t = 0
        mixed = 0
        pe.wait_ge(gated, 2 + 22)
        for v, kind in enumerate(order):
            if kind != "w":
                if t >= 4:
                    pe.wait_ge(pool_copied, t - 3)
                project(u + v, hh, hl, [(B[t % 4][:], 0, T)],
                        arrive=(lambda k: pe.wait_ge(h_ready, 8 * n + k + 1)) if v == 0 else None)
                t += 1
            else:
                plan = []
                for b in range(8):
                    g, m, k = mixed + b // 4, b // 2 % 2, b % 2

                    def before(g=g, m=m, k=k):
                        if k == 0 and m == 0:
                            pe.wait_ge(pooled_lo, 2 * g + 2)
                            if g == 0:
                                pe.wait_ge(rt_ready, n + 1)
                            if g >= 2:
                                pe.wait_ge(mix_lo, 4)
                    plan.append((before, xoh[:, (2 * g + k) % 4, :], xol[:, (2 * g + k) % 4, :],
                                 B[4 + (2 * g + m) % 4][:], k == 0, k == 1))
                blocks(u + v, plan)
                mixed += 2
        pe.wait_ge(pool_copied, 12)
        pe.wait_ge(mix_lo, 8)
        u = FIRST_UNIT["pool_out"]
        done = xr(1, 0)
        memory_attention(0, u, done)
        out_memory(u + 8, done + 8, 1, "ffn1")
        ffn(1, "ffn1", "ffn1", "ffn2")
        ffn(2, "ffn2", "ffn2", "diff")
        norm_spread("diff", T)
        n = NORM["diff"]
        u = FIRST_UNIT["diff"]
        for b in range(3):
            if b == 2:
                pe.wait_ge(d_copied, 1)
            project(u + b, hh, hl, [(B[b % 2][:], 0, T)],
                    arrive=(lambda k: pe.wait_ge(h_ready, 8 * n + k + 1)) if b == 0 else None)
        diff_head(0, 0, ahead=u + 3)
        with pe.Fori(0, 3) as i:
            diff_head(1, 1, i, ahead=u + 6, out=u + 9)
            diff_head(2, 0, i, ahead=u + 10, out=u + 13)
        diff_head(7, 1, ahead=u + 30, out=u + 33)
        project(u + 34, hh, hl, [(B[2][:], 0, T)])
        mean_square(7)
        out_head(7, 1, u + 35)
        pe.wait_ge(pool_copied, 16)
        pe.wait_ge(x_ready, xr(3, 1) + 64)
        memory_attention(1)
        out_memory(FIRST_UNIT["diff_out"], xr(3, 1) + 64, 2, "ffn3")
        ffn(3, "ffn3", "ffn3", "final")
        norm_spread("final", T)
        norm_sums("lat0", T)
        norm_spread("lat0", T)
        norm_sums("ctx0", TC)
        norm_spread("ctx0", TC)
        step_sizes()
        u = FIRST_UNIT["mamba"]
        for n in range(4):
            if n == 0:
                pe.wait_ge(t_ready, 1)
            if n:
                pe.wait_ge(m_cv, n)
            project(u + n, mh, ml, both(0))
        pe.wait_ge(m_cv, 4)
        group(0, z=u + 4, ahead=u + 6)
        with pe.Fori(0, MG - 2) as i:
            group(1, i, z=u + 10, out=u + 12, ahead=u + 14)
        group(MG - 1, z=u + 58, out=u + 60)
        group_out(MG - 1, None, u + 62)
        pe.wait_ge(m_sq, 2 * MG + 1)
        for c in range(NCH):
            last = nc.tensor.matmul(B[1][:, c:c + 1], sqacc[:, chunk(c)], ones[:, 0:1], start=True, stop=True)
        last.then_inc(m_ss, 1)
        pe.wait_ge(m_rs, 1)
        for c in range(NCH):
            last = nc.tensor.matmul(ps[:, 2 * T + c * P:2 * T + (c + 1) * P], rstd[:, c:c + 1].to_broadcast([P, P]), ident,
                                    start=True, stop=True)
        last.then_inc(m_rb, 1)
        norm_sums("lat1", T)
        norm_spread("lat1", T)
        u = FIRST_UNIT["attn_kv"]
        project(u, ah, al, [(B[0][:], 0, T)], arrive=lambda k: pe.wait_ge(h_ready, 8 * NORM["lat1"] - 8 + k + 1))
        norm_sums("ctx1", TC)
        norm_spread("ctx1", TC)
        project(u + 1, ah, al, [(B[2][:], 0, T)])
        keys_values(u + 2)
        pe.wait_ge(b_kd, 4)
        mean_square_q(0)
        rotate_q(0)
        u = FIRST_UNIT["attn_qg"] - 2
        pair(0, 0, ahead=u + 2)
        with pe.Fori(0, 3) as i:
            pair(1, 1, i, ahead=u + 4)
            pair(2, 0, i, ahead=u + 6)
        pair(7, 1)
        u = FIRST_UNIT["attn_out"]
        for m in range(KD):
            if m >= 2:
                pe.wait_ge(x_ready, X_ATTN + m - 1)
            project(u + m, ah, al, [(B[2 + m % 2][:], 0, T)],
                    arrive=(lambda k: pe.wait_ge(a_ol, k + 1)) if m == 0 else None)
        norm_sums("last", T)
        norm_spread("last", T)

    @block.scalar
    def _(act):
        def split(u, i=None, per=0):
            if i is None and u >= UNITS:
                return
            act.wait_ge(loaded[u % RAW], at(16 * (u // RAW + 1), i, 16 * per // RAW))
            if u >= RING:
                act.wait_ge(unit_done, at(u - RING + 1, i, per))
            nc.scalar.activation(wh[:, u % RING, :], raw[:, u % RAW, :], ACT.Copy).then_inc(s_hi, 1)

        def square(name, src, width, k, ready):
            n = NORM[name]
            act.wait_ge(*ready(k))
            if 8 * n + k >= 2:
                act.wait_ge(sq_used, 8 * n + k - 1)
            nc.scalar.activation(sqr[:, k % 2, 0:width], src[:, k, 0:width], ACT.Square).then_inc(sq_ready, 1)

        def root(name, width):
            n = NORM[name]
            act.wait_ge(ss_ready, n + 1)
            nc.scalar.activation(rt[:, 0:width // P], rstd[:, KD:KD + width // P], ACT.Sqrt, bias=eps6[:, 0:1],
                                 scale=1.0 / D).then_inc(rt_ready, 1)

        def norm(name, src, width, ready):
            for k in range(KD):
                square(name, src, width, k, ready)
            root(name, width)

        def norm_hi(name, width, h0=0, bias=None, hh=hh):
            n = NORM[name] - (1 if NORM[name] > NORM["final"] else 0)
            for k in range(KD):
                act.wait_ge(tmp_ready, 8 * n + k + 1)
                if bias is None:
                    nc.scalar.activation(hh[:, k, h0:h0 + width], tmp[:, k % 2, 0:width], ACT.Copy).then_inc(h_hi, 1)
                else:
                    nc.scalar.activation(hh[:, k, h0:h0 + width], tmp[:, k % 2, 0:width], ACT.Identity,
                                         bias=bias(k)).then_inc(h_hi, 1)

        def x_blocks(done):
            return lambda k: (x_ready, done + k + 1)

        def ffn(f, name, norm_name, following, ready):
            norm_hi(norm_name, T)
            u = FIRST_UNIT[name]
            pairs = f * sum(FF_PARTS)
            for p, w in enumerate(FF_PARTS):
                with act.Fori(0, w // 2) as i:
                    for jj in range(2):
                        g = u + 2 * jj
                        if w == KD and f < 3 and jj == 0:
                            v = 16 * f + 8 * p
                            act.wait_ge(mod_used, at(v + 2, i, 2))
                            for r in range(2):
                                act.dma_start(modw[:, r:r + 1, :], A["mod"][at(v + r, i, 2)].unsqueeze(1)).then_inc(mod_loaded[r], 16)
                        act.wait_ge(unit_done, at(g + 1, i, 4))
                        nc.scalar.activation(sg[:, jj, :], B[2 * jj][:], ACT.Silu).then_inc(silu_ready, 1)
                        split(g + RING, i, 4)
                        split(g + 1 + RING, i, 4)
                        act.wait_ge(gated, at(2 + pairs + jj + 1, i, 2))
                        nc.scalar.activation(fh[:, bass.ds(i * 2 + jj, 1), :], tmp[:, jj:jj + 1, :], ACT.Copy)\
                           .then_inc(hid_hi, 1)
                u += 2 * w
                if w == KD:
                    with act.Fori(0, 2) as i:
                        for m in range(4):
                            split(u + m + RING, i, 4)
                else:
                    for v in range(w):
                        for m in FF_TAIL[v]:
                            square(following, x, T, m, ready)
                        split(u + v + RING)
                u += w
                pairs += w
            for m in FF_TAIL[-1]:
                square(following, x, T, m, ready)
            root(following, T)

        def memory_attention(layer, u=None):
            with act.Fori(0, X_HEADS // 2) as i:
                def c(n):
                    return at(16 * layer + n, i, 8)

                nc.scalar.activation(qcur[:], qx[:, bass.ds(i * 2, 2), :], ACT.Copy).then_inc(att_q, 1)

                def exps(s):
                    act.wait_ge(att_max, c(s + 1))
                    nc.scalar.activation(pexp[:, s % 2, :], B[4 + s % 2][:, 0:TC], ACT.Exp, bias=nm[:, s:s + 1],
                                         accum_out=rs[:, s:s + 1]).then_inc(att_exp, 1)

                def output(r):
                    act.wait_ge(att_o, c(NB * (r + 1)))
                    nc.scalar.activation(xoh[:, bass.ds(i * 2 + r, 1), :], B[2 + r][:].unsqueeze(1), ACT.Copy).then_inc(xo_hi, 1)
                exps(0)
                exps(1)
                for s in range(8):
                    act.wait_ge(att_t, c(s + 1))
                    if s >= 2:
                        act.wait_ge(att_o, c(s - 1))
                    nc.scalar.activation(pT[:, s % 2], B[6 + s % 2][:, 0:2 * P].rearrange("p (k q) -> p k q", k=2),
                                         ACT.Copy).then_inc(att_pt, 1)
                    if s + 2 < 8:
                        exps(s + 2)
                    if u is not None and s % 2:
                        split(u + s // 2 + RING, i, 4)
                    if s == 5:
                        output(0)
                output(1)

        def out_memory(u, following, ready):
            for v in range(4):
                for m in MIX_TAIL[v]:
                    square(following, x, T, m, ready)
                split(u + v + RING)
            for m in MIX_TAIL[-1]:
                square(following, x, T, m, ready)
            root(following, T)

        def diff_head(h, par, i=None, ahead=None, out=None, memory=False):
            def c(n, per):
                return at(n, i, 2 * per)

            def exps(b):
                for r in range(2):
                    act.wait_ge(d_max, c(8 * h + 2 * b + r + 1, 8))
                    to = de[:, b % 2, r, 0:(b + 1) * P]
                    nc.scalar.activation(to, to, ACT.Exp, bias=dnm[:, b % 2, r:r + 1],
                                         accum_out=drs[:, b % 2, r:r + 1]).then_inc(d_exp, 1)
            exps(0)
            exps(1)
            if h or i is not None:
                diff_tail(h - 1, 1 - par, i)
            for b in range(NB):
                if b < 3 and ahead is not None:
                    diff_copy(b, 1 - par, ahead + b, i, memory)
                    split(ahead + b + RING, i, 8)
                if b == 3 and out is not None:
                    split(out + RING, i, 8)
                act.wait_ge(d_t, c(4 * h + b + 1, 4))
                if b == 0 and (h or i is not None):
                    act.wait_ge(d_o, c(h, 1))
                nc.scalar.activation(dT[:, 0:b + 1, b * P:(b + 1) * P],
                                     B[4][:, 0:(b + 1) * P].rearrange("p (k q) -> p k q", q=P), ACT.Copy).then_inc(d_pt, 1)
                if b < 2:
                    exps(b + 2)
            act.wait_ge(d_o, c(h + 1, 1))
            nc.scalar.activation(sqr[:, 0, :], B[5][:], ACT.Square).then_inc(d_sq, 1)

        def diff_tail(h, par, i=None):
            act.wait_ge(d_ss, at(h + 1, i, 2))
            nc.scalar.activation(rt[:], B[1][:], ACT.Sqrt, bias=eps5[:, 0:1], scale=1.0 / P).then_inc(d_rt, 1)
            act.wait_ge(d_ot, at(h + 1, i, 2))
            nc.scalar.activation(fh[:, par, :], tmp[:, par, :], ACT.Copy).then_inc(d_ohi, 1)

        def diff_copy(b, par, u, i=None, memory=False):
            act.wait_ge(unit_done, at(u + 1, i, 8))
            nc.scalar.activation((dq, dk, dv)[b][:, par, :], B[b % 2][:], ACT.Copy,
                                 scale=P ** -0.5 if memory else DIFF_SCALE if b == 0 else 1.0).then_inc(d_copied, 1)

        def step_sizes():
            f = lambda a: a.rearrange("p d c h -> p (d c h)")
            act.wait_ge(t_raw, 1)
            nc.scalar.activation(dtT, ps[0:64, 0:TA], ACT.Copy).then_inc(t_copied, 1)
            nc.scalar.activation(aexp, col("a_log", 0, 64), ACT.Exp).then_inc(t_a, 1)
            act.wait_ge(t_x, 1)
            nc.scalar.activation(f(ela), f(dt), ACT.Abs).then_inc(t_abs, 1)
            act.wait_ge(t_abs, 1)
            nc.scalar.activation(f(tend), f(ela), ACT.Exp, scale=-1.0).then_inc(t_exp, 1)
            act.wait_ge(t_exp, 1)
            nc.scalar.activation(f(cdec), f(tend), ACT.Ln, bias=one).then_inc(t_ln, 1)
            act.wait_ge(t_diff, 1)
            nc.scalar.activation(f(ela), f(la), ACT.Exp)
            nc.scalar.activation(f(tend), f(tend), ACT.Exp)
            nc.scalar.activation(f(cdec), B[2][:, 0:NCH * 64], ACT.Exp).then_inc(t_dec, 1)

        def copy_unit(n, u, i=None):
            act.wait_ge(unit_done, at(u + 1, i, 8))
            nc.scalar.activation(cvin[:, n, 2:2 + T], B[0][:], ACT.Copy)
            nc.scalar.activation(cvin[:, n, 4 + T:4 + TA], B[1][:, 0:TC], ACT.Copy).then_inc(m_cv, 1)

        def group(g, i=None, out=None, z=None, ahead=None):
            def c(per, n):
                return at(per * g + n, i, per)
            gg = g if i is None else i + g

            def convolved(n):
                act.wait_ge(m_acc, c(4, n + 1))
                to = (xs[:, 0], xs[:, 1], Bm, Cm)[n]
                k = COL["conv_b"] + ((gg * 2 + n) if n < 2 else (gg + 8 * n))
                for dst, a0, w in ((0, 0, T), (T, T + 2, TC)):
                    last = nc.scalar.activation(to[:, dst:dst + w], conv[n % 2][:, a0:a0 + w], ACT.Silu,
                                                bias=cols[:, bass.ds(k, 1)])
                last.then_inc(m_xbc, 1)

            def gate(j):
                act.wait_ge(unit_done, at(z + j + 1, i, 8))
                split(z + j + RING, i, 8)
                src = ps[:, 2 * j * T:2 * j * T + TA]
                nc.scalar.activation(zs[:, j, :], src, ACT.Silu).then_inc(m_z, 1)

            if not (i is None and g == 0):
                act.wait_ge(m_yl, c(2, 0))
            act.wait_ge(m_sq, c(2, 1))
            gate(0)
            convolved(0)
            convolved(1)
            gate(1)
            if out is not None:
                split(out + RING, i, 8)
            convolved(2)
            convolved(3)
            if out is not None:
                split(out + 1 + RING, i, 8)
            for n in range(5):
                act.wait_ge(m_tr, c(5, n + 1))
                if n < 2:
                    dst, src = xtok[:, 0:4, 2 * n:2 * n + 2, :], B[n][:].rearrange("p (c r e) -> p c r e", c=4, r=2)
                elif n == 2:
                    dst, src = btok[:, 0:4, :], B[2][:].rearrange("p (c n) -> p c n", c=4)
                elif n == 3:
                    for j in range(2):
                        last = nc.scalar.activation(xtok[:, 4:6, 2 * j:2 * j + 2, :],
                                                    B[3][:, 256 * j:256 * j + 256].rearrange("p (c r e) -> p c r e", c=2, r=2),
                                                    ACT.Copy)
                else:
                    dst, src = btok[:, 4:6, :], B[4][:, 0:256].rearrange("p (c n) -> p c n", c=2)
                if n != 3:
                    last = nc.scalar.activation(dst, src, ACT.Copy)
                last.then_inc(m_tok, 1)

            def exps(t):
                d, k = STEPS[t]
                act.wait_ge(m_cb, c(NS, t + 1))
                if t >= 4:
                    act.wait_ge(m_yp, c(NS, t - 3))
                for r in range(HPG):
                    last = nc.scalar.activation(decay[t % 4][:, chunk(r)], B[2 + t % 2][:, chunk(r)], ACT.Relu, scale=-1.0,
                                                bias=la[:, d, k, bass.ds(gg * HPG + r, 1)])
                last.then_inc(m_t, 1)
                act.wait_ge(m_t, c(NS, t + 1))
                nc.scalar.activation(decay[t % 4], decay[t % 4], ACT.Exp, scale=-1.0).then_inc(m_e, 1)
            exps(0)
            for t in range(NS):
                if t + 1 < NS:
                    exps(t + 1)
                if ahead is not None and t % 3 == 2:
                    n = t // 3
                    copy_unit(n, ahead + n, i)
                    split(ahead + n + RING, i, 8)
            for j in range(2):
                act.wait_ge(m_yg, c(2, j + 1))
                w = cols[:, bass.ds(COL["m_norm_w"] + gg * 2 + j, 1)]
                nc.scalar.activation(yh[:, j, :], zs[:, j, :], ACT.Copy, scale=w).then_inc(m_yh, 1)
                nc.scalar.activation(xs[:, j, :], zs[:, j, :], ACT.Square).then_inc(m_x, 1)

        def keys_values(u):
            for n in range(4):
                act.wait_ge(unit_done, u + n + 1)
                split(u + n + RING)
                src = ps[:, 2 * n * T:2 * n * T + TA]
                to = kraw[:, n] if n < 2 else vraw[:, n - 2]
                if n == 0:
                    nc.scalar.activation(ksq, src, ACT.Square).then_inc(b_sq, 1)
                nc.scalar.activation(to, src, ACT.Copy).then_inc(b_copied, 1)
            for j in range(2):
                act.wait_ge(b_ss, j + 1)
                nc.scalar.activation(krt, ps[:, 2 * j * T:2 * j * T + TA], ACT.Sqrt, bias=eps6[:, 0:1], scale=1.0 / 64)\
                  .then_inc(b_rt, 1)
                if j == 0:
                    act.wait_ge(b_copied, 2)
                    nc.scalar.activation(ksq, kraw[:, 1], ACT.Square).then_inc(b_sq, 1)
                act.wait_ge(b_vt, j + 1)
                nc.scalar.activation(vtok[:, :, j * P:(j + 1) * P],
                                     ps[:, (4 + 2 * j) * T:(4 + 2 * j) * T + TA].rearrange("p (c d) -> p c d", c=NCH),
                                     ACT.Copy).then_inc(b_v, 1)
                for r in range(2):
                    act.wait_ge(b_dup, 2 * j + r + 1)
                    nc.scalar.activation(kd[:, 2 * j + r], ps[:, (4 + 2 * j) * T:(4 + 2 * j) * T + TA], ACT.Copy).then_inc(b_kd, 1)

        def queries(p, u, i=None, per=4):
            act.wait_ge(unit_done, at(u + 1, i, per))
            split(u + RING, i, per)
            nc.scalar.activation(sqr[:, 0, :], B[0][:], ACT.Square).then_inc(a_sq, 1)
            nc.scalar.activation(tmp[:, 0, :], B[0][:], ACT.Copy).then_inc(a_qc, 1)

        def root_q(p, i=None):
            act.wait_ge(a_ss, at(p + 1, i, 2))
            nc.scalar.activation(rt[:], B[0][:], ACT.Sqrt, bias=eps6[:, 0:1], scale=1.0 / 64).then_inc(a_rt, 1)

        def gates(p, par, u, i=None, per=4, bank=0):
            act.wait_ge(unit_done, at(u + 1, i, per))
            split(u + RING, i, per)
            nc.scalar.activation(gs[:, par, :], B[bank][:], ACT.Silu).then_inc(a_g, 1)

        def pair(p, par, i=None, ahead=None):
            def c(per, n):
                return at(per * p + n, i, 2 * per)

            def exps(s):
                act.wait_ge(a_max, c(8, s + 1))
                if s >= 2 or p or i is not None:
                    act.wait_ge(a_t, c(8, s - 1))
                o = (2 + 2 * (s % 2)) * T
                nc.scalar.activation(pe2[:, s % 2, :], ps[:, o:o + TA], ACT.Exp, bias=nm2[:, s % 8:s % 8 + 1],
                                     accum_out=rs2[:, s % 8:s % 8 + 1]).then_inc(a_exp, 1)
            if p == 0 and i is None:
                exps(0)
                exps(1)
            for s in range(8):
                act.wait_ge(a_t, c(8, s + 1))
                if s >= 2 or p or i is not None:
                    act.wait_ge(a_pv, c(8, 8 + s - 1))
                nc.scalar.activation(pT2[:, s % 2, :, :], ps[:, 6 * T:6 * T + TA].rearrange("p (k q) -> p k q", k=NCH),
                                     ACT.Copy).then_inc(a_pt, 1)
                if s + 2 < 8 or ahead is not None:
                    exps(s + 2)
                if ahead is not None:
                    if s == Q_AT + 1:
                        queries(p + 1, ahead, i)
                    if s == SS_AT:
                        root_q(p + 1, i)
                    if s == G_AT + 2:
                        gates(p + 1, 1 - par, ahead + 1, i)
                elif s < 7:
                    out_half(s)

        def out_half(p):
            act.wait_ge(a_o, p + 1)
            nc.scalar.activation(ah[:, p, 0:T], og[:, p, :], ACT.Copy).then_inc(a_oh, 1)

        split(0)
        split(1)
        act.wait_ge(s_init, 1)
        norm("mem", side, TC, lambda k: (side_in, 16))
        split(2)
        split(3)
        norm_hi("mem", TC)
        u = FIRST_UNIT["memkv"]
        with act.Fori(0, 4) as i:
            for j in range(4):
                split(u + j + RING, i, 4)
                act.wait_ge(unit_done, at(u + j + 1, i, 4))
                if j % 2 == 0:
                    dst = mk[:, bass.ds(i * 2 + j // 2, 1), :]
                else:
                    dst = vt[:, j // 2:j // 2 + 1, :]
                nc.scalar.activation(dst, B[j][:, 0:TC].unsqueeze(1), ACT.Copy).then_inc(kv_copied, 1)

        act.wait_ge(consts_in, 32)
        nc.scalar.activation(csil[:].rearrange("p k c -> p (k c)"), col("c", 0, 16), ACT.Silu).then_inc(c_silu, 1)
        norm("ffn0", x, T, lambda k: (x_in, 16))
        act.wait_ge(h_ready, 8)
        act.dma_start(side[:], A["ctxT"]).then_inc(ctx_in, 16)
        ffn(0, "ffn0", "ffn0", "pool", x_blocks(xr(1, 0) - 8))
        norm_hi("pool", T)
        u = FIRST_UNIT["pool"]
        order = ["u", "u", "u", "u", "q", "q", "w", "u", "u", "u", "u", "q", "q", "w"]
        t = blk = head = 0

        halves = 0

        def pooled_half(b):
            act.wait_ge(pooled, b + 1)
            if b >= 4:
                act.wait_ge(unit_done, u + 7)
            nc.scalar.activation(xoh[:, b % 4, :], tmp[:, b % 2, :], ACT.Copy).then_inc(pooled_hi, 1)

        for v, kind in enumerate(order):
            act.wait_ge(unit_done, u + v + 1)
            split(u + v + RING)
            if kind == "u":
                if blk >= 2 and halves == blk - 2:
                    pooled_half(halves)
                    halves += 1
                nc.scalar.activation(ubuf[:, blk % 2, PAD:], B[t % 4][:], ACT.Copy).then_inc(pool_copied, 1)
                blk += 1
                t += 1
            elif kind == "q":
                nc.scalar.activation(qx[:, head, :], B[t % 4][:], ACT.Copy, scale=P ** -0.5).then_inc(pool_copied, 1)
                head += 1
                t += 1
                while head % 2 == 0 and halves < blk:
                    pooled_half(halves)
                    halves += 1
            else:
                for m in range(blk - 4, blk):
                    nc.scalar.activation(fh[:, m, :], B[4 + m % 4][:], ACT.Copy,
                                         scale=col("pool_scale", m)).then_inc(mix_hi, 1)
        u = FIRST_UNIT["pool_out"]
        act.wait_ge(pool_copied, 12)
        memory_attention(0, u)
        out_memory(u + 8, "ffn1", x_blocks(xr(1, 1) - 8))
        ffn(1, "ffn1", "ffn1", "ffn2", x_blocks(xr(2, 1) - 8))
        ffn(2, "ffn2", "ffn2", "diff", x_blocks(xr(3, 1) - 8))
        act.wait_ge(lam_sums, 1)
        nc.scalar.activation(lame[:], lams[:], ACT.Exp).then_inc(lam_exp, 1)
        norm_hi("diff", T)
        u = FIRST_UNIT["diff"]
        for b in range(3):
            diff_copy(b, 0, u + b)
            split(u + b + RING)
        diff_head(0, 0, ahead=u + 3)
        with act.Fori(0, 3) as i:
            diff_head(1, 1, i, ahead=u + 6, out=u + 9)
            diff_head(2, 0, i, ahead=u + 10, out=u + 13)
        diff_head(7, 1, ahead=u + 30, out=u + 33, memory=True)
        act.wait_ge(unit_done, u + 35)
        act.wait_ge(d_copied, 27)
        for j, q in enumerate((dq, dk, dv)):
            nc.scalar.activation(qx[:, j, :], q[:, 0, :], ACT.Copy).then_inc(pool_copied, 1)
        nc.scalar.activation(qx[:, 3, :], B[2][:], ACT.Copy, scale=P ** -0.5).then_inc(pool_copied, 1)
        split(u + 34 + RING)
        diff_tail(7, 1)
        split(u + 35 + RING)
        act.wait_ge(pool_copied, 16)
        memory_attention(1)
        out_memory(FIRST_UNIT["diff_out"], "ffn3", x_blocks(xr(3, 2) - 8))
        ffn(3, "ffn3", "ffn3", "final", x_blocks(xr(4, 2) - 8))
        act.dma_start(wdt, A["wdt"]).then_inc(wdt_in, 16)
        norm("lat0", x, T, x_blocks(xr(4, 2)))
        norm_hi("lat0", T, 0, lambda k: modv[:, k, 0:1], mh)
        act.wait_ge(tmp_ready, 8 * NORM["lat0"])
        act.dma_start(A["park"], x[:]).then_inc(parked, 16)
        act.wait_ge(wdt_in, 16)
        nc.scalar.activation(wdth, wdt, ACT.Copy).then_inc(t_wh, 1)
        norm("ctx0", side, TC, lambda k: (ctx_in, 16))
        norm_hi("ctx0", TC, T, lambda k: modv[:, k, 1:2], mh)
        step_sizes()
        u = FIRST_UNIT["mamba"]
        act.wait_ge(cv_zero, 1)
        act.wait_ge(parked, 16)
        for n in range(4):
            copy_unit(n, u + n)
            split(u + n + RING)
        group(0, z=u + 4, ahead=u + 6)
        with act.Fori(0, MG - 2) as i:
            group(1, i, z=u + 10, out=u + 12, ahead=u + 14)
        group(MG - 1, z=u + 58, out=u + 60)
        act.wait_ge(m_yp, NS * MG)
        act.wait_ge(m_yt, 2 * MG)
        act.dma_start(x[:], A["park"]).then_inc(parked, 16)
        act.wait_ge(m_y, NS * MG)
        act.dma_start(side[:], A["ctxT"]).then_inc(ctx_in, 16)
        for n in range(2):
            split(u + 62 + n + RING)
        act.wait_ge(m_ss, 1)
        nc.scalar.activation(rt[:, 0:NCH], B[1][:, 0:NCH], ACT.Sqrt, bias=eps6[:, 0:1], scale=1.0 / (2 * D)).then_inc(m_rt, 1)
        act.dma_start(cos[:], A["cos"]).then_inc(cs_in, 16)
        act.dma_start(sin[:], A["sin"]).then_inc(cs_in, 16)
        norm("lat1", x, T, x_blocks(X_ATTN - 8))
        norm_hi("lat1", T, 0, lambda k: modv[:, 24 + k, 0:1], ah)
        norm("ctx1", side, TC, lambda k: (ctx_ready, k + 1))
        norm_hi("ctx1", TC, T, lambda k: modv[:, 24 + k, 1:2], ah)
        act.wait_ge(h_ready, 8 * NORM["ctx1"])
        u = FIRST_UNIT["attn_kv"]
        queries(0, u)
        gates(0, 0, u + 1, bank=2)
        keys_values(u + 2)
        root_q(0)
        u = FIRST_UNIT["attn_qg"] - 2
        pair(0, 0, ahead=u + 2)
        with act.Fori(0, 3) as i:
            pair(1, 1, i, ahead=u + 4)
            pair(2, 0, i, ahead=u + 6)
        act.wait_ge(unit_done, u + 16)
        pair(7, 1)
        out_half(7)
        for n in range(4):
            split(FIRST_UNIT["attn_out"] + RING + n)
        norm("last", x, T, x_blocks(X_ATTN))

    @block.vector
    def _(dve):
        link = Link(dve, s_chain)

        def sums(name, width):
            dve.wait_ge(sq_used, 8 * NORM[name] + 8)
            nc.vector.tensor_reduce(rstd[:, KD:KD + width // P], B[7][:, 0:width // P * KD].rearrange("p (c k) -> p c k", k=KD),
                                    AX.X, ALU.add).then_inc(ss_ready, 1)

        def reciprocal_root(name, width):
            sums(name, width)
            dve.wait_ge(rt_ready, NORM[name] + 1)
            nc.vector.reciprocal(rstd[:, 0:width // P], rt[:, 0:width // P]).then_inc(rs_ready, 1)
            dve.wait_ge(rb_ready, NORM[name] + 1)

        def norm(name, src, width, gain, h0=0, bias=None, hh=hh, hl=hl):
            n0 = NORM[name]
            n = n0 - (1 if n0 > NORM["final"] else 0)
            reciprocal_root(name, width)

            def rest(k):
                dve.wait_ge(h_hi, 8 * n + k + 1)
                half = hh[:, k, h0:h0 + width].bitcast(FP32)
                if bias is None:
                    ins = nc.vector.tensor_tensor(hl[:, k, h0:h0 + width], tmp[:, k % 2, 0:width], half, ALU.subtract)
                else:
                    ins = nc.vector.scalar_tensor_tensor(hl[:, k, h0:h0 + width], tmp[:, k % 2, 0:width], bias(k),
                                                         half, ALU.add, ALU.subtract)
                ins.then_inc(h_ready, 1)
            for k in range(KD):
                if k >= 2:
                    dve.wait_ge(h_ready, 8 * n + k - 1)
                nc.vector.scalar_tensor_tensor(tmp[:, k % 2, 0:width], src[:, k, 0:width], gain(k), B[6][:, 0:width],
                                               ALU.mult, ALU.mult).then_inc(tmp_ready, 1)
                if k >= 1:
                    rest(k - 1)
            rest(KD - 1)

        def modulation(v, i):
            dve.wait_ge(mod_loaded[v % 2], at(16 * (v // 2 + 1), i, 16))
            dve.wait_ge(mod_used, at(v + 1, i, 2))
            done = {}
            for k in range(KD):
                for r in range(2):
                    to, block, c = modp[:, v % 2, r, :], modw[:, v % 2, chunk(k)], csil[:, k, r:r + 1]
                    if k:
                        link.until(done[r])
                        ins = nc.vector.scalar_tensor_tensor(to, block, c, to, ALU.mult, ALU.add)
                    else:
                        ins = nc.vector.tensor_scalar(to, block, c, None, ALU.mult)
                    if k < KD - 1:
                        done[r] = link.mark(ins)
                    else:
                        ins.then_inc(mod_part, 1)

        def ffn(f, name, norm_name, gain):
            norm(norm_name, x, T, gain)
            u = FIRST_UNIT[name]
            pairs = f * sum(FF_PARTS)
            for p, w in enumerate(FF_PARTS):
                with dve.Fori(0, w // 2) as i:
                    link.enter(i, 2 * 2 * (KD - 1) if w == KD and f < 3 else 0)
                    for jj in range(2):
                        dve.wait_ge(silu_ready, at(pairs + jj + 1, i, 2))
                        dve.wait_ge(unit_done, at(u + 2 * jj + 2, i, 4))
                        nc.vector.tensor_tensor(tmp[:, jj, :], sg[:, jj, :], B[2 * jj + 1][:], ALU.mult).then_inc(gated, 1)
                        dve.wait_ge(hid_hi, at(pairs + jj + 1, i, 2))
                        nc.vector.tensor_tensor(fl[:, bass.ds(i * 2 + jj, 1), :], tmp[:, jj:jj + 1, :],
                                                fh[:, bass.ds(i * 2 + jj, 1), :].bitcast(FP32), ALU.subtract)\
                          .then_inc(hid_lo, 1)
                        dve.wait_ge(hid_lo, at(pairs + jj + 1, i, 2))
                        if w == KD and f < 3 and jj == 0:
                            modulation(16 * f + 8 * p, i)
                            modulation(16 * f + 8 * p + 1, i)
                    link.leave(w // 2)
                u += 2 * w

                if p == 1 and f < 3:
                    dve.wait_ge(mod_used, 2 + 16 * (f + 1))
                    nc.vector.tensor_tensor(modv[:, 16 * f:16 * f + 16], B[6][:, 32 * f:32 * f + 32].rearrange("p (m c) -> p m c", c=2),
                                            col("mod_b_2", 16 * f, 16).unsqueeze(2).to_broadcast([P, 16, 2]), ALU.add)\
                      .then_inc(mod_read, 1)
                    if f == 2:
                        dve.wait_ge(mod_read, 3)
                        for layer in range(2):
                            for r in range(2):
                                nc.vector.scalar_tensor_tensor(gmod[:, 8 * layer:8 * layer + 8, r],
                                                               modv[:, 24 * layer + 8:24 * layer + 16, r], 1.0,
                                                               col("norm_w_2", 8 * layer, 8), ALU.add, ALU.mult)\
                                  .then_inc(gmod_ready, 1)

                def add(m, slot, unit, i=None, per=0):
                    dve.wait_ge(unit_done, at(unit + 1, i, per))
                    nc.vector.scalar_tensor_tensor(x[:, m, :], B[4 + slot][:].unsqueeze(1), 0.5, x[:, m, :],
                                                   ALU.mult, ALU.add).then_inc(x_ready, 1)
                if w == KD:
                    with dve.Fori(0, 2) as i:
                        for m in range(4):
                            add(bass.ds(i * 4 + m, 1), m % 2, u + m, i, 4)
                else:
                    for m in range(KD):
                        add(slice(m, m + 1), m % 2, u + (w * m + w - 1) // 8)
                u += w
                pairs += w

        def memory_attention(layer, u=None):
            with dve.Fori(0, X_HEADS // 2) as i:
                link.enter(i, 8)

                def c(n):
                    return at(16 * layer + n, i, 8)

                nc.vector.tensor_copy(vcur[:], mv[:, bass.ds(i * 2 + X_HEADS * layer, 2), :, :]).then_inc(att_v, 1)

                def maximum(s):
                    dve.wait_ge(att_s, c(s + 1))
                    nc.vector.tensor_reduce(nm[:, s:s + 1], B[4 + s % 2][:, 0:TC], AX.X, ALU.max, negate=True)\
                      .then_inc(att_max, 1)

                def normalize(s):
                    dve.wait_ge(att_exp, c(s + 1))
                    link(nc.vector.reciprocal(rr[:, s:s + 1], rs[:, s:s + 1]))
                    nc.vector.tensor_scalar(pexp[:, s % 2, :], pexp[:, s % 2, :], rr[:, s:s + 1], None,
                                            ALU.mult).then_inc(att_p, 1)

                def output(r):
                    dve.wait_ge(xo_hi, at(X_HEADS * layer + r + 1, i, 2))
                    nc.vector.tensor_tensor(xol[:, bass.ds(i * 2 + r, 1), :], B[2 + r][:].unsqueeze(1),
                                            xoh[:, bass.ds(i * 2 + r, 1), :].bitcast(FP32), ALU.subtract).then_inc(xo_lo, 1)

                def add(m):
                    dve.wait_ge(unit_done, at(u + m + 1, i, 4))
                    nc.vector.tensor_tensor(x[:, bass.ds(i * 4 + m, 1), :], B[m % 2][:].unsqueeze(1),
                                            x[:, bass.ds(i * 4 + m, 1), :], ALU.add).then_inc(x_ready, 1)
                maximum(0)
                maximum(1)
                normalize(0)
                for s in range(8):
                    if s + 1 < 8:
                        normalize(s + 1)
                    if s + 2 < 8:
                        maximum(s + 2)
                    if u is not None and s and s % 2 == 0:
                        add(s // 2 - 1)
                    if s == 6:
                        output(0)
                output(1)
                if u is not None:
                    add(3)
                link.leave(X_HEADS // 2)

        def out_memory(u):
            for m in range(KD):
                dve.wait_ge(unit_done, u + m // 2 + 1)
                nc.vector.tensor_tensor(x[:, m, :], B[m % 2][:], x[:, m, :], ALU.add).then_inc(x_ready, 1)

        def diff_head(h, par, i=None, ahead=None, out=None):
            def c(n, per):
                return at(n, i, 2 * per)
            hcol = h if i is None else i * 2 + h

            def maximum(b):
                n = (b + 1) * P
                for r in range(2):
                    dve.wait_ge(d_s, c(8 * h + 2 * b + r + 1, 8))
                    nc.vector.scalar_tensor_tensor(de[:, b % 2, r, 0:n], dist[:, T - n:T],
                                                   cols[:, bass.ds(hcol + COL["slopes"], 1)],
                                                   B[2 + r][:, 0:n], ALU.mult, ALU.add).then_inc(d_biased, 1)
                for r in range(2):
                    dve.wait_ge(d_biased, c(8 * h + 2 * b + r + 1, 8))
                    nc.vector.tensor_reduce(dnm[:, b % 2, r:r + 1], de[:, b % 2, r, 0:n], AX.X, ALU.max, negate=True)\
                      .then_inc(d_max, 1)

            def weights(b):
                n = (b + 1) * P
                first, second = de[:, b % 2, 0, 0:n], de[:, b % 2, 1, 0:n]
                dve.wait_ge(d_exp, c(8 * h + 2 * b + 2, 8))
                link(nc.vector.reciprocal(drr[:, b % 2], drs[:, b % 2]))
                link(nc.vector.tensor_tensor(drl[:], drr[:, b % 2, 1:2], lam[:], ALU.mult))
                link(nc.vector.tensor_scalar(second, second, drl[:, 0:1], None, ALU.mult))
                if b or h or i is not None:
                    dve.wait_ge(d_t, c(4 * h + b, 4))
                nc.vector.scalar_tensor_tensor(dw[:, 0:n], first, drr[:, b % 2, 0:1], second,
                                               ALU.mult, ALU.subtract).then_inc(d_w, 1)
                dve.wait_ge(d_w, c(4 * h + b + 1, 4))

            maximum(0)
            maximum(1)
            if h or i is not None:
                dve.wait_ge(d_o, c(h, 1))
            dve.wait_ge(d_vt, c(h + 1, 1))
            nc.vector.tensor_copy(dvt[:].rearrange("p k d -> p (k d)"), B[4][:]).then_inc(d_vtok, 1)
            if h or i is not None:
                normed(h - 1, 1 - par, i)
            weights(0)
            if h or i is not None:
                normed_rest(h - 1, 1 - par, i)
            maximum(2)
            weights(1)
            maximum(3)
            weights(2)
            weights(3)
            if out is not None:
                out_head(h - 1, out, i)

        def normed(h, par, i=None):
            dve.wait_ge(d_rt, at(h + 1, i, 2))
            link(nc.vector.reciprocal(rstd[:], rt[:]))
            nc.vector.scalar_tensor_tensor(tmp[:, par, :], B[5][:], dgain[:, 0:1], rstd[:], ALU.mult, ALU.mult)\
              .then_inc(d_ot, 1)

        def normed_rest(h, par, i=None):
            dve.wait_ge(d_ohi, at(h + 1, i, 2))
            nc.vector.tensor_tensor(fl[:, par, :], tmp[:, par, :], fh[:, par, :].bitcast(FP32), ALU.subtract).then_inc(d_olo, 1)

        def out_head(h, u, i=None):
            for m in range(KD):
                if m < KD - 1:
                    dve.wait_ge(d_m, at(7 * h + m + 1, i, 14))
                else:
                    dve.wait_ge(unit_done, at(u + 1, i, 8))
                nc.vector.tensor_tensor(x[:, m, :], B[6 + m % 2][:], x[:, m, :], ALU.add).then_inc(x_ready, 1)

        def keys_values():
            link(nc.vector.tensor_scalar(aqg[:], col("a_q_norm"), A_SCALE, None, ALU.mult))
            dve.wait_ge(cs_in, 32)
            for j in range(2):
                dve.wait_ge(b_rt, j + 1)
                link(nc.vector.reciprocal(krs, krt))
                nc.vector.scalar_tensor_tensor(kn, kraw[:, j], col("a_k_norm"), krs, ALU.mult, ALU.mult).then_inc(b_kn, 1)
                dve.wait_ge(b_kn, j + 1)
                link(nc.vector.tensor_tensor(kraw[:, j, 0:T], kn[:, 0:T], cos[:], ALU.mult))
                nc.vector.tensor_copy(kraw[:, j, T:TA], kn[:, T:TA])
                dve.wait_ge(b_rot, j + 1)
                link(nc.vector.tensor_tensor(krs[:, 0:T], B[2 * j][:], sin[:], ALU.mult))
                nc.vector.tensor_tensor(kraw[:, j, 0:T], kraw[:, j, 0:T], krs[:, 0:T], ALU.add).then_inc(b_kr, 1)
                dve.wait_ge(b_kr, j + 1)

        def normed_q(p, i=None):
            dve.wait_ge(a_rt, at(p + 1, i, 2))
            link(nc.vector.reciprocal(rstd[:], rt[:]))
            nc.vector.scalar_tensor_tensor(tmp[:, 1, :], tmp[:, 0, :], aqg[:, 0:1], rstd[:], ALU.mult, ALU.mult).then_inc(a_qn, 1)

        def rotated_q(p, par, i=None):
            dve.wait_ge(a_qn, at(p + 1, i, 2))
            link(nc.vector.tensor_tensor(qr[:, par, :], tmp[:, 1, :], cos[:], ALU.mult))
            dve.wait_ge(a_rot, at(p + 1, i, 2))
            link(nc.vector.tensor_tensor(sqr[:, 1, :], B[0][:], sin[:], ALU.mult))
            nc.vector.tensor_tensor(qr[:, par, :], qr[:, par, :], sqr[:, 1, :], ALU.add).then_inc(a_qr, 1)

        def pair(p, par, i=None, ahead=None):
            def c(per, n):
                return at(per * p + n, i, 2 * per)
            def maximum(s):
                dve.wait_ge(a_s, c(8, s + 1))
                o = (2 + 2 * (s % 2)) * T
                nc.vector.tensor_reduce(nm2[:, s % 8:s % 8 + 1], ps[:, o:o + TA], AX.X, ALU.max, negate=True).then_inc(a_max, 1)

            def normalize(s):
                dve.wait_ge(a_exp, c(8, s + 1))
                link(nc.vector.reciprocal(rr2[:, s % 8:s % 8 + 1], rs2[:, s % 8:s % 8 + 1]))
                nc.vector.tensor_scalar(pe2[:, s % 2, :], pe2[:, s % 2, :], rr2[:, s % 8:s % 8 + 1], None, ALU.mult)\
                  .then_inc(a_p, 1)

            if p == 0 and i is None:
                keys(0, 0)
                maximum(0)
                maximum(1)
                normalize(0)
                values(0)
            for s in range(8):
                if s + 1 < 8 or ahead is not None:
                    normalize(s + 1)
                if s + 2 < 8 or ahead is not None:
                    maximum(s + 2)
                if s == 0 and (p or i is not None):
                    gate(p - 1, 1 - par, i)
                    if p % 2 == 0:
                        values(p // 2, i)
                if ahead is not None:
                    if s == SS_AT:
                        normed_q(p + 1, i)
                    if s == ROT_AT:
                        rotated_q(p + 1, 1 - par, i)
                        keys(p + 1, 1 - par, i)
                elif s < 7:
                    out_rest(s)

        def keys(p, par, i=None):
            nc.vector.tensor_copy(kcur[:, par:par + 1, :], kd[:, bass.ds(p // 2 if i is None else i + p // 2, 1), :])\
              .then_inc(a_kc, 1)

        def values(group, i=None):
            at_group = group if i is None else i + group
            nc.vector.tensor_copy(vcur2[:], vtok[:, :, bass.ds(at_group * 64, 64)]).then_inc(a_kv, 1)

        def gate(p, par, i=None):
            dve.wait_ge(a_pv, at(8 * p + 16, i, 16))
            dve.wait_ge(a_g, at(p + 1, i, 2))
            nc.vector.tensor_tensor(og[:, bass.ds(p if i is None else i * 2 + p, 1), :], B[1][:].unsqueeze(1),
                                    gs[:, par:par + 1, :], ALU.mult).then_inc(a_o, 1)

        def out_rest(p):
            dve.wait_ge(a_oh, p + 1)
            nc.vector.tensor_tensor(al[:, p, 0:T], og[:, p, :], ah[:, p, 0:T].bitcast(FP32), ALU.subtract).then_inc(a_ol, 1)

        def norm_in_place(name, gain="final_norm_g"):
            reciprocal_root(name, T)
            for k in range(KD):
                nc.vector.scalar_tensor_tensor(x[:, k, :], x[:, k, :], col(gain, k), B[6][:],
                                               ALU.mult, ALU.mult).then_inc(x_ready, 1)

        def step_sizes():
            f = lambda a: a.rearrange("p d c h -> p (d c h)")
            n = NCH * 64
            heads = [P, NCH, 32]
            dve.wait_ge(t_dt, 1)
            for d in range(2):
                last = nc.vector.tensor_tensor(dt[:, d], B[3][:, d * n // 2:(d + 1) * n // 2].rearrange("p (c h) -> p c h", c=NCH),
                                               col("dt_bias", 32 * d, 32).unsqueeze(1).to_broadcast(heads), ALU.add)
            last.then_inc(t_x, 1)
            dve.wait_ge(t_ln, 1)
            link(nc.vector.scalar_tensor_tensor(f(dt), f(dt), 0.0, f(cdec), ALU.max, ALU.add))
            dve.wait_ge(t_a, 1)
            for d in range(2):
                link(nc.vector.tensor_tensor(da[:, d], dt[:, d], aexp[:, 32 * d:32 * d + 32].unsqueeze(1).to_broadcast(heads),
                                             ALU.mult))
            nc.vector.tensor_scalar(f(da[:]), f(da[:]), -1.0, None, ALU.mult).then_inc(t_da, 1)
            dve.wait_ge(t_cum, 1)
            link(nc.vector.tensor_copy(f(la), B[1][:, 0:n]))
            nc.vector.tensor_tensor(f(tend), B[2][:, 0:n], f(la), ALU.subtract).then_inc(t_diff, 1)
            dve.wait_ge(t_dec, 1)
            nc.vector.tensor_tensor(f(tend), f(tend), f(dt), ALU.mult).then_inc(t_ready, 1)

        def group(g, i=None, out=None, z=None, ahead=None):
            def c(per, n):
                return at(per * g + n, i, per)
            gg = g if i is None else i + g

            def per_head(a, d, k):
                return a[:, d, k, bass.ds(gg * HPG, HPG)].unsqueeze(2).to_broadcast([P, HPG, 64])

            nc.vector.tensor_copy(dag[:].rearrange("p d c r -> p (d c) r"),
                                  da[:, :, :, bass.ds(gg * HPG, HPG)].rearrange("p d c r -> p (d c) r")).then_inc(m_dag, 1)
            dve.wait_ge(m_cv, c(4, 4))
            done = {}

            def taps(tap, pair):
                for n in pair:
                    k = (gg * 2 + n) if n < 2 else (gg + 8 * n)
                    to = conv[n % 2]
                    w = cols[:, bass.ds(COL["conv_w"] + 32 * tap + k, 1)]
                    src = cvin[:, n, tap:tap + TA + 2]
                    if tap == 0:
                        if n >= 2:
                            dve.wait_ge(m_xbc, c(4, n - 1))
                        ins = nc.vector.tensor_scalar(to, src, w, None, ALU.mult)
                    else:
                        link.until(done[n])
                        ins = nc.vector.scalar_tensor_tensor(to, src, w, to, ALU.mult, ALU.add)
                    if tap < 4:
                        done[n] = link.mark(ins)
                    else:
                        ins.then_inc(m_acc, 1)

            for tap in range(5):
                taps(tap, (0, 1))
            for tap, adds in enumerate(((), (0,), (1, 2), (3, 4), (5, 6, 7))):
                taps(tap, (2, 3))
                if out is not None:
                    for m in adds:
                        group_add(g - 1, i, out, m)
            dve.wait_ge(m_py, c(1, 1))

            def weigh(t):
                d, k = STEPS[t]
                dve.wait_ge(m_cb, c(NS, t + 1))
                if not (i is None and g == 0 and t == 0):
                    dve.wait_ge(m_w, c(NS, t))
                link(nc.vector.tensor_tensor(cbm, B[4 + t % 2][:, 0:P], SQ["from" if d else "upto"], ALU.mult))
                dve.wait_ge(m_e, c(NS, t + 1))
                e = decay[t % 4].rearrange("p (r l) -> p r l", r=HPG)
                nc.vector.tensor_tensor(e, e, cbm.unsqueeze(1).to_broadcast([P, HPG, P]), ALU.mult).then_inc(m_w, 1)

            def update(t):
                d, k = STEPS[t]
                if t % NCH == NCH - 1:
                    return
                n = updates(t)
                dve.wait_ge(m_cb, c(NS, t + 1))
                st = B[4 + t % 2][:, P:P + 256].rearrange("p (r e) -> p r e", r=HPG)
                if t % NCH == 0:
                    nc.vector.tensor_copy(state[:, n % 2], st).then_inc(m_st, 1)
                else:
                    dve.wait_ge(m_st, c(updates(NS - 1), n - 1))
                    link(nc.vector.tensor_tensor(state[:, n % 2], state[:, 1 - n % 2], per_head(cdec, d, k), ALU.mult))
                    nc.vector.tensor_tensor(state[:, n % 2], st, state[:, n % 2], ALU.add).then_inc(m_st, 1)

            def output(t):
                d, k = STEPS[t]
                dve.wait_ge(m_yp, c(NS, t + 1))
                if not (i is None and g == 0 and t == 0):
                    dve.wait_ge(m_y, c(NS, t))
                bank = B[6 + t % 2]
                inner = bank[:, 0:256].rearrange("p (r e) -> p r e", r=HPG)
                if t % NCH:
                    link.mark(nc.vector.tensor_tensor(yt[:], bank[:, 256:512].rearrange("p (r e) -> p r e", r=HPG),
                                                      per_head(ela, d, k), ALU.mult))
                    link(nc.vector.tensor_tensor(ytok[:, k], inner, ytok[:, k], ALU.add))
                    nc.vector.tensor_tensor(ytok[:, k], ytok[:, k], yt[:], ALU.add).then_inc(m_y, 1)
                else:
                    nc.vector.tensor_tensor(ytok[:, k], inner, ytok[:, k], ALU.add).then_inc(m_y, 1)

            weigh(0)
            for t in range(NS):
                update(t)
                output(t)
                if t + 1 < NS:
                    weigh(t + 1)
            for j in range(2):
                dve.wait_ge(m_yt, c(2, j + 1))
                lat, con = (B[6], B[7]) if j == 0 else (B[4], B[5])
                link(nc.vector.tensor_tensor(zs[:, j, 0:T], lat[:], zs[:, j, 0:T], ALU.mult))
                nc.vector.tensor_tensor(zs[:, j, T:TA], con[:, 0:TC], zs[:, j, T:TA], ALU.mult).then_inc(m_yg, 1)
            for j in range(2):
                dve.wait_ge(m_yh, c(2, j + 1))
                w = cols[:, bass.ds(COL["m_norm_w"] + gg * 2 + j, 1)]
                nc.vector.scalar_tensor_tensor(yl[:, j, :], zs[:, j, :], w, yh[:, j, :].bitcast(FP32),
                                               ALU.mult, ALU.subtract).then_inc(m_yl, 1)

        def group_add(g, i, u, m):
            if m % 4 < 3:
                dve.wait_ge(m_om, at(6 * g + 3 * (m // 4) + m % 4 + 1, i, 6))
            else:
                dve.wait_ge(unit_done, at(u + m // 4 + 1, i, 8))
            lat, con = (B[6], B[7]) if m % 2 == 0 else (B[4], B[5])
            nc.vector.tensor_tensor(acc[:, m, 0:T], lat[:], acc[:, m, 0:T], ALU.add)
            nc.vector.tensor_tensor(acc[:, m, T:TA], con[:, 0:TC], acc[:, m, T:TA], ALU.add).then_inc(m_add, 1)

        nc.vector.memset(eps6[:], 1e-6)
        nc.vector.memset(eps5[:], 1e-5).then_inc(s_init, 1)
        free = 0
        for signal, banks in ((gated, 2), (x_ready, X0), (kv_ready, 2), (kv_copied, 4), (mod_used, 2)):
            for _ in range(banks):
                nc.vector.memset(credit[:, free:free + 1], 0.0).then_inc(signal, 1)
                free += 1
        dve.wait_ge(consts_in, 32)
        dve.wait_ge(side_in, 16)
        norm("mem", side, TC, lambda k: col("mem_norm_g", k))
        u = FIRST_UNIT["memkv"]
        with dve.Fori(0, 4) as i:
            for v in range(2):
                dve.wait_ge(kv_t, at(v + 1, i, 2))
                nc.vector.tensor_copy(mv[:, bass.ds(i * 2 + v, 1), :, :],
                                      B[5 + v][:, 0:TC].rearrange("p (o k d) -> p o k d", o=1, k=2)).then_inc(kv_ready, 1)

        dve.wait_ge(x_in, 16)
        dve.wait_ge(c_silu, 1)
        ffn(0, "ffn0", "ffn0", lambda k: col("norm_g", k))
        norm("pool", x, T, lambda k: col("norm_g", 8 + k))
        nc.vector.memset(ubuf[:, :, 0:PAD], 0.0)
        nc.vector.memset(pa[:, 0:PAD], 0.0)
        link(nc.vector.memset(pb_[:, 0:PAD], 0.0))
        u = FIRST_UNIT["pool"]
        copied = [1, 2, 3, 4, 7, 8, 9, 10]

        def half(b):
            dve.wait_ge(pooled_hi, b + 1)
            nc.vector.tensor_tensor(xol[:, b % 4, :], tmp[:, b % 2, :], xoh[:, b % 4, :].bitcast(FP32),
                                    ALU.subtract).then_inc(pooled_lo, 1)

        def mixed(m):
            dve.wait_ge(mix_hi, m + 1)
            nc.vector.scalar_tensor_tensor(fl[:, m, :], B[4 + m % 4][:], col("pool_scale", m),
                                           fh[:, m, :].bitcast(FP32), ALU.mult, ALU.subtract).then_inc(mix_lo, 1)
        for b in range(KD):
            if b == 2 * 2:
                half(2)
                half(3)
                for m in range(4):
                    mixed(m)
            elif b >= 2 and b != 5:
                half(b - 2)
            w = POOL_WINDOWS[b // 2]
            if b >= 1:
                dve.wait_ge(pooled, b)
            if b >= 2:
                dve.wait_ge(pooled_lo, b - 1)
            dve.wait_ge(pool_copied, copied[b])
            s, d, to = ubuf[:, b % 2, :], 1, pa
            while d < w:
                link(nc.vector.tensor_tensor(to[:, PAD:], s[:, PAD:], s[:, PAD - d:PAD + T - d], ALU.add))
                s, to, d = to, (pb_ if to is pa else pa), 2 * d
            c = ubuf[:, b % 2, :]
            link(nc.vector.scalar_tensor_tensor(tmp[:, b % 2, :], s[:, PAD:], 1.0 / w, c[:, PAD:],
                                                ALU.mult, ALU.subtract))
            link(nc.vector.tensor_tensor(to[:, PAD:PAD + w], s[:, PAD:PAD + w],
                                         col("pool_rcount", 16 * (b // 2), w), ALU.mult))
            nc.vector.tensor_tensor(tmp[:, b % 2, 0:w], to[:, PAD:PAD + w], c[:, PAD:PAD + w],
                                    ALU.subtract).then_inc(pooled, 1)
        half(6)
        half(7)
        for m in range(4, 8):
            mixed(m)
        u = FIRST_UNIT["pool_out"]
        memory_attention(0, u)
        out_memory(u + 8)
        ffn(1, "ffn1", "ffn1", lambda k: col("norm_g", 16 + k))
        ffn(2, "ffn2", "ffn2", lambda k: col("norm_g", 24 + k))
        dve.wait_ge(dist_in, 16)
        lp = col("diff_lambda", 0, 256).rearrange("p (a b d) -> p a b d", a=2, b=2)
        link(nc.vector.tensor_tensor(lamt[:], lp[:, :, 0, :], lp[:, :, 1, :], ALU.mult))
        nc.vector.tensor_reduce(lams[:], lamt[:], AX.X, ALU.add).then_inc(lam_sums, 1)
        norm("diff", x, T, lambda k: col("norm_g", 32 + k))
        dve.wait_ge(lam_exp, 1)
        link(nc.vector.tensor_tensor(lam[:], lame[:, 0:1], lame[:, 1:2], ALU.subtract))
        link(nc.vector.tensor_scalar(lam[:], lam[:], LAM_INIT, None, ALU.add))
        link(nc.vector.tensor_scalar(dgain[:], col("diff_norm_g"), 1.0 - LAM_INIT, None, ALU.mult))
        u = FIRST_UNIT["diff"]
        diff_head(0, 0)
        with dve.Fori(0, 3) as i:
            link.enter(i, 2 * (3 * NB + 1))
            diff_head(1, 1, i, out=u + 9)
            diff_head(2, 0, i, out=u + 13)
            link.leave(3)
        diff_head(7, 1, out=u + 33)
        normed(7, 1)
        normed_rest(7, 1)
        out_head(7, u + 35)
        memory_attention(1)
        out_memory(FIRST_UNIT["diff_out"])
        ffn(3, "ffn3", "ffn3", lambda k: col("norm_g", 40 + k))
        norm_in_place("final")
        dve.wait_ge(gmod_ready, 4)
        dve.wait_ge(x_ready, xr(4, 2) + 8)
        norm("lat0", x, T, lambda k: gmod[:, k, 0:1], 0, lambda k: modv[:, k, 0:1], mh, ml)
        dve.wait_ge(t_wh, 1)
        nc.vector.tensor_tensor(wdtl, wdt, wdth.bitcast(FP32), ALU.subtract).then_inc(t_wl, 1)
        norm("ctx0", side, TC, lambda k: gmod[:, k, 1:2], T, lambda k: modv[:, k, 1:2], mh, ml)
        for n, (w, at0) in enumerate(((2, 0), (2, 2 + T), (2, 4 + TA))):
            link(nc.vector.memset(cvin[:, :, at0:at0 + w], 0.0))
        nc.vector.memset(credit[:, 29:30], 0.0).then_inc(cv_zero, 1)
        nc.vector.memset(sqacc[:], 0.0).then_inc(m_sq, 1)
        step_sizes()
        dve.wait_ge(m_sq, 1)
        dve.wait_ge(parked, 16)
        dve.wait_ge(m_zero, 1)
        u = FIRST_UNIT["mamba"]
        group(0, z=u + 4, ahead=u + 6)
        with dve.Fori(0, MG - 2) as i:
            link.enter(i, 4 * 4 + NS + 2 * (NS - 2) + (NS - 4) + 2)
            group(1, i, z=u + 10, out=u + 12, ahead=u + 14)
            link.leave(MG - 2)
        group(MG - 1, z=u + 58, out=u + 60)
        for m in range(KD):
            group_add(MG - 1, None, u + 62, m)
        dve.wait_ge(m_add, 8 * MG)
        dve.wait_ge(m_rt, 1)
        nc.vector.reciprocal(rstd[:, 0:NCH], rt[:, 0:NCH]).then_inc(m_rs, 1)
        dve.wait_ge(m_rb, 1)
        dve.wait_ge(parked, 32)
        dve.wait_ge(ctx_in, 32)
        for m in range(KD):
            link(nc.vector.scalar_tensor_tensor(acc[:, m, 0:T], acc[:, m, 0:T], modv[:, 16 + m, 0:1], B[2][:],
                                                ALU.mult, ALU.mult))
            nc.vector.tensor_tensor(x[:, m, :], acc[:, m, 0:T], x[:, m, :], ALU.add).then_inc(x_ready, 1)
        for m in range(KD):
            link(nc.vector.scalar_tensor_tensor(acc[:, m, T:TA], acc[:, m, T:TA], modv[:, 16 + m, 1:2], B[3][:, 0:TC],
                                                ALU.mult, ALU.mult))
            nc.vector.tensor_tensor(side[:, m, :], acc[:, m, T:TA], side[:, m, :], ALU.add).then_inc(ctx_ready, 1)
        norm("lat1", x, T, lambda k: gmod[:, 8 + k, 0:1], 0, lambda k: modv[:, 24 + k, 0:1], ah, al)
        norm("ctx1", side, TC, lambda k: gmod[:, 8 + k, 1:2], T, lambda k: modv[:, 24 + k, 1:2], ah, al)
        keys_values()
        dve.wait_ge(b_kd, 4)
        for n in range(8):
            nc.vector.memset(credit[:, 21 + n:22 + n], 0.0).then_inc(a_pv, 1)
        normed_q(0)
        rotated_q(0, 0)
        pair(0, 0, ahead=True)
        with dve.Fori(0, 3) as i:
            link.enter(i, 2 * (8 + 3))
            pair(1, 1, i, ahead=True)
            pair(2, 0, i, ahead=True)
            link.leave(3)
        pair(7, 1)
        gate(7, 1)
        out_rest(7)
        u = FIRST_UNIT["attn_out"]
        for m in range(KD):
            dve.wait_ge(unit_done, u + m + 1)
            nc.vector.scalar_tensor_tensor(x[:, m, :], B[2 + m % 2][:], modv[:, 40 + m, 0:1], x[:, m, :],
                                           ALU.mult, ALU.add).then_inc(x_ready, 1)
        norm_in_place("last", "final_norm_w_2")


def square_constants():
    i = np.arange(P)
    upto = (i[:, None] <= i[None, :]).astype(np.float32)
    rot = np.zeros((P, P), np.float32)
    for b in range(P):
        half = b // 16 % 2
        if half == 0:
            rot[b + 16, b] = -1.0
        else:
            rot[b - 16, b] = 1.0
    dup = np.zeros((2, P, P), np.float32)
    for r in range(2):
        dup[r, 64 * r + i % 64, i] = 1.0
    return np.stack([np.eye(P, dtype=np.float32), np.ones((P, P), np.float32),
                     (i[:, None] // 64 == i[None, :] // 64).astype(np.float32), upto, upto.T,
                     rot, dup[0], dup[1]], 1)


def distances():
    q, k = np.arange(P)[:, None], np.arange(T)[None, :]
    d = (q + T - P - k).astype(np.float32)
    return np.where(d >= 0, -d, np.float32(MASKED))


def rope():
    t, half = np.arange(T), 32
    inv = (np.float32(10000.0) ** (-np.arange(0, half, 2, dtype=np.float32) / np.float32(half))).astype(np.float32)
    b = np.arange(P) % 64
    place = np.where(b[:, None] // 32 == 0, t[None, :] // 64, t[None, :] % 64).astype(np.float32)
    angle = (place * inv[b % 16][:, None]).astype(np.float32)
    return np.cos(angle).astype(np.float32), np.sin(angle).astype(np.float32)


def columns(a):
    return np.ascontiguousarray(a, np.float32).reshape(-1, P).T


def outputs_first(w, m0, m1):
    k = w.shape[0] // P
    return [w[b * P:(b + 1) * P, m * P:(m + 1) * P] for m in range(m0, m1) for b in range(k)]


def units(blocks):
    return np.ascontiguousarray(np.stack(blocks).reshape(-1, 8, P, P).transpose(0, 2, 1, 3).reshape(-1, P, UNIT))


def weight_stream(I):
    blocks = []
    for i in range(2):
        for h in range(X_HEADS):
            blocks += outputs_first(I["mem_w_kv"][i], h, h + 1) + outputs_first(I["mem_w_kv"][i], 4 + h, 5 + h)

    def ffn(i, j):
        up, down, out, b0 = I["ffn_w_up"][i, j], I["ffn_w_down"][i, j], [], 0
        for w in FF_PARTS:
            for b in range(b0, b0 + w):
                out += outputs_first(up, b, b + 1) + outputs_first(up, D_FF // P + b, D_FF // P + b + 1)
            out += outputs_first(down[b0 * P:(b0 + w) * P], 0, KD)
            b0 += w
        return out

    blocks += ffn(0, 0)
    win, wg = I["pool_w_in"][0], I["pool_w_group"][0]
    for r in range(2):
        blocks += outputs_first(win, 4 * r, 4 * r + 4) + outputs_first(win, 8 + 2 * r, 10 + 2 * r)
        for g in range(2 * r, 2 * r + 2):
            blocks += outputs_first(wg[g], 0, 2)
    blocks += outputs_first(I["pool_w_out"][0][:D], 0, 8) + outputs_first(I["pool_w_out"][0][D:], 0, 8)
    blocks += ffn(0, 1) + ffn(1, 0)
    win, wout = I["diff_w_in"][0], I["diff_w_out"][0]

    def head(h):
        return sum((outputs_first(win, 8 * r + h, 8 * r + h + 1) for r in range(3)), [])

    def head_out(h):
        return outputs_first(wout[h * P:(h + 1) * P], 0, 8)
    blocks += head(0) + head(1)
    for h in range(1, 7):
        blocks += head(h + 1) + head_out(h - 1)
    blocks += outputs_first(win, 24, 27) + head_out(6) + outputs_first(win, 27, 28) + head_out(7)
    blocks += outputs_first(wout[D:], 0, 8)
    blocks += ffn(1, 1)
    win, wout = I["m_in_w_2"][0], I["m_out_w_2"][0]

    def z(g):
        return outputs_first(win, 2 * g, 2 * g + 2)

    def xbc(g):
        return sum((outputs_first(win, m, m + 1) for m in (16 + 2 * g, 17 + 2 * g, 32 + g, 40 + g)), [])

    def group_out(g):
        return outputs_first(wout[2 * P * g:2 * P * (g + 1)], 0, 8)
    blocks += xbc(0) + z(0) + xbc(1)
    for g in range(1, MG - 1):
        blocks += z(g) + group_out(g - 1) + xbc(g + 1)
    blocks += z(MG - 1) + group_out(MG - 2) + group_out(MG - 1)
    win = I["a_in_w_2"][0]
    queries_gates = [outputs_first(win, p, p + 1) + outputs_first(win, 12 + p, 13 + p) for p in range(A_HEADS // 2)]
    blocks += queries_gates[0] + outputs_first(win, 8, 12) + sum(queries_gates[1:], [])
    blocks += outputs_first(I["a_out_w_2"][0], 0, 8)
    return blocks


def kernel(**inputs):
    import concourse.bacc as _bacc
    from concourse.bass_utils import run_bass_kernel_spmd as _run

    I = {k: np.asarray(v) for k, v in inputs.items()}
    f32 = np.float32
    parts = {
        "norm_g": columns(I["norm_g"]), "final_norm_g": columns(I["final_norm_g"]),
        "mem_norm_g": columns(I["mem_norm_g"]), "pool_scale": columns(I["pool_scale"]),
        "diff_norm_g": columns(I["diff_norm_g"]), "norm_w_2": columns(I["norm_w_2"]),
        "final_norm_w_2": columns(I["final_norm_w_2"]), "mod_b_2": columns(I["mod_b_2"]),
        "conv_w": columns(I["m_conv_w_2"]), "conv_b": columns(I["m_conv_b_2"]), "m_norm_w": columns(I["m_norm_w_2"]),
        "a_q_norm": columns(np.tile(I["a_q_norm_2"][0], 2)), "a_k_norm": columns(np.tile(I["a_k_norm_2"][0], 2)),
        "c": np.stack([columns(I["c_2"]), columns(I["c_ctx_2"])], 2).reshape(P, 16),
        "dt_bias": np.tile(I["m_dt_bias_2"].reshape(1, 64), (P, 1)),
        "a_log": np.tile(I["m_a_log_2"].reshape(1, 64), (P, 1)),
        "m_d": np.tile(I["m_d_2"].reshape(1, 32), (P, 1)),
        "diff_lambda": np.tile(I["diff_lambda"].reshape(1, 256), (P, 1)),
        "slopes": np.tile(np.array([2.0 ** (-8.0 * (h + 1) / DIFF_HEADS) for h in range(DIFF_HEADS)], f32), (P, 1)),
        "pool_rcount": np.tile(np.concatenate([1.0 / np.minimum(np.arange(1, 17), w) for w in POOL_WINDOWS])
                               .astype(f32), (P, 1)),
    }
    arrays = {
        "xT": np.ascontiguousarray(I["x"][0].T.reshape(KD, P, T).transpose(1, 0, 2)),
        "memT": np.ascontiguousarray(I["mem"][0].T.reshape(KD, P, TC).transpose(1, 0, 2)),
        "cols": np.ascontiguousarray(np.concatenate([parts[n] for n, _ in COLUMNS], 1)),
        "ctxT": np.ascontiguousarray(I["ctx_2"][0].T.reshape(KD, P, TC).transpose(1, 0, 2)),
        "wdt": np.ascontiguousarray(I["m_in_w_2"][0][:, 6144:].reshape(KD, P, 64).transpose(1, 0, 2)),
        "dist": distances(),
        "cos": rope()[0],
        "sin": rope()[1],
        "squares": np.ascontiguousarray(square_constants()),
        "stream": units(weight_stream(I)),
        "mod": units(outputs_first(I["mod_w_2"][0], 0, 24) + outputs_first(I["mod_w_2"][1], 0, 24)),
    }
    nc = _bacc.Bacc("TRN2", target_bir_lowering=False, num_devices=1)
    A = {k: nc.dram_tensor(k + "_dram", v.shape, FP32, kind="ExternalInput").ap() for k, v in arrays.items()}
    A["out"] = nc.dram_tensor("out_dram", (P, KD, T), FP32, kind="ExternalOutput").ap()
    A["park"] = nc.dram_tensor("park_dram", (P, KD, T), FP32, kind="Internal").ap()
    program(nc, A)
    r = _run(nc, [{k + "_dram": v for k, v in arrays.items()}], core_ids=[0])
    out = np.asarray(r.results[0]["out_dram"])
    return np.ascontiguousarray(out.transpose(2, 1, 0).reshape(1, T, D))
```
